# Optimizing a Trainium2 kernel written in Bass

```python
import math
import jax, jax.numpy as jnp
from jax import lax
import numpy as np

D_MODEL = 1024
BATCH = 1
SEQ = 512
DEPTH = 2

N_EVEN = (DEPTH + 1) // 2
N_ODD = DEPTH // 2

A_HEADS = 8
HEAD_DIM = 64
A_WIDTH = A_HEADS * HEAD_DIM
ATTN_BLOCK = 128
B_WIDTH = D_MODEL // 2
B_BLOCKS = 8
B_BLOCK_DIM = B_WIDTH // B_BLOCKS
CONV_WIDTH = 4
RG_C = 8.0
IN_AB = 3 * A_WIDTH + A_HEADS + 2 * B_WIDTH
C_WIDTH = 2 * D_MODEL
C_GROUPS = 8
C_GROUP_DIM = C_WIDTH // C_GROUPS
C_CHUNK = 128
MEM_LEN = 256
X_HEADS = 4
X_HEAD_DIM = D_MODEL // X_HEADS
N_GROUPS = 4
EXPERTS_PER_GROUP = 8
N_EXPERTS = N_GROUPS * EXPERTS_PER_GROUP
TOP_K = 2
D_EXPERT = D_MODEL // 2
EPS = 1e-6

kernel_name = "hybrid_fox_rglru_gmlp_hmoe"

def rms_norm(x, g):
    xf = x.astype(jnp.float32)
    y = xf * lax.rsqrt(jnp.mean(xf * xf, axis=-1, keepdims=True) + EPS)
    return (y * g.astype(jnp.float32)).astype(x.dtype)

def forgetting_attention(q, k, v, f_logit, f_bias, q_gain, k_gain):
    B, S, _ = q.shape
    q = rms_norm(q.reshape(B, S, A_HEADS, HEAD_DIM), q_gain).transpose(0, 2, 1, 3)
    k = rms_norm(k.reshape(B, S, A_HEADS, HEAD_DIM), k_gain).transpose(0, 2, 1, 3)
    v = v.reshape(B, S, A_HEADS, HEAD_DIM).transpose(0, 2, 1, 3)
    log_f = jax.nn.log_sigmoid(f_logit.astype(jnp.float32) + f_bias.astype(jnp.float32))
    c = jnp.cumsum(log_f, axis=1).transpose(0, 2, 1)
    scale = HEAD_DIM ** -0.5
    kpos = jnp.arange(S)

    def block(i):
        start = i * ATTN_BLOCK
        qb = lax.dynamic_slice_in_dim(q, start, ATTN_BLOCK, axis=2)
        cq = lax.dynamic_slice_in_dim(c, start, ATTN_BLOCK, axis=2)
        s = jnp.einsum('bhqd,bhkd->bhqk', qb, k, preferred_element_type=jnp.float32) * scale
        s = s + cq[..., :, None] - c[..., None, :]
        qpos = start + jnp.arange(ATTN_BLOCK)
        s = jnp.where(kpos[None, :] <= qpos[:, None], s, -jnp.inf)
        p = jax.nn.softmax(s, axis=-1).astype(v.dtype)
        return jnp.einsum('bhqk,bhkd->bhqd', p, v)

    o = lax.map(block, jnp.arange(S // ATTN_BLOCK))
    return o.transpose(1, 0, 3, 2, 4).reshape(B, S, A_WIDTH)

def causal_depthwise_conv(x, w, b):
    S = x.shape[1]
    xp = jnp.pad(x, ((0, 0), (CONV_WIDTH - 1, 0), (0, 0)))
    y = sum(xp[:, k:k + S] * w[k] for k in range(CONV_WIDTH))
    return y + b

def rglru_branch(xb, gb, conv_w, conv_b, wa, ba, wx, bx, lam):
    B, S, _ = xb.shape
    gate = jax.nn.gelu(gb)
    xc = causal_depthwise_conv(xb, conv_w, conv_b)
    xg = xc.reshape(B, S, B_BLOCKS, B_BLOCK_DIM)
    r = jax.nn.sigmoid(jnp.einsum('bsgi,gij->bsgj', xg, wa).reshape(B, S, B_WIDTH) + ba)
    i = jax.nn.sigmoid(jnp.einsum('bsgi,gij->bsgj', xg, wx).reshape(B, S, B_WIDTH) + bx)
    log_a = -RG_C * r.astype(jnp.float32) * jax.nn.softplus(-lam.astype(jnp.float32))
    a = jnp.exp(log_a)
    beta = jnp.sqrt(-jnp.expm1(2.0 * log_a))
    bterm = beta * (i * xc).astype(jnp.float32)

    def combine(left, right):
        a_l, b_l = left
        a_r, b_r = right
        return a_l * a_r, a_r * b_l + b_r

    _, h = lax.associative_scan(combine, (a, bterm), axis=1)
    return gate * h.astype(xb.dtype)

def fox_rglru_mixer(xn, w_in, f_bias, q_gain, k_gain, conv_w, conv_b, wa, ba, wx, bx, lam, w_out):
    proj = xn @ w_in
    cuts = [A_WIDTH, 2 * A_WIDTH, 3 * A_WIDTH, 3 * A_WIDTH + A_HEADS,
            3 * A_WIDTH + A_HEADS + B_WIDTH]
    q, k, v, f_logit, xb, gb = jnp.split(proj, cuts, axis=-1)
    attn = forgetting_attention(q, k, v, f_logit, f_bias, q_gain, k_gain)
    rec = rglru_branch(xb, gb, conv_w, conv_b, wa, ba, wx, bx, lam)
    return jnp.concatenate([attn, rec], axis=-1) @ w_out

def spatial_gating_mixer(xn, w_in, b_in, v_gain, w_s, b_s, w_out):
    B, S, _ = xn.shape
    z = jax.nn.gelu(xn @ w_in + b_in)
    u, v = jnp.split(z, 2, axis=-1)
    v = rms_norm(v, v_gain)
    v = v.reshape(B, S // C_CHUNK, C_CHUNK, C_GROUPS, C_GROUP_DIM)
    w_causal = jnp.tril(w_s)
    mixed = jnp.einsum('gts,bnsgc->bntgc', w_causal, v) + b_s.T[:, :, None]
    return (u * mixed.reshape(B, S, C_WIDTH)) @ w_out

def memory_cross_attention(xn, memn, wq, wkv, wo, q_gain, k_gain):
    B, S, _ = xn.shape
    q = rms_norm((xn @ wq).reshape(B, S, X_HEADS, X_HEAD_DIM), q_gain)
    k, v = jnp.split(memn @ wkv, 2, axis=-1)
    k = rms_norm(k.reshape(B, MEM_LEN, X_HEADS, X_HEAD_DIM), k_gain)
    v = v.reshape(B, MEM_LEN, X_HEADS, X_HEAD_DIM)
    s = jnp.einsum('bqhd,bkhd->bhqk', q, k, preferred_element_type=jnp.float32) * X_HEAD_DIM ** -0.5
    p = jax.nn.softmax(s, axis=-1).astype(v.dtype)
    o = jnp.einsum('bhqk,bkhd->bqhd', p, v).reshape(B, S, D_MODEL)
    return o @ wo

def hierarchical_moe(xn, wg, bg, we, be, w_gate, w_up, w_down):
    B, S, D = xn.shape
    T = B * S
    xf = xn.reshape(T, D)
    g_prob = jax.nn.softmax((xf @ wg + bg).astype(jnp.float32), axis=-1)
    g_idx = jnp.argmax(g_prob, axis=-1)
    g_w = jnp.take_along_axis(g_prob, g_idx[:, None], axis=-1)
    e_logits = (xf @ we + be).astype(jnp.float32).reshape(T, N_GROUPS, EXPERTS_PER_GROUP)
    e_sel = jnp.take_along_axis(e_logits, g_idx[:, None, None], axis=1)[:, 0]
    top_v, top_i = lax.top_k(e_sel, TOP_K)
    weights = (g_w * jax.nn.softmax(top_v, axis=-1)).astype(xn.dtype)
    expert = (g_idx[:, None] * EXPERTS_PER_GROUP + top_i).reshape(-1)
    order = jnp.argsort(expert)
    tok = order // TOP_K
    sizes = jnp.bincount(expert, length=N_EXPERTS).astype(jnp.int32)
    xs = xf[tok]
    h = jax.nn.silu(lax.ragged_dot(xs, w_gate, sizes)) * lax.ragged_dot(xs, w_up, sizes)
    y = lax.ragged_dot(h, w_down, sizes) * weights.reshape(-1)[order][:, None]
    out = jax.ops.segment_sum(y, tok, num_segments=T)
    return out.reshape(B, S, D)

def setup_inputs(seed: int = 0) -> dict:
    key = jax.random.key(seed)
    keys = list(jax.random.split(key, 40))
    kit = iter(keys)

    def nrm(shape, scale):
        return jax.random.normal(next(kit), shape, jnp.float32) * scale

    def gain(shape):
        return 1.0 + nrm(shape, 0.02)

    D = D_MODEL
    x = nrm((BATCH, SEQ, D), 1.0)
    mem = nrm((BATCH, MEM_LEN, D), 1.0)
    u = jax.random.uniform(next(kit), (N_EVEN, B_WIDTH), jnp.float32, 0.9, 0.999)
    sg = u ** (1.0 / RG_C)
    lam = jnp.log(sg) - jnp.log1p(-sg)
    return {
        "x": x,
        "mem": mem,
        "norm_mix": gain((DEPTH, D)),
        "norm_cross": gain((DEPTH, D)),
        "norm_mem": gain((DEPTH, D)),
        "norm_ffn": gain((DEPTH, D)),
        "ab_w_in": nrm((N_EVEN, D, IN_AB), D ** -0.5),
        "ab_f_bias": 3.0 + nrm((N_EVEN, A_HEADS), 1.0),
        "ab_q_gain": gain((N_EVEN, HEAD_DIM)),
        "ab_k_gain": gain((N_EVEN, HEAD_DIM)),
        "ab_conv_w": nrm((N_EVEN, CONV_WIDTH, B_WIDTH), CONV_WIDTH ** -0.5),
        "ab_conv_b": nrm((N_EVEN, B_WIDTH), 0.02),
        "ab_wa": nrm((N_EVEN, B_BLOCKS, B_BLOCK_DIM, B_BLOCK_DIM), B_BLOCK_DIM ** -0.5),
        "ab_ba": nrm((N_EVEN, B_WIDTH), 0.02),
        "ab_wx": nrm((N_EVEN, B_BLOCKS, B_BLOCK_DIM, B_BLOCK_DIM), B_BLOCK_DIM ** -0.5),
        "ab_bx": nrm((N_EVEN, B_WIDTH), 0.02),
        "ab_lambda": lam,
        "ab_w_out": nrm((N_EVEN, A_WIDTH + B_WIDTH, D), (A_WIDTH + B_WIDTH) ** -0.5),
        "c_w_in": nrm((N_ODD, D, 2 * C_WIDTH), D ** -0.5),
        "c_b_in": nrm((N_ODD, 2 * C_WIDTH), 0.02),
        "c_v_gain": gain((N_ODD, C_WIDTH)),
        "c_w_s": nrm((N_ODD, C_GROUPS, C_CHUNK, C_CHUNK), C_CHUNK ** -0.5),
        "c_b_s": 1.0 + nrm((N_ODD, C_GROUPS, C_CHUNK), 0.1),
        "c_w_out": nrm((N_ODD, C_WIDTH, D), C_WIDTH ** -0.5),
        "x_wq": nrm((DEPTH, D, D), D ** -0.5),
        "x_wkv": nrm((DEPTH, D, 2 * D), D ** -0.5),
        "x_wo": nrm((DEPTH, D, D), D ** -0.5),
        "x_q_gain": gain((DEPTH, X_HEAD_DIM)),
        "x_k_gain": gain((DEPTH, X_HEAD_DIM)),
        "moe_wg": nrm((DEPTH, D, N_GROUPS), D ** -0.5),
        "moe_bg": nrm((DEPTH, N_GROUPS), 0.01),
        "moe_we": nrm((DEPTH, D, N_EXPERTS), D ** -0.5),
        "moe_be": nrm((DEPTH, N_EXPERTS), 0.01),
        "moe_w_gate": nrm((DEPTH, N_EXPERTS, D, D_EXPERT), D ** -0.5),
        "moe_w_up": nrm((DEPTH, N_EXPERTS, D, D_EXPERT), D ** -0.5),
        "moe_w_down": nrm((DEPTH, N_EXPERTS, D_EXPERT, D), D_EXPERT ** -0.5),
    }

def reference(x, mem, norm_mix, norm_cross, norm_mem, norm_ffn,
              ab_w_in, ab_f_bias, ab_q_gain, ab_k_gain, ab_conv_w, ab_conv_b,
              ab_wa, ab_ba, ab_wx, ab_bx, ab_lambda, ab_w_out,
              c_w_in, c_b_in, c_v_gain, c_w_s, c_b_s, c_w_out,
              x_wq, x_wkv, x_wo, x_q_gain, x_k_gain,
              moe_wg, moe_bg, moe_we, moe_be, moe_w_gate, moe_w_up, moe_w_down):
    for layer in range(DEPTH):
        j = layer // 2
        h = rms_norm(x, norm_mix[layer])
        if layer % 2 == 0:
            x = x + fox_rglru_mixer(h, ab_w_in[j], ab_f_bias[j], ab_q_gain[j], ab_k_gain[j],
                                    ab_conv_w[j], ab_conv_b[j], ab_wa[j], ab_ba[j],
                                    ab_wx[j], ab_bx[j], ab_lambda[j], ab_w_out[j])
        else:
            x = x + spatial_gating_mixer(h, c_w_in[j], c_b_in[j], c_v_gain[j],
                                         c_w_s[j], c_b_s[j], c_w_out[j])
        x = x + memory_cross_attention(rms_norm(x, norm_cross[layer]),
                                       rms_norm(mem, norm_mem[layer]),
                                       x_wq[layer], x_wkv[layer], x_wo[layer],
                                       x_q_gain[layer], x_k_gain[layer])
        x = x + hierarchical_moe(rms_norm(x, norm_ffn[layer]), moe_wg[layer], moe_bg[layer],
                                 moe_we[layer], moe_be[layer], moe_w_gate[layer],
                                 moe_w_up[layer], moe_w_down[layer])
    return x


_drawn_inputs = setup_inputs


def setup_inputs(seed=0):
    import zlib

    import numpy as np

    out = dict(_drawn_inputs(seed))
    spreads = {}
    factors = {'norm_cross': 7.366,
     'norm_mem': 3.443,
     'ab_q_gain': 2.975,
     'ab_k_gain': 4.272,
     'ab_ba': 8.0,
     'ab_bx': 4.592,
     'c_v_gain': 4.675,
     'x_q_gain': 4.586,
     'x_k_gain': 4.577,
     'moe_bg': 17.935,
     'moe_be': 3.639}
    for name, (base, spread) in spreads.items():
        noise = np.random.default_rng([zlib.crc32(name.encode()), seed]).standard_normal(out[name].shape)
        drawn = base * np.exp(spread * noise) if base else spread * noise
        out[name] = __import__('jax').numpy.asarray(drawn.astype(out[name].dtype))
    for name, factor in factors.items():
        out[name] = (out[name] * factor).astype(out[name].dtype)
    return out
```

```python
from contextlib import ExitStack

import concourse.bass as bass
from concourse import mybir

F32 = mybir.dt.float32
F32R = mybir.dt.float32r
U32 = mybir.dt.uint32
I32 = mybir.dt.int32
ACT = mybir.ActivationFunctionType
ALU = mybir.AluOpType
AX = mybir.AxisListType

P = 128
D = 1024
KD = D // P
T = 512
TM = T // P
MEM = 256
MM = MEM // P
LAYERS = 2
EPS = 1e-6
A_HEADS, A_DIM = 8, 64
X_HEADS, X_DIM = 4, 256
A_W = A_HEADS * A_DIM
B_W = 512
CONV = 4
RG_C = 8.0
C_W = 2048
C_GROUPS, C_DIM = 8, 256
GROUPS, PER_GROUP = 4, 8
EXPERTS = GROUPS * PER_GROUP
FE = 512
KF = FE // P
SLOTS = 64
PASSES = T // SLOTS
NOWHERE = 4096.0
BIG = 1e30

RING = 6
UNIT = 2048
STAGE = 3
STEPS = 4


def dense_plan():
    plan, unit = {}, 0
    for layer in range(LAYERS):
        dense = ([("in", 10), ("out", 4)] if layer % 2 == 0 else [("cin", 16), ("cout", 8)])
        for name, units in dense + [("kv", 8), ("xq", 4), ("xo", 4)]:
            plan[name, layer] = (unit, units)
            unit += units
        plan["moe", layer] = (unit, EXPERTS * 6)
        unit += EXPERTS * 6
    return plan


PLAN = dense_plan()
STEP0 = {}
_steps = 0
for _key, (_u, _n) in PLAN.items():
    if _key[0] != "moe":
        STEP0[_key] = _steps
        _steps += STEPS * _n


def round_plan():
    names = []
    for l in range(LAYERS):
        names += [("nmix", l, m) for m in range(TM)]
        if l % 2 == 0:
            names += [("in", l, c) for c in range(3)] + [("f", l, 0)] + [("in", l, c) for c in (3, 4)]
            names += [("fT", l, 0)] + [("qT", l, 0), ("qT", l, 1), ("kT", l, 0), ("kT", l, 1)]
            names += [("rg", l, 0), ("rg", l, 1)]
            names += [("oT", l, m) for m in range(TM)]
            names += [("out", l, c) for c in range(2)]
        else:
            names += [("cin", l, c) for c in range(4)] + [("wsT", l, 0)] + [("cin", l, c) for c in range(4, 8)]
            names += [("mix", l, c) for c in range(4)]
            names += [("cout", l, c) for c in range(4)]
        names += [("nmem", l, m) for m in range(MM)] + [("kv", l, c) for c in range(4)]
        names += [("xkT", l, 0), ("xkT", l, 1)]
        names += [("ncross", l, m) for m in range(TM)] + [("xq", l, c) for c in range(2)]
        names += [("xqT", l, c) for c in range(2)] + [("xoT", l, m) for m in range(TM)]
        names += [("xo", l, c) for c in range(2)]
        names += [("nffn", l, m) for m in range(TM)] + [("route", l, 0), ("rank", l, 0)]
    return {name: i for i, name in enumerate(names)}


ROUND = round_plan()
DENSE = ("in", "out", "cin", "cout", "kv", "xq", "xo")
PLAIN = {}
for _name in ROUND:
    if _name[0] not in DENSE:
        PLAIN[_name] = len(PLAIN)
NORMS = [(kind, l) for l in range(LAYERS) for kind in ("mix", "mem", "cross", "ffn")]


PACK = {}
PACKED = 0
for _name, _parts, _shape in (("fbias", P, (A_HEADS,)), ("qg", A_DIM, (1,)), ("kg", A_DIM, (1,)),
                              ("convw", P, (4, CONV)), ("convb", P, (4,)), ("bab", P, (4,)), ("bxb", P, (4,)),
                              ("lam", P, (4,)), ("xqg", P, (LAYERS, 2)), ("xkg", P, (LAYERS, 2)),
                              ("gcol", P, (LAYERS, KD)), ("ub", P, (16,)), ("vg", P, (16,)),
                              ("rbias", P, (LAYERS, GROUPS + EXPERTS))):
    _n = 1
    for _s in _shape:
        _n *= _s
    PACK[_name] = (PACKED, _n, _parts, _shape)
    PACKED += _n


def program(nc, A, out):
    ctx = ExitStack()
    with ctx:
        at = [-(-nc.sbuf_base // 32) * 32]
        spot = {}

        def width(shape):
            n = 4
            for s in shape[1:]:
                n *= s
            return n

        def sb(name, shape, dt=F32, over=None, skip=0):
            if over is None:
                off = at[0]
                at[0] += -(-width(shape) // 32) * 32
            else:
                off = spot[over][0] + skip
                assert skip + width(shape) <= spot[over][1], (name, over)
            spot[name] = (off, width(shape))
            return nc.alloc_sbuf_tensor_at(name, shape, dt, offset=off)

        def sem(name):
            return ctx.enter_context(nc.semaphore(name))

        x = sb("x", [P, TM, D])
        ring = sb("ring", [P, RING, UNIT])
        wh = sb("wh", [P, STAGE, 512], F32R)
        wl = sb("wl", [P, STAGE, 512], F32R)
        acts = sb("acts", [P, 8192])
        ah = sb("ah", [P, KD, T], F32R, over="acts")
        al = sb("al", [P, KD, T], F32R, over="acts", skip=16384)
        nat = sb("nat", [P, 2, D])
        gain = sb("gain", [P, 2, D])
        ident = sb("ident", [P, P])
        before = sb("before", [P, P])
        ones = sb("ones", [P, P])
        causal = sb("causal", [P, P])
        iota = sb("iota", [P, SLOTS])
        halfp = sb("halfp", [P, 32])
        onecol = sb("onecol", [P, 1])
        big2 = sb("big2", [P, 1])
        tok2 = sb("tok2", [P, TM])
        rowid = sb("rowid", [P, 1])
        ss = sb("ss", [P, 32])
        rstd = sb("rstd", [P, 32])
        rx = sb("rx", [P, TM])
        nmax = sb("nmax", [P, 32])
        rsum = sb("rsum", [P, 32])
        rinv = sb("rinv", [P, 32])
        work = sb("work", [P, 2048])
        extra = sb("extra", [P, 16384])
        small = sb("small", [P, PACKED])
        assert at[0] <= nc.sbuf_usable_end, (at[0], nc.sbuf_usable_end)
        junk = sb("junk", [P, D], over="work")
        prob = sb("prob", [P, 2, 512], over="work")
        probT = sb("probT", [P, 2, 512], over="work", skip=4096)
        sq = sb("sq", [P, 2, 512], over="work", skip=4096)

        def sm(name):
            lo, n, parts, shape = PACK[name]
            v = small[0:parts, lo:lo + n]
            if len(shape) == 2:
                v = v.rearrange("p (a b) -> p a b", b=shape[1])
            return v

        fbias, qg, kg = sm("fbias"), sm("qg"), sm("kg")
        convw, convb, bab, bxb, lam = sm("convw"), sm("convb"), sm("bab"), sm("bxb"), sm("lam")
        xqg, xkg, gcol, ub, vg, rbias = sm("xqg"), sm("xkg"), sm("gcol"), sm("ub"), sm("vg"), sm("rbias")
        lam2 = sb("lam2", [P, 4])
        zf = sb("zf", [P, TM, A_HEADS])
        ef = sb("ef", [P, TM, A_HEADS])
        spl = sb("spl", [P, 4])
        wsmall = sb("wsmall", [P, KD, 36], over="work", skip=4096)
        whs = sb("whs", [P, KD, 36], F32R)
        wls = sb("wls", [P, KD, 36], F32R)
        assert at[0] <= nc.sbuf_usable_end, (at[0], nc.sbuf_usable_end)

        E = 1024
        qT = sb("qT", [A_DIM + 1, A_HEADS, T], over="extra", skip=0)
        kT = sb("kT", [A_DIM + 1, A_HEADS, T], over="extra", skip=16 * E)
        v0 = sb("v0", [P, TM, A_W], over="extra", skip=32 * E)
        xbT = sb("xbT", [P, 4, T], over="extra", skip=40 * E)
        gbT = sb("gbT", [P, 4, T], over="extra", skip=48 * E)
        kn = sb("kn", [P, TM, A_W], over="extra", skip=56 * E)
        on0 = sb("on0", [P, TM, A_W], over="extra", skip=56 * E)
        qn = sb("qn", [P, TM, A_W], over="nat")
        xcT = sb("xcT", [P, 4, T], over="gain")
        iT = sb("iT", [P, 4, T], over="nat")
        aT = sb("aT", [P, 4, T], over="gain")
        wblk = sb("wblk", [P, 2, 4, P])
        tanhs = sb("tanhs", [P, 2, T], over="wblk")
        negc = sb("negc", [A_HEADS, T], over="work")
        assert at[0] <= nc.sbuf_usable_end, (at[0], nc.sbuf_usable_end)
        v1 = sb("v1", [P, TM, C_W], over="extra", skip=0)
        uT = sb("uT", [P, 16, T], over="extra", skip=32 * E)
        gh = sb("gh", [P, 16, T], F32R, over="acts")
        gl = sb("gl", [P, 16, T], F32R, over="extra", skip=32 * E)
        vbias = sb("vbias", [P, 2048], over="nat")
        wsT = sb("wsT", [P, C_GROUPS, P], over="wblk")
        wsn = sb("wsn", [P, C_GROUPS, P], over="extra", skip=32 * E)
        bs = sb("bs", [P, C_GROUPS, P], over="work", skip=4096)
        gt = sb("gt", [P, 2, T], over="work")
        vjunk = sb("vjunk", [P, T], over="extra", skip=36 * E)
        mem = sb("mem", [P, MM, D], over="extra", skip=0)
        mh = sb("mh", [P, KD, MEM], F32R, over="extra", skip=8 * E)
        ml = sb("ml", [P, KD, MEM], F32R, over="extra", skip=16 * E)
        xkn = sb("xkn", [P, MM, D], over="extra", skip=24 * E)
        xkT = sb("xkT", [P, KD, MEM], over="extra", skip=32 * E)
        xv = sb("xv", [P, MM, D], over="extra", skip=40 * E)
        xqT = sb("xqT", [P, KD, T], over="extra", skip=48 * E)
        xqn = sb("xqn", [P, TM, D], over="extra", skip=0)
        xon = sb("xon", [P, TM, D], over="extra", skip=16 * E)
        lg = sb("lg", [P, TM, 36], over="extra", skip=0)
        gpad = sb("gpad", [P, TM, 8], over="extra", skip=1 * E)
        gm8 = sb("gm8", [P, TM, 8], over="extra", skip=1 * E + 128)
        gi8 = sb("gi8", [P, TM, 8], U32, over="extra", skip=1 * E + 256)
        gif = sb("gif", [P, TM, 1], over="extra", skip=1 * E + 384)
        ge = sb("ge", [P, TM, 4], over="extra", skip=1 * E + 448)
        gee = sb("gee", [P, TM, 4], over="extra", skip=1 * E + 512)
        gw = sb("gw", [P, TM, 1], over="extra", skip=1 * E + 576)
        oh4 = sb("oh4", [P, TM, 4], over="extra", skip=1 * E + 640)
        esel = sb("esel", [P, TM, 8], over="extra", skip=1 * E + 704)
        em8 = sb("em8", [P, TM, 8], over="extra", skip=1 * E + 832)
        ei8 = sb("ei8", [P, TM, 8], U32, over="extra", skip=2 * E)
        w01 = sb("w01", [P, TM, 2], over="extra", skip=2 * E + 128)
        ed = sb("ed", [P, TM, 1], over="extra", skip=2 * E + 192)
        ex = sb("ex", [P, TM, 1], over="extra", skip=2 * E + 256)
        eid = sb("eid", [P, TM, 2], over="extra", skip=2 * E + 320)
        etmp = sb("etmp", [P, TM, 8, 4], over="extra", skip=3 * E)
        sel0 = sb("sel0", [P, TM, EXPERTS], over="extra", skip=4 * E)
        sel1 = sb("sel1", [P, TM, EXPERTS], over="extra", skip=5 * E)
        cnt = sb("cnt", [P, TM, EXPERTS], over="extra", skip=6 * E)
        rt1 = sb("rt1", [P, TM, EXPERTS], over="extra", skip=7 * E)
        rt2 = sb("rt2", [P, TM, EXPERTS], over="extra", skip=8 * E)
        tab = sb("tab", [P, EXPERTS, TM, 3], over="extra", skip=9 * E)
        most = sb("most", [P, 1], over="extra", skip=11 * E)
        mosti = sb("mosti", [P, 1], I32, over="extra", skip=11 * E + 64)
        te = sb("te", [P, 2, TM, 3], over="extra", skip=11 * E + 128)
        oh = sb("oh", [P, 2, TM, SLOTS], over="extra", skip=12 * E)
        ohr = sb("ohr", [P, 2, TM, SLOTS], over="extra", skip=14 * E)
        xg = sb("xg", [P, 2, KD, SLOTS], over="extra", skip=16 * E)
        sg = sb("sg", [P, FE], over="extra", skip=20 * E)
        hh = sb("hh", [P, FE], over="extra", skip=22 * E)
        hT = sb("hT", [P, KF, SLOTS], over="extra", skip=24 * E)
        yw = sb("yw", [P, 2, 512], over="extra", skip=25 * E)
        wcol = sb("wcol", [P, 2, 1], over="extra", skip=29 * E)
        idx = sb("idx", [P, 2, 1], U32, over="extra", skip=29 * E + 64)
        iotac = sb("iotac", [P, SLOTS], over="extra", skip=30 * E)
        yin = sb("yin", [P, 2, 2, D], over="extra", skip=32 * E)

        ps = ctx.enter_context(nc.psum_tensor("ps", [P, 8, 512], F32))
        ydram = [nc.dram_tensor(f"y_scratch{l}", [4 * T, 512], F32).ap() for l in range(LAYERS)]

        ring_full = [sem(f"ring_full{i}") for i in range(RING)]
        wh_ready, wl_ready, w_used = sem("wh_ready"), sem("wl_ready"), sem("w_used")
        acc_done = sem("acc_done")
        taken = [sem("taken0"), sem("taken1")]
        expert_used = sem("expert_used")
        consts_ready = sem("consts_ready")
        params = sem("params_loaded")
        x_loaded = sem("x_loaded")
        gain_loaded = [sem("gain_loaded0"), sem("gain_loaded1")]
        norms_done = sem("norms_done")
        squares = sem("squares")
        var_ready, rstd_ready = sem("var_ready"), sem("rstd_ready")
        nat_ready = sem("nat_ready")
        hi_ready = sem("hi_ready")
        sq_ready, sq_used = sem("sq_ready"), sem("sq_used")
        heads_ready = sem("heads_ready")
        res_added = sem("res_added")
        out_stored = sem("out_stored")
        S = {n: sem(n) for n in (
            "small_loaded0 small_loaded1 small_loaded2 small_hi small_lo "
            "f_z f_e f_ln f_ready negc_ready c_row v_ready xb_ready sp_e sp_ln xc_ready rg_sig rg_l rg_exp rg_var "
            "rg_sqrt rec_ready rec_hi rec_lo gate_ready "
            "s_done mx_done p_done pt_done pt_copied o_done o_copied "
            "mem_loaded v_pre v_out vbias_loaded bs_loaded v_scaled ws_loaded ws_masked gt_ready gt_hi gt_lo "
            "g_sub g_exp e_sub e_exp cnt_ready tab_ready "
            "oh_ready x_gathered xg_ready info_ready gu_done silu_done h_ready hT_done hT_ready y_done yw_ready y_added"
        ).split()}
        y_stored = [[sem(f"y_stored{l}_{p}") for p in range(2)] for l in range(LAYERS)]
        y_in = [sem("y_in0"), sem("y_in1")]
        over_full = [sem(f"over_full{l}") for l in range(LAYERS)]
        over_step = [sem(f"over_step{l}") for l in range(LAYERS)]
        over_stored = [sem(f"over_stored{l}") for l in range(LAYERS)]
        chain, achain, pchain = sem("dve_chain"), sem("act_chain"), sem("pool_chain")
        dve_loop = sem("dve_loop_chain")
        settled = sem("settled")

        block = ctx.enter_context(nc.Block())

        x_in = A["x"].rearrange("b (m p) d -> p (b m) d", p=P)
        x_out = out.rearrange("b (m p) d -> p (b m) d", p=P)
        mem_in = A["mem"].rearrange("b (m p) d -> p (b m) d", p=P)
        IN_COL = [0, A_W, 2 * A_W, 3 * A_W + A_HEADS, 3 * A_W + A_HEADS + B_W]

        def kcols(w, c0, n):
            return w[:, c0:c0 + n].rearrange("(k p) n -> p k n", p=P)

        def dense_unit(name, l, u):
            if name == "cout":
                c, half = divmod(u, 2)
                return kcols(A["c_w_out"][0], 256 * c, 256)[:, 8 * half:8 * half + 8], 256
            c = u // 2
            w, col = {"in": (A["ab_w_in"][0], IN_COL[c % 5]),
                      "out": (A["ab_w_out"][0], 512 * c),
                      "cin": (A["c_w_in"][0], 512 * ((c + 4) % 8)),
                      "kv": (A["x_wkv"][l], 512 * c),
                      "xq": (A["x_wq"][l], 512 * c),
                      "xo": (A["x_wo"][l], 512 * c)}[name]
            return kcols(w, col, 512)[:, 4 * (u % 2):4 * (u % 2) + 4], 512

        def row_bcast(v, n):
            return v.rearrange("(a n) -> a n", a=1).to_broadcast([P, n])

        def expert_unit(l, e, j):
            w = A["moe_w_down"] if j >= 4 else A[("moe_w_gate", "moe_w_up")[j % 2]]
            src = w[l][bass.ds(e, 1)].rearrange("a (k p) f -> p (a k) f", p=P)
            return (src[:, 4 * (j // 2):4 * (j // 2) + 4], 512) if j < 4 else (src[:, 2 * (j - 4):2 * (j - 4) + 2], 1024)

        def units_before(unit):
            dense = sum(min(max(unit - u, 0), n) for (name, _), (u, n) in PLAN.items() if name != "moe")
            return dense, unit - dense

        def slot(unit, cols):
            return ring[:, unit % RING, :].rearrange("p (k n) -> p k n", n=cols)

        def after(eng, s, n):
            if not isinstance(n, int) or n > 0:
                eng.wait_ge(s, n)

        def settle(eng):
            eng.sem_inc(settled, 1)

        def round_done(eng, name):
            if name[0] in DENSE:
                steps = {"cout": 8}.get(name[0], 8)
                eng.wait_ge(w_used, STEP0[name[:2]] + steps * (name[2] + 1))
            else:
                eng.wait_ge(acc_done, PLAIN[name] + 1)
            return 4 * (ROUND[name] % 2)

        def took(name):
            return taken[ROUND[name] % 2]

        def wait_taken(eng, name):
            eng.wait_ge(taken[ROUND[name] % 2], ROUND[name] // 2 + 1)

        def all_taken(eng, next_name):
            r = ROUND[next_name] if next_name in ROUND else len(ROUND)
            eng.wait_ge(taken[0], (r + 1) // 2)
            eng.wait_ge(taken[1], r // 2)

        def split_hi(act, pos, upto):
            for t in range(pos, upto):
                unit, s = unit_of_step(t)
                if s == 0:
                    act.wait_ge(ring_full[unit % RING], 16 * (unit // RING + 1))
                after(act, w_used, t - STAGE + 1)
                act.activation(wh[:, t % STAGE, :], ring[:, unit % RING, 512 * s:512 * (s + 1)],
                               ACT.Copy).then_inc(wh_ready, 1)
            return max(pos, upto)

        def split_lo(dve, pos, upto):
            for t in range(pos, upto):
                unit, s = unit_of_step(t)
                dve.wait_ge(wh_ready, t + 1)
                dve.tensor_tensor(wl[:, t % STAGE, :], ring[:, unit % RING, 512 * s:512 * (s + 1)],
                                  wh[:, t % STAGE, :].bitcast(F32), ALU.subtract).then_inc(wl_ready, 1)
            return max(pos, upto)

        def unit_of_step(t):
            for key, t0 in STEP0.items():
                if t0 <= t < t0 + STEPS * PLAN[key][1]:
                    return PLAN[key][0] + (t - t0) // STEPS, (t - t0) % STEPS
            raise AssertionError(t)

        N_STEPS = _steps
        items_a = [(h, i) for h in range(A_HEADS) for i in range(TM)]
        items_x = [(h, i) for h in range(X_HEADS) for i in range(TM)]
        ATT0 = {}
        n_att = 0
        for l in range(LAYERS):
            if l % 2 == 0:
                ATT0["a", l] = n_att
                n_att += len(items_a)
            ATT0["x", l] = n_att
            n_att += len(items_x)


        @block.sync
        def _(sp):
            for m in range(TM):
                sp.dma_start(x[:, m, :], x_in[:, m, :]).then_inc(x_loaded, 16)

            def expert_done_with(l, e, j):
                if j in (3, 5):
                    sp.wait_ge(S["gu_done" if j == 3 else "y_done"], e + EXPERTS * l)
                else:
                    sp.wait_ge(expert_used, e * 4 + (4 * (EXPERTS * l - 1) + (1, 2, 3, 0, 4)[j]))

            def free_slot(unit):
                if unit >= RING:
                    dense, moe = units_before(unit - RING + 1)
                    if dense > units_before(unit - RING)[0]:
                        sp.wait_ge(wl_ready, STEPS * dense)
                    else:
                        expert_done_with((moe - 1) // (6 * EXPERTS), EXPERTS, (moe - 1) % 6)

            for (name, l), (u0, n) in PLAN.items():
                if name != "moe":
                    for u in range(u0, u0 + n):
                        free_slot(u)
                        src, cols = dense_unit(name, l, u - u0)
                        sp.dma_start(slot(u, cols), src).then_inc(ring_full[u % RING], 16)
                    continue
                for j in range(6):
                    free_slot(u0 + j)
                    src, cols = expert_unit(l, 0, j)
                    sp.dma_start(slot(u0 + j, cols), src).then_inc(ring_full[(u0 + j) % RING], 16)
                with sp.Fori(1, EXPERTS) as e:
                    for j in range(6):
                        expert_done_with(l, e, j)
                        src, cols = expert_unit(l, e, j)
                        sp.dma_start(slot(u0 + j, cols), src).then_inc(ring_full[(u0 + j) % RING], 16)
                sp.wait_ge(S["tab_ready"], l + 1)
                n = sp.value_load(mosti[0:1, 0:1], min_val=0, max_val=T)
                with sp.Fori(1, PASSES) as c:
                    with sp.If(n > c * SLOTS):
                        expert_done_with(l, EXPERTS, 5)
                        with sp.Fori(0, EXPERTS) as e:
                            sp.wait_ge(over_step[l], c * (15 * EXPERTS) + e * 15 + (1 - 15 * EXPERTS))
                            for j in range(6):
                                src, cols = expert_unit(l, e, j)
                                sp.dma_start(slot(u0 + j, cols), src).then_inc(over_full[l], 16)
                        sp.wait_ge(over_step[l], c * (15 * EXPERTS) + 1)
                        settle(sp)
                    sp.nop()
            sp.wait_ge(out_stored, 16 * TM)

        @block.tensor
        def _(pe):
            pe.wait_ge(consts_ready, 1)

            def begin(name):
                r = ROUND[name]
                after(pe, taken[r % 2], r // 2)
                return 4 * (r % 2)

            def dense(name, l, c, hi, lo, cols=512, flip=False, rows=TM):
                b = begin((name, l, c))
                per = 512 // cols
                for s in range(8):
                    t = STEP0[name, l] + 8 * c + s
                    pe.wait_ge(wl_ready, t + 1)
                    for kk in range(per):
                        k = s * per + kk
                        for m in range(rows):
                            for i, (w, a) in enumerate(((wh, hi), (wl, hi), (wh, lo))):
                                flags = dict(start=(k == 0 and i == 0), stop=(k == 8 * per - 1 and i == 2))
                                if flip:
                                    mm = pe.matmul(ps[:, b + m, 0:T], w[:, t % STAGE, m * P:(m + 1) * P],
                                                   a[:, k, :], **flags)
                                else:
                                    mm = pe.matmul(ps[:, b + m, 0:cols], a[:, k, m * P:(m + 1) * P],
                                                   w[:, t % STAGE, kk * cols:(kk + 1) * cols], **flags)
                    mm.then_inc(w_used, 1)

            nats = [0]

            def norm_T(kind, l, tiles):
                for m in range(tiles):
                    b = begin((kind, l, m))
                    nats[0] += 1
                    pe.wait_ge(nat_ready, nats[0])
                    for k in range(KD):
                        mm = pe.transpose(ps[:, b + k // 4, (k % 4) * P:(k % 4 + 1) * P],
                                          nat[:, m % 2, k * P:(k + 1) * P], ident[:, :])
                    mm.then_inc(acc_done, 1)
                for m in range(max(0, tiles - 2), tiles):
                    wait_taken(pe, (kind, l, m))

            def small(name, l, cols, which, count):
                b = begin((name, l, 0))
                pe.wait_ge(S["small_lo"], which + 1)
                for m in range(TM):
                    for k in range(KD):
                        for i, (w, a) in enumerate(((whs, ah), (wls, ah), (whs, al))):
                            mm = pe.matmul(ps[:, b, m * 64:m * 64 + cols], a[:, k, m * P:(m + 1) * P],
                                           w[:, k, 0:cols], start=(k == 0 and i == 0), stop=(k == KD - 1 and i == 2))
                mm.then_inc(acc_done, 1)

            def attention(kind, l, items, nk_of, score, v_of, ow, next_name):
                n0 = ATT0[kind, l]
                all_taken(pe, next_name)

                def scores(n):
                    if n >= 2:
                        pe.wait_ge(S["p_done"], n0 + n - 1)
                    score(*items[n], n % 2).then_inc(S["s_done"], 1)

                def transposes(n):
                    h, i = items[n]
                    pe.wait_ge(S["p_done"], n0 + n + 1)
                    if n >= 2:
                        pe.wait_ge(S["pt_copied"], n0 + n - 1)
                    for j in range(nk_of(i)):
                        mm = pe.transpose(ps[:, 2 + n % 2, j * P:(j + 1) * P],
                                          prob[:, n % 2, j * P:(j + 1) * P], ident[:, :])
                    mm.then_inc(S["pt_done"], 1)

                def values(n):
                    h, i = items[n]
                    pe.wait_ge(S["pt_copied"], n0 + n + 1)
                    if n >= 2:
                        pe.wait_ge(S["o_copied"], n0 + n - 1)
                    for j in range(nk_of(i)):
                        mm = pe.matmul(ps[:, 4 + n % 2, 0:ow], probT[:, n % 2, j * P:(j + 1) * P],
                                       v_of(j, h), start=(j == 0), stop=(j == nk_of(i) - 1))
                    mm.then_inc(S["o_done"], 1)

                scores(0)
                for n in range(len(items)):
                    if n + 1 < len(items):
                        scores(n + 1)
                    transposes(n)
                    if n:
                        values(n - 1)
                values(len(items) - 1)
                pe.wait_ge(S["o_copied"], n0 + len(items))

            def fox(l):
                for c in range(3):
                    dense("in", l, c, ah, al)
                small("f", l, A_HEADS, 0, 0)
                for c in (3, 4):
                    dense("in", l, c, ah, al, flip=True)
                b = begin(("fT", l, 0))
                pe.wait_ge(S["f_ready"], 1)
                for m in range(TM):
                    mm = pe.transpose(ps[0:A_HEADS, b, m * P:(m + 1) * P], zf[:, m, :], ident[:, :])
                mm.then_inc(acc_done, 1)
                for name, src, n in (("qT", qn, 1), ("kT", kn, 2)):
                    pe.wait_ge(heads_ready, n)
                    for r in range(2):
                        b = begin((name, l, r))
                        for j in range(4):
                            h = 4 * r + j
                            for m in range(TM):
                                mm = pe.transpose(ps[0:A_DIM, b + j, m * P:(m + 1) * P],
                                                  src[:, m, h * A_DIM:(h + 1) * A_DIM], ident[:, :])
                        mm.then_inc(acc_done, 1)
                pe.wait_ge(S["xc_ready"], 1)
                for g in range(2):
                    b = begin(("rg", l, g))
                    for m in range(4):
                        mm = pe.matmul(ps[:, b + m, :], wblk[:, g, m, :], xcT[:, m, :], start=True, stop=True)
                    mm.then_inc(acc_done, 1)
                pe.wait_ge(S["c_row"], 16)
                wait_taken(pe, ("in", l, 2))

                def score(h, i, bank):
                    n = (i + 1) * P
                    pe.matmul(ps[:, bank, 0:n], qT[:, h, i * P:(i + 1) * P], kT[:, h, 0:n], start=True, stop=False)
                    return pe.matmul(ps[:, bank, i * P:n], ident[:, :], causal[:, :], start=False, stop=True)

                attention("a", l, items_a, lambda i: i + 1, score,
                          lambda j, h: v0[:, j, h * A_DIM:(h + 1) * A_DIM], A_DIM, ("oT", l, 0))
                for m in range(TM):
                    b = begin(("oT", l, m))
                    for k in range(4):
                        mm = pe.transpose(ps[:, b, k * P:(k + 1) * P], on0[:, m, k * P:(k + 1) * P], ident[:, :])
                    mm.then_inc(acc_done, 1)
                for m in (TM - 2, TM - 1):
                    wait_taken(pe, ("oT", l, m))
                pe.wait_ge(S["rec_lo"], 4)
                for c in range(2):
                    dense("out", l, c, ah, al)

            def gmlp(l):
                for c in range(4):
                    dense("cin", l, c, ah, al)
                b = begin(("wsT", l, 0))
                pe.wait_ge(S["ws_masked"], 1)
                for g in range(C_GROUPS):
                    mm = pe.transpose(ps[:, b + g // 4, (g % 4) * P:(g % 4 + 1) * P], wsn[:, g, :], ident[:, :])
                mm.then_inc(acc_done, 1)
                for c in range(4, 8):
                    dense("cin", l, c, ah, al, flip=True)
                pe.wait_ge(S["v_scaled"], TM)
                for r in range(4):
                    b = begin(("mix", l, r))
                    for j in range(4):
                        kt = 4 * r + j
                        for n in range(TM):
                            mm = pe.matmul(ps[:, b + j, n * P:(n + 1) * P], v1[:, n, kt * P:(kt + 1) * P],
                                           wsT[:, kt // 2, :], start=True, stop=True)
                    mm.then_inc(acc_done, 1)
                pe.wait_ge(S["gt_lo"], 16)
                for c in range(4):
                    dense("cout", l, c, gh, gl, cols=256)

            def cross(l):
                norm_T("nmem", l, MM)
                for c in range(4):
                    dense("kv", l, c, mh, ml, rows=MM)
                n0 = (2 if l == 0 else 6)
                pe.wait_ge(heads_ready, n0 + 2)
                for r in range(2):
                    b = begin(("xkT", l, r))
                    for j in range(4):
                        for m in range(MM):
                            mm = pe.transpose(ps[:, b + j, m * P:(m + 1) * P],
                                              xkn[:, m, (4 * r + j) * P:(4 * r + j + 1) * P], ident[:, :])
                    mm.then_inc(acc_done, 1)
                norm_T("ncross", l, TM)
                for c in range(2):
                    dense("xq", l, c, ah, al)
                for r in range(2):
                    b = begin(("xqT", l, r))
                    pe.wait_ge(heads_ready, n0 + 3 + r)
                    for j in range(4):
                        for m in range(TM):
                            mm = pe.transpose(ps[:, b + j, m * P:(m + 1) * P],
                                              xqn[:, m, (4 * r + j) * P:(4 * r + j + 1) * P], ident[:, :])
                    mm.then_inc(acc_done, 1)

                def score(h, i, bank):
                    for kk in range(2):
                        mm = pe.matmul(ps[:, bank, 0:MEM], xqT[:, 2 * h + kk, i * P:(i + 1) * P],
                                       xkT[:, 2 * h + kk, :], start=(kk == 0), stop=(kk == 1))
                    return mm

                attention("x", l, items_x, lambda i: MM, score,
                          lambda j, h: xv[:, j, h * X_DIM:(h + 1) * X_DIM], X_DIM, ("xoT", l, 0))
                for m in range(TM):
                    b = begin(("xoT", l, m))
                    for k in range(KD):
                        mm = pe.transpose(ps[:, b + k // 4, (k % 4) * P:(k % 4 + 1) * P],
                                          xon[:, m, k * P:(k + 1) * P], ident[:, :])
                    mm.then_inc(acc_done, 1)
                for m in (TM - 2, TM - 1):
                    wait_taken(pe, ("xoT", l, m))
                for c in range(2):
                    dense("xo", l, c, ah, al)

            def gather(l, p):
                for k in range(KD):
                    for m in range(TM):
                        pe.matmul(ps[:, 0, k * SLOTS:(k + 1) * SLOTS], x[:, m, k * P:(k + 1) * P], ohr[:, p, m, :],
                                  start=(m == 0), stop=(m == TM - 1))
                for half in range(2):
                    for m in range(TM):
                        mm = pe.matmul(ps[half * SLOTS:(half + 1) * SLOTS, 1, 0:2], oh[:, p, m, :], te[:, p, m, 1:3],
                                       start=(m == 0), stop=(m == TM - 1))
                return mm

            def gate_up(u0, p, full, used):
                for k in range(KD):
                    if k % 4 == 0:
                        full(k // 2)
                        full(k // 2 + 1)
                    for half in range(2):
                        w = slot(u0 + 2 * (k // 4) + half, 512)
                        mm = pe.matmul(ps[half * SLOTS:(half + 1) * SLOTS, 2 + p, :], xg[:, p, k, :], w[:, k % 4, :],
                                       start=(k == 0), stop=(k == KD - 1))
                        if k % 4 == 3 and used and k < KD - 1:
                            mm.then_inc(expert_used, 1)
                        if k == KD - 1 and half == 0 and used:
                            mm.then_inc(expert_used, 1)
                return mm

            def hidden_T():
                for k in range(KF):
                    mm = pe.transpose(ps[:, 4, k * P:(k + 1) * P], hh[:, k * P:(k + 1) * P],
                                      ident[:, :])
                return mm

            def down(u0, p, full, used):
                for k in range(KF):
                    if k % 2 == 0:
                        full(4 + k // 2)
                    w = slot(u0 + 4 + k // 2, 1024)
                    for half in range(2):
                        mm = pe.matmul(ps[half * SLOTS:(half + 1) * SLOTS, 5 + p, :], hT[:, k, :],
                                       w[:, k % 2, 512 * half:512 * (half + 1)], start=(k == 0), stop=(k == KF - 1))
                    if k == 1 and used:
                        mm.then_inc(expert_used, 1)
                return mm

            def experts(l):
                u0 = PLAN["moe", l][0]
                e0 = EXPERTS * l
                all_taken(pe, ("nmix", l + 1, 0))

                def do_gather(e, p):
                    pe.wait_ge(S["oh_ready"], e + (e0 + 1))
                    after(pe, S["info_ready"], e + e0)
                    gather(l, p).then_inc(S["x_gathered"], 1)

                def expert(e, p, last=False):
                    def full(j):
                        pe.wait_ge(ring_full[(u0 + j) % RING], (e + ((u0 + j) // RING + 1)) * 16)
                    pe.wait_ge(S["xg_ready"], e + (e0 + 1))
                    after(pe, S["h_ready"], e + (e0 - 1))
                    gate_up(u0, p, full, True).then_inc(S["gu_done"], 1)
                    if not last:
                        do_gather(e + 1, 1 - p)
                    pe.wait_ge(S["h_ready"], e + (e0 + 1))
                    after(pe, S["hT_ready"], e + e0)
                    hidden_T().then_inc(S["hT_done"], 1)
                    pe.wait_ge(S["hT_ready"], e + (e0 + 1))
                    after(pe, S["yw_ready"], e + (e0 - 1))
                    down(u0, p, full, True).then_inc(S["y_done"], 1)

                do_gather(0, 0)
                expert(0, 0)
                expert(1, 1)
                with pe.Fori(1, EXPERTS // 2 - 1) as i:
                    for p in range(2):
                        expert(i * 2 + p, p)
                expert(EXPERTS - 2, 0)
                expert(EXPERTS - 1, 1, last=True)
                n = pe.value_load(mosti[0:1, 0:1], min_val=0, max_val=T)
                with pe.Fori(1, PASSES) as c:
                    with pe.If(n > c * SLOTS):
                        with pe.Fori(0, EXPERTS) as e:
                            at_ = lambda k: c * (15 * EXPERTS) + e * 15 + (1 - 15 * EXPERTS + k)
                            pe.wait_ge(over_step[l], at_(3))
                            gather(l, 0).then_inc(over_step[l], 1)
                            pe.wait_ge(over_step[l], at_(7))
                            pe.wait_ge(over_full[l], c * (96 * EXPERTS) + e * 96 + (96 - 96 * EXPERTS))
                            gate_up(u0, 0, lambda j: None, False).then_inc(over_step[l], 1)
                            pe.wait_ge(over_step[l], at_(10))
                            hidden_T().then_inc(over_step[l], 1)
                            pe.wait_ge(over_step[l], at_(12))
                            down(u0, 0, lambda j: None, False).then_inc(over_step[l], 1)
                        pe.wait_ge(over_step[l], c * (15 * EXPERTS) + 1)
                        settle(pe)
                    pe.nop()

            for l in range(LAYERS):
                norm_T("nmix", l, TM)
                fox(l) if l % 2 == 0 else gmlp(l)
                cross(l)
                norm_T("nffn", l, TM)
                small("route", l, GROUPS + EXPERTS, l + 1, 0)
                b = begin(("rank", l, 0))
                pe.wait_ge(S["cnt_ready"], l + 1)
                for m in range(TM):
                    for mm_ in range(m + 1):
                        mm = pe.matmul(ps[:, b, m * EXPERTS:(m + 1) * EXPERTS], (before if mm_ == m else ones)[:, :],
                                       cnt[:, mm_, :], start=(mm_ == 0), stop=(mm_ == m))
                for m in range(TM):
                    mm = pe.matmul(ps[:, b, TM * EXPERTS:(TM + 1) * EXPERTS], ones[:, :], cnt[:, m, :],
                                   start=(m == 0), stop=(m == TM - 1))
                mm.then_inc(acc_done, 1)
                experts(l)

        @block.scalar
        def _(act):
            pos = [0]
            links = [0]

            def link(ins):
                links[0] += 1
                ins.then_inc(achain, 1)
                act.wait_ge(achain, links[0])

            def split(key, c):
                pos[0] = split_hi(act, pos[0], STEP0[key] + 8 * (c + 1))

            def split_next():
                pos[0] = split_hi(act, pos[0], min(pos[0] + STAGE, N_STEPS))

            nsq = [0]

            def norm_squares(src, tiles, ready):
                ready()
                for m in range(tiles):
                    after(act, squares, nsq[0])
                    nsq[0] += 1
                    act.activation(junk[:, :], src[:, m, :], ACT.Square, accum_out=ss[:, m:m + 1]).then_inc(squares, 1)

            def tile_hi(name, dst, m, kts, k0=0):
                b = round_done(act, name)
                src = ps[:, b:b + -(-kts // 4), :].rearrange("p a (k n) -> p (a k) n", n=P)
                act.activation(dst[:, k0:k0 + kts, m * P:(m + 1) * P], src, ACT.Copy).then_inc(hi_ready, 1)

            sqs = [0]

            def head_squares(name, tiles):
                b = round_done(act, name)
                for m in range(tiles):
                    after(act, sq_used, sqs[0] - 1)
                    act.activation(sq[:, sqs[0] % 2, :], ps[:, b + m, :], ACT.Square).then_inc(sq_ready, 1)
                    sqs[0] += 1

            def copy_out(name, dst, tiles, func=ACT.Copy, bias=None):
                b = round_done(act, name)
                for m in range(tiles):
                    kw = {} if bias is None else dict(bias=bias(m))
                    ins = act.activation(dst(m), ps[:, b + m, :], func, **kw)
                ins.then_inc(took(name), 1)

            def attention(kind, l, items, nk_of, hooks):
                n0 = ATT0[kind, l]

                def exps(n):
                    h, i = items[n]
                    w = nk_of(i) * P
                    act.wait_ge(S["mx_done"], n0 + n + 1)
                    if n >= 2:
                        act.wait_ge(S["pt_done"], n0 + n - 1)
                    act.activation(prob[:, n % 2, 0:w], ps[:, n % 2, 0:w], ACT.Exp, bias=nmax[:, n:n + 1],
                                   accum_out=rsum[:, n:n + 1]).then_inc(S["p_done"], 1)

                def copies(n):
                    w = nk_of(items[n][1]) * P
                    act.wait_ge(S["pt_done"], n0 + n + 1)
                    if n >= 2:
                        act.wait_ge(S["o_done"], n0 + n - 1)
                    act.activation(probT[:, n % 2, 0:w], ps[:, 2 + n % 2, 0:w], ACT.Copy).then_inc(S["pt_copied"], 1)

                exps(0)
                for n in range(len(items)):
                    if n + 1 < len(items):
                        exps(n + 1)
                    copies(n)
                    if n in hooks:
                        hooks[n]()

            def fox(l):
                split(("in", l), 0)
                split(("in", l), 1)
                head_squares(("in", l, 0), TM)
                split(("in", l), 2)
                head_squares(("in", l, 1), TM)
                split_next()
                copy_out(("in", l, 2), lambda m: v0[:, m, :], TM)
                split(("in", l), 3)
                act.wait_ge(S["f_z"], 2)
                act.activation(ef[:, :, :], ef[:, :, :], ACT.Exp).then_inc(S["f_e"], 1)
                act.activation(spl[:, :], spl[:, :], ACT.Exp).then_inc(S["f_e"], 1)
                act.wait_ge(S["f_e"], 2)
                act.activation(ef[:, :, :], ef[:, :, :], ACT.Ln, bias=onecol[:, :]).then_inc(S["f_ln"], 1)
                act.activation(spl[:, :], spl[:, :], ACT.Ln, bias=onecol[:, :]).then_inc(S["f_ln"], 1)
                split(("in", l), 4)
                copy_out(("in", l, 3), lambda m: xbT[:, m, :], 4)
                split_next()
                copy_out(("in", l, 4), lambda m: gbT[:, m, :], 4, ACT.Gelu_apprx_tanh)
                act.wait_ge(S["negc_ready"], 1)
                act.dma_start(kT[A_DIM:A_DIM + 1, :, :], negc[:, :]).then_inc(S["c_row"], 16)
                for r in range(2):
                    b = round_done(act, ("qT", l, r))
                    for j in range(4):
                        ins = act.activation(qT[0:A_DIM, 4 * r + j, :], ps[0:A_DIM, b + j, :], ACT.Copy, scale=qg[:, :])
                    ins.then_inc(took(("qT", l, r)), 1)
                for g, (dst, bias) in enumerate(((xbT, bab), (iT, bxb))):
                    b = round_done(act, ("rg", l, g))
                    if g == 1:
                        wait_taken(act, ("qT", l, 1))
                    for m in range(4):
                        ins = act.activation(dst[:, m, :], ps[:, b + m, :], ACT.Sigmoid, bias=bias[:, m:m + 1])
                    ins.then_inc(took(("rg", l, g)), 1)

                def decay(m):
                    def run():
                        act.wait_ge(S["rg_l"], m + 1)
                        if m >= 2:
                            act.wait_ge(S["rg_var"], m - 1)
                        act.activation(aT[:, m, :], xbT[:, m, :], ACT.Exp)
                        act.activation(tanhs[:, m % 2, :], xbT[:, m, :], ACT.Tanh, scale=-1.0).then_inc(S["rg_exp"], 1)
                    return run

                def roots():
                    act.wait_ge(S["rg_var"], 4)
                    for m in range(4):
                        act.activation(xbT[:, m, :], xbT[:, m, :], ACT.Sqrt).then_inc(S["rg_sqrt"], 1)

                def rec_his():
                    for m in range(4):
                        act.wait_ge(S["rec_ready"], m + 1)
                        act.activation(ah[:, 4 + m, :], gbT[:, m, :], ACT.Copy).then_inc(S["rec_hi"], 1)

                attention("a", l, items_a, lambda i: i + 1,
                          {2: decay(0), 5: decay(1), 9: decay(2), 13: decay(3), 17: roots, 30: rec_his})
                for m in range(TM):
                    tile_hi(("oT", l, m), ah, m, 4)
                split(("out", l), 0)
                split(("out", l), 1)

            def gmlp(l):
                for c in range(5):
                    if c < 4:
                        split(("cin", l), c)
                    else:
                        split_next()
                    if c:
                        for m in range(TM):
                            n = (c - 1) * TM + m
                            act.wait_ge(S["v_pre"], n + 1)
                            link(act.activation(v1[:, m, (c - 1) * 512:c * 512], gt[:, n % 2, :], ACT.Gelu_apprx_tanh))
                            act.activation(vjunk[:, :], v1[:, m, (c - 1) * 512:c * 512], ACT.Square,
                                           accum_out=ss[:, 4 * m + c - 1:4 * m + c]).then_inc(S["v_out"], 1)
                split(("cin", l), 4)
                b = round_done(act, ("wsT", l, 0))
                act.activation(wsT[:, :, :], ps[:, b:b + 2, :].rearrange("p a (g n) -> p (a g) n", n=P),
                               ACT.Copy).then_inc(took(("wsT", l, 0)), 1)
                for c in range(4, 8):
                    if c < 7:
                        split(("cin", l), c + 1)
                    else:
                        split_next()
                    copy_out(("cin", l, c), lambda m: uT[:, 4 * (c - 4) + m, :], 4, ACT.Gelu_apprx_tanh,
                             lambda m: ub[:, 4 * (c - 4) + m:4 * (c - 4) + m + 1])
                for kt in range(16):
                    act.wait_ge(S["gt_ready"], kt + 1)
                    act.activation(gh[:, kt, :], gt[:, kt % 2, :], ACT.Copy).then_inc(S["gt_hi"], 1)
                for c in range(4):
                    split(("cout", l), c)

            def cross(l):
                norm_squares(mem, MM, lambda: act.wait_ge(S["mem_loaded"], 16 * (l + 1)))
                for m in range(MM):
                    tile_hi(("nmem", l, m), mh, m, KD)
                for c in range(4):
                    split(("kv", l), c)
                    if c in (1, 2):
                        head_squares(("kv", l, c - 1), MM)
                    if c == 3:
                        copy_out(("kv", l, 2), lambda m: xv[:, m, 0:512], MM)
                split_next()
                copy_out(("kv", l, 3), lambda m: xv[:, m, 512:1024], MM)
                norm_squares(x, TM, lambda: act.wait_ge(res_added, 3 * l + 1))
                for m in range(TM):
                    tile_hi(("ncross", l, m), ah, m, KD)
                split(("xq", l), 0)
                split(("xq", l), 1)
                head_squares(("xq", l, 0), TM)
                split_next()
                head_squares(("xq", l, 1), TM)
                for r in range(2):
                    b = round_done(act, ("xqT", l, r))
                    for j in range(4):
                        ins = act.activation(xqT[:, 4 * r + j, :], ps[:, b + j, :], ACT.Copy,
                                             scale=xqg[:, l, j % 2:j % 2 + 1])
                    ins.then_inc(took(("xqT", l, r)), 1)
                attention("x", l, items_x, lambda i: MM, {})
                for m in range(TM):
                    tile_hi(("xoT", l, m), ah, m, KD)
                split(("xo", l), 0)
                split(("xo", l), 1)

            def silu(p):
                return act.activation(sg[SLOTS:P, :], ps[0:SLOTS, 2 + p, :], ACT.Silu)

            def hidden_copy():
                return act.activation(hT[:, :, :], ps[:, 4, :].rearrange("p (k n) -> p k n", n=P)[:, :, 0:SLOTS], ACT.Copy)

            def weigh(p):
                return act.activation(yw[:, p, :], ps[:, 5 + p, :], ACT.Copy, scale=wcol[:, p, :])

            def experts(l):
                e0 = EXPERTS * l
                act.wait_ge(S["g_sub"], l + 1)
                act.activation(gee[:, :, :], ge[:, :, :], ACT.Exp).then_inc(S["g_exp"], 1)
                act.wait_ge(S["e_sub"], l + 1)
                act.activation(ex[:, :, :], ed[:, :, :], ACT.Exp).then_inc(S["e_exp"], 1)

                def expert(e, p, stored):
                    act.wait_ge(S["gu_done"], e + (e0 + 1))
                    after(act, S["h_ready"], e + e0)
                    silu(p).then_inc(S["silu_done"], 1)
                    act.wait_ge(S["hT_done"], e + (e0 + 1))
                    after(act, S["y_done"], e + e0)
                    hidden_copy().then_inc(S["hT_ready"], 1)
                    act.wait_ge(S["y_done"], e + (e0 + 1))
                    act.wait_ge(S["info_ready"], e + (e0 + 1))
                    after(act, y_stored[l][p], stored)
                    weigh(p).then_inc(S["yw_ready"], 1)

                expert(0, 0, 0)
                expert(1, 1, 0)
                with act.Fori(1, EXPERTS // 2) as i:
                    for p in range(2):
                        expert(i * 2 + p, p, i * 16)
                for p in range(2):
                    act.wait_ge(y_stored[l][p], 16 * (EXPERTS // 2))
                n = act.value_load(mosti[0:1, 0:1], min_val=0, max_val=T)
                with act.Fori(1, PASSES) as c:
                    with act.If(n > c * SLOTS):
                        with act.Fori(0, EXPERTS) as e:
                            at_ = lambda k: c * (15 * EXPERTS) + e * 15 + (1 - 15 * EXPERTS + k)
                            act.wait_ge(over_step[l], at_(8))
                            silu(0).then_inc(over_step[l], 1)
                            act.wait_ge(over_step[l], at_(11))
                            hidden_copy().then_inc(over_step[l], 1)
                            act.wait_ge(over_step[l], at_(13))
                            weigh(0).then_inc(over_step[l], 1)
                        act.wait_ge(over_step[l], c * (15 * EXPERTS) + 1)
                        settle(act)
                    act.nop()
                yv = ydram[l].rearrange("(k m p h) c -> p m k (h c)", k=2, m=TM, p=P)
                for m in range(TM):
                    if m >= 2:
                        act.wait_ge(S["y_added"], TM * l + m - 1)
                    act.dma_start(yin[:, m % 2, :, :], yv[:, m]).then_inc(y_in[m % 2], 16)

            act.wait_ge(S["small_loaded0"], 16)
            act.activation(whs[:, :, 0:A_HEADS], wsmall[:, :, 0:A_HEADS], ACT.Copy).then_inc(S["small_hi"], 1)
            for l in range(LAYERS):
                norm_squares(x, TM, (lambda: act.wait_ge(x_loaded, 16 * TM)) if l == 0
                             else (lambda: act.wait_ge(res_added, 3 * l)))
                for m in range(TM):
                    tile_hi(("nmix", l, m), ah, m, KD)
                fox(l) if l % 2 == 0 else gmlp(l)
                cross(l)
                act.wait_ge(S[f"small_loaded{l + 1}"], 32)
                act.activation(whs[:, :, :], wsmall[:, :, :], ACT.Copy).then_inc(S["small_hi"], 1)
                norm_squares(x, TM, lambda: act.wait_ge(res_added, 3 * l + 2))
                for m in range(TM):
                    tile_hi(("nffn", l, m), ah, m, KD)
                experts(l)
            for m in range(TM):
                act.wait_ge(S["y_added"], TM * (LAYERS - 1) + m + 1)
                act.dma_start(x_out[:, m, :], x[:, m, :]).then_inc(out_stored, 16)
            act.wait_ge(out_stored, 16 * TM)

        @block.vector
        def _(dve):
            pos = [0]
            links = [0]

            def link(ins):
                links[0] += 1
                ins.then_inc(chain, 1)
                dve.wait_ge(chain, links[0])

            def split(key, c):
                pos[0] = split_lo(dve, pos[0], STEP0[key] + 8 * (c + 1))

            def split_next():
                pos[0] = split_lo(dve, pos[0], min(pos[0] + STAGE, N_STEPS))

            norms, rstds, nsq, sqs = [0], [0], [0], [0]

            def inverse_rms(n, width):
                rstds[0] += 1
                dve.tensor_scalar(ss[:, 0:n], ss[:, 0:n], 1.0 / width, EPS, ALU.mult, ALU.add).then_inc(var_ready, 1)
                dve.wait_ge(rstd_ready, rstds[0])

            def norm(kind, l, src, tiles, dst_hi, dst_lo):
                n = norms[0]
                nsq[0] += tiles
                dve.wait_ge(squares, nsq[0])
                inverse_rms(tiles, D)
                dve.wait_ge(gain_loaded[n % 2], 16 * (n // 2 + 1))

                def scale(m):
                    if m >= 2:
                        round_done(dve, (kind, l, m - 2))
                    dve.scalar_tensor_tensor(out=nat[:, m % 2, :], in0=src[:, m, :], scalar=rstd[:, m:m + 1],
                                             in1=gain[:, n % 2, :], op0=ALU.mult, op1=ALU.mult).then_inc(nat_ready, 1)

                scale(0)
                scale(1)
                for m in range(tiles):
                    tile_lo((kind, l, m), dst_hi, dst_lo, m, KD)
                    if m + 2 < tiles:
                        scale(m + 2)
                norms[0] += 1
                if kind == "nffn":
                    link(dve.tensor_copy(rx[:, :], rstd[:, 0:TM]))
                link(dve.tensor_copy(rinv[:, 0:1], rstd[:, 0:1]))
                dve.engine_nop().then_inc(norms_done, 1)

            his = [0]

            def tile_lo(name, hi, lo, m, kts):
                his[0] += 1
                dve.wait_ge(hi_ready, his[0])
                b = 4 * (ROUND[name] % 2)
                src = ps[:, b:b + -(-kts // 4), :].rearrange("p a (k n) -> p (a k) n", n=P)
                dve.tensor_tensor(lo[:, 0:kts, m * P:(m + 1) * P], src,
                                  hi[:, 0:kts, m * P:(m + 1) * P].bitcast(F32), ALU.subtract).then_inc(took(name), 1)

            def heads(name, tiles, nh, dim, dst):
                for m in range(tiles):
                    dve.wait_ge(sq_ready, sqs[0] + 1)
                    ins = dve.tensor_reduce(ss[:, m * nh:(m + 1) * nh],
                                            sq[:, sqs[0] % 2, :].rearrange("p (h d) -> p h d", d=dim), AX.X, ALU.add)
                    ins.then_inc(sq_used, 1)
                    sqs[0] += 1
                dve.wait_ge(sq_used, sqs[0])
                inverse_rms(tiles * nh, dim)
                b = 4 * (ROUND[name] % 2)
                for m in range(tiles):
                    ins = dve.tensor_tensor(dst(m).rearrange("p (h d) -> p h d", d=dim),
                                            ps[:, b + m, :].rearrange("p (h d) -> p h d", d=dim),
                                            rstd[:, m * nh:(m + 1) * nh].unsqueeze(2).to_broadcast([P, nh, dim]), ALU.mult)
                ins.then_inc(took(name), 1)
                wait_taken(dve, name)
                dve.engine_nop().then_inc(heads_ready, 1)

            def residual(name, cols, last):
                b = round_done(dve, name)
                c = name[2]
                for m in range(TM):
                    xs = x[:, m, c * cols:(c + 1) * cols]
                    ins = dve.tensor_tensor(xs, ps[:, b + m, 0:cols], xs, ALU.add)
                ins.then_inc(took(name), 1)
                if last:
                    wait_taken(dve, name)
                    dve.engine_nop().then_inc(res_added, 1)

            def attention(kind, l, items, nk_of, ow, dst, hooks):
                n0 = ATT0[kind, l]

                def maxima(n):
                    w = nk_of(items[n][1]) * P
                    dve.wait_ge(S["s_done"], n0 + n + 1)
                    dve.tensor_reduce(nmax[:, n:n + 1], ps[:, n % 2, 0:w], AX.X, ALU.max, negate=True)\
                       .then_inc(S["mx_done"], 1)

                def outputs(n):
                    h, i = items[n]
                    dve.wait_ge(S["p_done"], n0 + n + 1)
                    link(dve.reciprocal(rinv[:, n:n + 1], rsum[:, n:n + 1]))
                    dve.wait_ge(S["o_done"], n0 + n + 1)
                    dve.tensor_scalar(dst[:, i, h * ow:(h + 1) * ow], ps[:, 4 + n % 2, 0:ow], rinv[:, n:n + 1], None,
                                      ALU.mult).then_inc(S["o_copied"], 1)

                maxima(0)
                for n in range(len(items)):
                    if n + 1 < len(items):
                        maxima(n + 1)
                    if n:
                        outputs(n - 1)
                    if n in hooks:
                        hooks[n]()
                outputs(len(items) - 1)

            def fox(l):
                split(("in", l), 0)
                split(("in", l), 1)
                heads(("in", l, 0), TM, A_HEADS, A_DIM, lambda m: qn[:, m, :])
                split(("in", l), 2)
                heads(("in", l, 1), TM, A_HEADS, A_DIM, lambda m: kn[:, m, :])
                split(("in", l), 3)
                b = round_done(dve, ("f", l, 0))
                fv = ps[:, b, 0:TM * 64].rearrange("p (m n) -> p m n", n=64)[:, :, 0:A_HEADS]
                dve.tensor_tensor(zf[:, :, :], fv, fbias[:, :].unsqueeze(1).to_broadcast([P, TM, A_HEADS]),
                                  ALU.add).then_inc(took(("f", l, 0)), 1)
                wait_taken(dve, ("f", l, 0))
                for dst, src in ((ef[:, :, :], zf[:, :, :]), (spl[:, :], lam[:, :])):
                    link(dve.tensor_scalar(dst, src, -1.0, None, ALU.mult))
                    dve.tensor_tensor(dst, dst, src, ALU.min).then_inc(S["f_z"], 1)
                link(dve.tensor_scalar(zf[:, :, :], zf[:, :, :], 0.0, None, ALU.min))
                link(dve.tensor_scalar(lam2[:, :], lam[:, :], 0.0, None, ALU.min))
                dve.wait_ge(S["f_ln"], 2)
                dve.tensor_tensor(zf[:, :, :], zf[:, :, :], ef[:, :, :], ALU.subtract).then_inc(S["f_ready"], 1)
                link(dve.tensor_tensor(spl[:, :], lam2[:, :], spl[:, :], ALU.subtract))
                link(dve.tensor_scalar(spl[:, :], spl[:, :], RG_C, None, ALU.mult))
                split(("in", l), 4)
                wait_taken(dve, ("in", l, 3))
                wait_taken(dve, ("nmix", l, TM - 1))
                for m in range(4):
                    link(dve.tensor_scalar(xcT[:, m, :], xbT[:, m, :], convw[:, m, CONV - 1:CONV], convb[:, m:m + 1],
                                           ALU.mult, ALU.add))
                    for k in range(CONV - 1):
                        s = CONV - 1 - k
                        ins = dve.scalar_tensor_tensor(out=xcT[:, m, s:T], in0=xbT[:, m, 0:T - s],
                                                       scalar=convw[:, m, k:k + 1], in1=xcT[:, m, s:T],
                                                       op0=ALU.mult, op1=ALU.add)
                        if m == 3 and k == CONV - 2:
                            ins.then_inc(S["xc_ready"], 1)
                        else:
                            link(ins)
                split_next()
                b = round_done(dve, ("fT", l, 0))
                link(dve.tensor_tensor_scan(negc[:, :], onecol[0:A_HEADS, :].to_broadcast([A_HEADS, T]), ps[0:A_HEADS, b, :], 0.0, ALU.mult, ALU.subtract))
                dve.engine_nop().then_inc(took(("fT", l, 0)), 1)
                dve.engine_nop().then_inc(S["negc_ready"], 1)
                for r in range(2):
                    b = round_done(dve, ("kT", l, r))
                    ins = dve.tensor_scalar(kT[0:A_DIM, 4 * r:4 * r + 4, :], ps[0:A_DIM, b:b + 4, :], kg[:, :], None,
                                            ALU.mult)
                    ins.then_inc(took(("kT", l, r)), 1)
                wait_taken(dve, ("rg", l, 0))
                wait_taken(dve, ("rg", l, 1))
                for m in range(4):
                    dve.tensor_tensor(iT[:, m, :], iT[:, m, :], xcT[:, m, :], ALU.mult)
                    dve.tensor_scalar(xbT[:, m, :], xbT[:, m, :], spl[:, m:m + 1], None, ALU.mult).then_inc(S["rg_l"], 1)

                def variance(m):
                    def run():
                        dve.wait_ge(S["rg_exp"], m + 1)
                        link(dve.tensor_tensor(xbT[:, m, :], aT[:, m, :], aT[:, m, :], ALU.mult))
                        dve.scalar_tensor_tensor(out=xbT[:, m, :], in0=xbT[:, m, :], scalar=1.0, in1=tanhs[:, m % 2, :],
                                                 op0=ALU.add, op1=ALU.mult).then_inc(S["rg_var"], 1)
                    return run

                def recur(m):
                    def run():
                        dve.wait_ge(S["rg_sqrt"], m + 1)
                        link(dve.tensor_tensor(iT[:, m, :], iT[:, m, :], xbT[:, m, :], ALU.mult))
                        link(dve.tensor_tensor_scan(xbT[:, m, :], aT[:, m, :], iT[:, m, :], 0.0, ALU.mult, ALU.add))
                        dve.tensor_tensor(gbT[:, m, :], gbT[:, m, :], xbT[:, m, :], ALU.mult).then_inc(S["rec_ready"], 1)
                    return run

                attention("a", l, items_a, lambda i: i + 1, A_DIM, on0,
                          {3: variance(0), 6: variance(1), 10: variance(2), 14: variance(3),
                           19: recur(0), 21: recur(1), 23: recur(2), 25: recur(3)})
                for m in range(4):
                    dve.wait_ge(S["rec_hi"], m + 1)
                    dve.tensor_tensor(al[:, 4 + m, :], gbT[:, m, :], ah[:, 4 + m, :].bitcast(F32),
                                      ALU.subtract).then_inc(S["rec_lo"], 1)
                for m in range(TM):
                    tile_lo(("oT", l, m), ah, al, m, 4)
                split(("out", l), 0)
                split(("out", l), 1)
                residual(("out", l, 0), 512, False)
                residual(("out", l, 1), 512, True)

            def gmlp(l):
                for c in range(5):
                    if c < 4:
                        split(("cin", l), c)
                    else:
                        split_next()
                    if c:
                        if c == 1:
                            dve.wait_ge(S["vbias_loaded"], 16)
                        b = round_done(dve, ("cin", l, c - 1))
                        for m in range(TM):
                            n = (c - 1) * TM + m
                            after(dve, S["v_out"], n - 1)
                            ins = dve.tensor_tensor(gt[:, n % 2, :], ps[:, b + m, :], vbias[:, (c - 1) * 512:c * 512], ALU.add)
                            ins.then_inc(S["v_pre"], 1)
                        dve.wait_ge(S["v_pre"], c * TM)
                        dve.engine_nop().then_inc(took(("cin", l, c - 1)), 1)
                split(("cin", l), 4)
                dve.wait_ge(S["v_out"], 16)
                link(dve.tensor_reduce(rinv[:, 0:TM], ss[:, 0:16].rearrange("p (m c) -> p m c", c=4), AX.X, ALU.add))
                link(dve.tensor_copy(ss[:, 0:TM], rinv[:, 0:TM]))
                inverse_rms(TM, C_W)
                link(dve.tensor_copy(rx[:, :], rstd[:, 0:TM]))
                for c in range(5, 8):
                    split(("cin", l), c)
                    dve.tensor_scalar(v1[:, c - 5, :], v1[:, c - 5, :], rx[:, c - 5:c - 4], None, ALU.mult)\
                       .then_inc(S["v_scaled"], 1)
                split_next()
                dve.tensor_scalar(v1[:, 3, :], v1[:, 3, :], rx[:, 3:4], None, ALU.mult).then_inc(S["v_scaled"], 1)
                dve.wait_ge(S["bs_loaded"], 16)
                wait_taken(dve, ("cin", l, 7))

                def split_gated(kt):
                    dve.wait_ge(S["gt_hi"], kt + 1)
                    dve.tensor_tensor(gl[:, kt, :], gt[:, kt % 2, :], gh[:, kt, :].bitcast(F32),
                                      ALU.subtract).then_inc(S["gt_lo"], 1)

                for kt in range(16):
                    name = ("mix", l, kt // 4)
                    b = round_done(dve, name)
                    if kt >= 2:
                        split_gated(kt - 2)
                        dve.wait_ge(S["gt_lo"], kt - 1)
                    ins = dve.scalar_tensor_tensor(
                        out=gt[:, kt % 2, :].rearrange("p (n t) -> p n t", t=P),
                        in0=ps[:, b + kt % 4, :].rearrange("p (n t) -> p n t", t=P), scalar=vg[:, kt:kt + 1],
                        in1=bs[:, kt // 2, :].unsqueeze(1).to_broadcast([P, TM, P]), op0=ALU.mult, op1=ALU.add)
                    link(ins)
                    if kt % 4 == 3:
                        dve.engine_nop().then_inc(took(name), 1)
                    dve.tensor_tensor(gt[:, kt % 2, :], gt[:, kt % 2, :], uT[:, kt, :], ALU.mult).then_inc(S["gt_ready"], 1)
                split_gated(14)
                split_gated(15)
                for c in range(4):
                    split(("cout", l), c)
                    if c:
                        residual(("cout", l, c - 1), 256, False)
                residual(("cout", l, 3), 256, True)

            def cross(l):
                norm("nmem", l, mem, MM, mh, ml)
                for c in range(4):
                    split(("kv", l), c)
                    if c in (1, 2):
                        heads(("kv", l, c - 1), MM, 2, X_DIM, lambda m: xkn[:, m, 512 * (c - 1):512 * c])
                split_next()
                for r in range(2):
                    b = round_done(dve, ("xkT", l, r))
                    for j in range(4):
                        ins = dve.tensor_scalar(xkT[:, 4 * r + j, :], ps[:, b + j, 0:MEM], xkg[:, l, j % 2:j % 2 + 1],
                                                None, ALU.mult)
                    ins.then_inc(took(("xkT", l, r)), 1)
                norm("ncross", l, x, TM, ah, al)
                split(("xq", l), 0)
                split(("xq", l), 1)
                heads(("xq", l, 0), TM, 2, X_DIM, lambda m: xqn[:, m, 0:512])
                split_next()
                heads(("xq", l, 1), TM, 2, X_DIM, lambda m: xqn[:, m, 512:1024])
                attention("x", l, items_x, lambda i: MM, X_DIM, xon, {})
                for m in range(TM):
                    tile_lo(("xoT", l, m), ah, al, m, KD)
                split(("xo", l), 0)
                split(("xo", l), 1)
                residual(("xo", l, 0), 512, False)
                residual(("xo", l, 1), 512, True)

            def route(l):
                b = round_done(dve, ("route", l, 0))
                lv = ps[:, b, 0:TM * 64].rearrange("p (m n) -> p m n", n=64)[:, :, 0:36]
                dve.tensor_tensor(lg[:, :, :], lv, rbias[:, l, :].unsqueeze(1).to_broadcast([P, TM, 36]),
                                  ALU.add).then_inc(took(("route", l, 0)), 1)
                wait_taken(dve, ("route", l, 0))
                link(dve.memset(gpad[:, :, :], -3.0e38))
                link(dve.tensor_copy(gpad[:, :, 0:GROUPS], lg[:, :, 0:GROUPS]))
                for m in range(TM):
                    link(dve.max(gm8[:, m, :], gpad[:, m, :]))
                    link(dve.max_index(gi8[:, m, :], gm8[:, m, :], gpad[:, m, :]))
                link(dve.tensor_copy(gif[:, :, :], gi8[:, :, 0:1]))
                dve.tensor_tensor(ge[:, :, :], lg[:, :, 0:GROUPS], gm8[:, :, 0:1].to_broadcast([P, TM, GROUPS]),
                                  ALU.subtract).then_inc(S["g_sub"], 1)
                link(dve.tensor_tensor(oh4[:, :, :], iota[:, 0:GROUPS].unsqueeze(1).to_broadcast([P, TM, GROUPS]),
                                       gif[:, :, :].to_broadcast([P, TM, GROUPS]), ALU.is_equal))
                link(dve.tensor_tensor(etmp[:, :, :, :],
                                       lg[:, :, GROUPS:36].rearrange("p m (g j) -> p m j g", g=GROUPS),
                                       oh4[:, :, :].unsqueeze(2).to_broadcast([P, TM, PER_GROUP, GROUPS]), ALU.mult))
                link(dve.tensor_reduce(esel[:, :, :], etmp[:, :, :, :], AX.X, ALU.add))
                for m in range(TM):
                    link(dve.max(em8[:, m, :], esel[:, m, :]))
                    link(dve.max_index(ei8[:, m, :], em8[:, m, :], esel[:, m, :]))
                dve.tensor_tensor(ed[:, :, :], em8[:, :, 1:2], em8[:, :, 0:1], ALU.subtract).then_inc(S["e_sub"], 1)
                link(dve.tensor_copy(eid[:, :, :], ei8[:, :, 0:2]))
                link(dve.scalar_tensor_tensor(out=eid[:, :, :], in0=gif[:, :, :].to_broadcast([P, TM, 2]),
                                              scalar=float(PER_GROUP), in1=eid[:, :, :], op0=ALU.mult, op1=ALU.add))
                ids = iota[:, 0:EXPERTS].unsqueeze(1).to_broadcast([P, TM, EXPERTS])
                link(dve.tensor_tensor(sel0[:, :, :], ids, eid[:, :, 0:1].to_broadcast([P, TM, EXPERTS]), ALU.is_equal))
                link(dve.tensor_tensor(sel1[:, :, :], ids, eid[:, :, 1:2].to_broadcast([P, TM, EXPERTS]), ALU.is_equal))
                dve.tensor_tensor(cnt[:, :, :], sel0[:, :, :], sel1[:, :, :], ALU.add).then_inc(S["cnt_ready"], 1)
                dve.wait_ge(S["g_exp"], l + 1)
                link(dve.tensor_reduce(gw[:, :, 0], gee[:, :, :], AX.X, ALU.add))
                link(dve.reciprocal(gw[:, :, :], gw[:, :, :]))
                dve.wait_ge(S["e_exp"], l + 1)
                link(dve.tensor_scalar(w01[:, :, 0:1], ex[:, :, :], 1.0, None, ALU.add))
                link(dve.reciprocal(w01[:, :, 0:1], w01[:, :, 0:1]))
                link(dve.tensor_tensor(w01[:, :, 0:1], w01[:, :, 0:1], gw[:, :, :], ALU.mult))
                link(dve.tensor_tensor(w01[:, :, 1:2], w01[:, :, 0:1], ex[:, :, :], ALU.mult))
                full = [P, TM, EXPERTS]
                link(dve.tensor_tensor(rt1[:, :, :], sel0[:, :, :], w01[:, :, 0:1].to_broadcast(full), ALU.mult))
                link(dve.tensor_tensor(rt2[:, :, :], sel1[:, :, :], w01[:, :, 1:2].to_broadcast(full), ALU.mult))
                tb = lambda j: tab[:, :, :, j].rearrange("p e m -> p m e")
                link(dve.tensor_tensor(tb(1), rt1[:, :, :], rt2[:, :, :], ALU.add))
                tk = tok2[:, :].unsqueeze(2).to_broadcast(full)
                link(dve.scalar_tensor_tensor(out=rt1[:, :, :], in0=tk, scalar=-NOWHERE, in1=sel0[:, :, :],
                                              op0=ALU.add, op1=ALU.mult))
                link(dve.scalar_tensor_tensor(out=rt2[:, :, :], in0=tk, scalar=2.0 * T - NOWHERE, in1=sel1[:, :, :],
                                              op0=ALU.add, op1=ALU.mult))
                link(dve.tensor_tensor(tb(2), rt1[:, :, :], rt2[:, :, :], ALU.add))
                b = round_done(dve, ("rank", l, 0))
                link(dve.scalar_tensor_tensor(out=rt1[:, :, :], in0=ps[:, b, 0:TM * EXPERTS].rearrange("p (m e) -> p m e", e=EXPERTS),
                                              scalar=1.0, in1=cnt[:, :, :], op0=ALU.add, op1=ALU.mult))
                link(dve.tensor_scalar(tb(0), rt1[:, :, :], -1.0, None, ALU.add))
                link(dve.tensor_reduce(most[:, :], ps[:, b, TM * EXPERTS:(TM + 1) * EXPERTS], AX.X, ALU.max))
                link(dve.tensor_copy(mosti[:, :], most[:, :]))
                link(dve.tensor_copy(iotac[:, :], iota[:, :]))
                link(dve.memset(hh[:, :], 0.0))
                dve.engine_nop().then_inc(took(("rank", l, 0)), 1)
                dve.engine_nop().then_inc(over_step[l], 1)
                dve.engine_nop().then_inc(S["tab_ready"], 1)

            def columns(src, p, e, stage):
                stage(dve.tensor_copy(te[:, p, :, :], tab[:, bass.ds(e, 1), :, :].rearrange("p a m c -> p (a m) c")))
                stage(dve.tensor_tensor(oh[:, p, :, :], src[:, :].unsqueeze(1).to_broadcast([P, TM, SLOTS]),
                                        te[:, p, :, 0:1].to_broadcast([P, TM, SLOTS]), ALU.is_equal))
                return dve.tensor_tensor(ohr[:, p, :, :], oh[:, p, :, :],
                                         rx[:, :].unsqueeze(2).to_broadcast([P, TM, SLOTS]), ALU.mult)

            def tokens_out(l, p):
                return dve.tensor_tensor(xg[:, p, :, :], ps[:, 0, :].rearrange("p (k n) -> p k n", n=SLOTS),
                                         gcol[:, l, :].unsqueeze(2).to_broadcast([P, KD, SLOTS]), ALU.mult)

            def hidden(p):
                return dve.tensor_tensor(hh[0:SLOTS, :], ps[SLOTS:P, 2 + p, :], sg[SLOTS:P, :], ALU.mult)

            def experts(l):
                e0 = EXPERTS * l
                two = 2 * e0

                def prepare(e, p):
                    after(dve, S["x_gathered"], e + (e0 - 1))
                    n = [0]

                    def stage(ins):
                        n[0] += 1
                        ins.then_inc(dve_loop, 1)
                        dve.wait_ge(dve_loop, e * 2 + (two + n[0]))
                    columns(iota, p, e, stage).then_inc(S["oh_ready"], 1)

                def take(e, p, stored):
                    dve.wait_ge(S["x_gathered"], e + (e0 + 1))
                    after(dve, S["gu_done"], e + (e0 - 1))
                    tokens_out(l, p).then_inc(S["xg_ready"], 1)
                    after(dve, S["yw_ready"], e + (e0 - 1))
                    after(dve, y_stored[l][p], stored)
                    dve.tensor_copy(wcol[:, p, :], ps[:, 1, 0:1])
                    dve.tensor_scalar(idx[:, p, :], ps[:, 1, 1:2], big2[:, :], None, ALU.add).then_inc(S["info_ready"], 1)

                def hide(e, p):
                    dve.wait_ge(S["silu_done"], e + (e0 + 1))
                    after(dve, S["hT_done"], e + e0)
                    hidden(p).then_inc(S["h_ready"], 1)

                prepare(0, 0)
                take(0, 0, 0)
                prepare(1, 1)
                hide(0, 0)
                take(1, 1, 0)
                with dve.Fori(1, EXPERTS // 2) as i:
                    prepare(i * 2, 0)
                    hide(i * 2 - 1, 1)
                    take(i * 2, 0, i * 16)
                    prepare(i * 2 + 1, 1)
                    hide(i * 2, 0)
                    take(i * 2 + 1, 1, i * 16)
                hide(EXPERTS - 1, 1)
                n = dve.value_load(mosti[0:1, 0:1], min_val=0, max_val=T)
                with dve.Fori(1, PASSES) as c:
                    with dve.If(n > c * SLOTS):
                        dve.wait_ge(S["yw_ready"], e0 + EXPERTS)
                        for p in range(2):
                            dve.wait_ge(y_stored[l][p], 16 * (EXPERTS // 2))
                        dve.tensor_scalar(iotac[:, :], iotac[:, :], float(SLOTS), None, ALU.add)
                        dve.drain()
                        with dve.Fori(0, EXPERTS) as e:
                            at_ = lambda k: c * (15 * EXPERTS) + e * 15 + (1 - 15 * EXPERTS + k)
                            dve.wait_ge(over_step[l], at_(0))
                            n_ = [0]

                            def stage(ins):
                                n_[0] += 1
                                ins.then_inc(over_step[l], 1)
                                dve.wait_ge(over_step[l], at_(n_[0]))
                            columns(iotac, 0, e, stage).then_inc(over_step[l], 1)
                            dve.wait_ge(over_step[l], at_(4))
                            tokens_out(l, 0).then_inc(over_step[l], 1)
                            dve.tensor_copy(wcol[:, 0, :], ps[:, 1, 0:1]).then_inc(over_step[l], 1)
                            dve.tensor_scalar(idx[:, 0, :], ps[:, 1, 1:2], big2[:, :], None, ALU.add)\
                               .then_inc(over_step[l], 1)
                            dve.wait_ge(over_step[l], at_(9))
                            hidden(0).then_inc(over_step[l], 1)
                        dve.wait_ge(over_step[l], c * (15 * EXPERTS) + 1)
                        settle(dve)
                    dve.nop()
                for m in range(TM):
                    dve.wait_ge(y_in[m % 2], 16 * (2 * l + m // 2 + 1))
                    link(dve.tensor_tensor(x[:, m, :], x[:, m, :], yin[:, m % 2, 0, :], ALU.add))
                    dve.tensor_tensor(x[:, m, :], x[:, m, :], yin[:, m % 2, 1, :], ALU.add).then_inc(S["y_added"], 1)
                dve.wait_ge(S["y_added"], TM * (l + 1))
                dve.engine_nop().then_inc(res_added, 1)

            dve.wait_ge(S["small_hi"], 1)
            dve.tensor_tensor(wls[:, :, 0:A_HEADS], wsmall[:, :, 0:A_HEADS], whs[:, :, 0:A_HEADS].bitcast(F32),
                              ALU.subtract).then_inc(S["small_lo"], 1)
            dve.wait_ge(params, 32)
            link(dve.tensor_scalar(qg[:, :], qg[:, :], float(A_DIM) ** -0.5, None, ALU.mult))
            link(dve.tensor_scalar(xqg[:, :, :], xqg[:, :, :], float(X_DIM) ** -0.5, None, ALU.mult))
            for l in range(LAYERS):
                norm("nmix", l, x, TM, ah, al)
                fox(l) if l % 2 == 0 else gmlp(l)
                cross(l)
                dve.wait_ge(S["small_hi"], l + 2)
                dve.tensor_tensor(wls[:, :, :], wsmall[:, :, :], whs[:, :, :].bitcast(F32),
                                  ALU.subtract).then_inc(S["small_lo"], 1)
                norm("nffn", l, x, TM, ah, al)
                route(l)
                experts(l)

        @block.gpsimd
        def _(pool):
            links = [0]

            def link(ins):
                links[0] += 1
                ins.then_inc(pchain, 1)
                pool.wait_ge(pchain, links[0])

            def load_gain(n):
                kind, l = NORMS[n]
                pool.dma_start(gain[:, n % 2, :], row_bcast(A["norm_" + kind][l], D)).then_inc(gain_loaded[n % 2], 16)

            load_gain(0)
            pool.dma_start(wsmall[:, :, 0:A_HEADS], kcols(A["ab_w_in"][0], 3 * A_W, A_HEADS)).then_inc(S["small_loaded0"], 16)
            link(pool.memset(halfp[:, :], -0.5))
            link(pool.memset(onecol[:, :], 1.0))
            link(pool.memset(ones[:, :], 1.0))
            link(pool.memset(qT[A_DIM:A_DIM + 1, :, :], 1.0))
            link(pool.memset(causal[:, :], 0.0))
            link(pool.memset(ident[:, :], 0.0))
            link(pool.affine_select(out=ident[:, :], in_=ident[:, :], compare_op=ALU.not_equal, fill=1.0, base=0,
                               pattern=[[-1, P]], channel_multiplier=1))
            link(pool.affine_select(out=causal[:, :], in_=causal[:, :], compare_op=ALU.is_ge, fill=-BIG, base=0,
                               pattern=[[-1, P]], channel_multiplier=1))
            link(pool.affine_select(out=before[:, :], in_=ones[:, :], compare_op=ALU.is_ge, fill=0.0, base=-1,
                               pattern=[[1, P]], channel_multiplier=-1))
            link(pool.iota(iota[:, :], pattern=[[1, SLOTS]], base=0, channel_multiplier=0, allow_small_or_imprecise_dtypes=True))
            link(pool.iota(tok2[:, :], pattern=[[2 * P, TM]], base=0, channel_multiplier=2, allow_small_or_imprecise_dtypes=True))
            link(pool.memset(big2[0:SLOTS, :], NOWHERE))
            link(pool.memset(big2[SLOTS:P, :], NOWHERE + 1))
            pool.engine_nop().then_inc(consts_ready, 1)
            pool.dma_start(small[:, 0:PACKED], A["packed"]).then_inc(params, 16)
            pool.dma_start(wblk[:, :, :, :].rearrange("p a m n -> p (a m n)"), A["blocks"]).then_inc(params, 16)

            powers = [0]

            def power(n):
                powers[0] += 1
                pool.wait_ge(var_ready, powers[0])
                pool.tensor_tensor(rstd[:, 0:n], ss[:, 0:n], halfp[:, 0:n], ALU.pow).then_inc(rstd_ready, 1)

            def next_gain(n):
                if n < len(NORMS):
                    after(pool, norms_done, n - 1)
                    if NORMS[n] == ("cross", 0):
                        pool.wait_ge(S["rec_ready"], 4)
                    if NORMS[n] == ("mem", 0):
                        pool.wait_ge(S["rec_ready"], 4)
                    load_gain(n)

            n = 0
            for l in range(LAYERS):
                power(TM)
                n += 1
                if l % 2 == 0:
                    power(TM * A_HEADS)
                    power(TM * A_HEADS)
                    next_gain(n)
                    round_done(pool, ("oT", l, TM - 1))
                else:
                    wait_taken(pool, ("nmix", l, TM - 1))
                    pool.wait_ge(nat_ready, 18)
                    pool.dma_start(vbias[:, :], row_bcast(A["c_b_in"][0, C_W:2 * C_W], C_W)).then_inc(S["vbias_loaded"], 16)
                    pool.dma_start(wsn[:, :, :], A["c_w_s"][0].rearrange("g t s -> t g s")).then_inc(S["ws_loaded"], 16)
                    pool.dma_start(bs[:, :, :], A["c_b_s"][0].rearrange("(a g) t -> a g t", a=1)
                                   .to_broadcast([P, C_GROUPS, P])).then_inc(S["bs_loaded"], 16)
                    pool.wait_ge(S["ws_loaded"], 16)
                    pool.affine_select(out=wsn[:, :, :], in_=wsn[:, :, :], compare_op=ALU.is_ge, fill=0.0, base=0,
                                       pattern=[[0, C_GROUPS], [-1, P]], channel_multiplier=1).then_inc(S["ws_masked"], 1)
                    next_gain(n)
                    power(TM)
                    round_done(pool, ("mix", l, 3))
                pool.dma_start(mem[:, :, :], mem_in).then_inc(S["mem_loaded"], 16)
                power(MM)
                n += 1
                next_gain(n)
                power(2 * MM)
                power(2 * MM)
                power(TM)
                n += 1
                next_gain(n)
                power(2 * TM)
                power(2 * TM)
                round_done(pool, ("xoT", l, TM - 1))
                pool.dma_start(wsmall[:, :, 0:GROUPS], A["moe_wg"][l].rearrange("(k p) n -> p k n", p=P))\
                    .then_inc(S[f"small_loaded{l + 1}"], 16)
                pool.dma_start(wsmall[:, :, GROUPS:36], A["moe_we"][l].rearrange("(k p) n -> p k n", p=P))\
                    .then_inc(S[f"small_loaded{l + 1}"], 16)
                power(TM)
                n += 1
                next_gain(n)

                e0 = EXPERTS * l

                def scatter(p):
                    return pool.indirect_dma_start(
                        out=ydram[l], out_offset=bass.IndirectOffsetOnAxis(ap=idx[:, p, :], axis=0),
                        in_=yw[:, p, :], in_offset=None, bounds_check=4 * T - 1, oob_is_err=False)

                with pool.Fori(0, EXPERTS // 2) as i:
                    for p in range(2):
                        pool.wait_ge(S["yw_ready"], i * 2 + (e0 + p + 1))
                        settle(pool)
                        scatter(p).then_inc(y_stored[l][p], 16)
                nn = pool.value_load(mosti[0:1, 0:1], min_val=0, max_val=T)
                with pool.Fori(1, PASSES) as c:
                    with pool.If(nn > c * SLOTS):
                        with pool.Fori(0, EXPERTS) as e:
                            pool.wait_ge(over_step[l], c * (15 * EXPERTS) + e * 15 + (15 - 15 * EXPERTS))
                            settle(pool)
                            scatter(0).then_inc(over_stored[l], 16)
                            pool.wait_ge(over_stored[l], c * (16 * EXPERTS) + e * 16 + (16 - 16 * EXPERTS))
                            pool.sem_inc(over_step[l], 1)
                        pool.wait_ge(over_step[l], c * (15 * EXPERTS) + 1)
                        settle(pool)
                    pool.nop()


_BIG = ["x", "mem", "norm_mix", "norm_cross", "norm_mem", "norm_ffn", "ab_w_in", "ab_w_out", "c_w_in", "c_b_in",
        "c_w_s", "c_b_s", "c_w_out", "x_wq", "x_wkv", "x_wo", "moe_wg", "moe_we", "moe_w_gate", "moe_w_up", "moe_w_down"]


def layout(inputs):
    import numpy as np
    a = {n: np.asarray(inputs[n]) for n in inputs}
    arrays = {n: np.ascontiguousarray(a[n]) for n in _BIG}
    packed = np.zeros((P, PACKED), np.float32)

    def put(name, value):
        lo, n, parts, _ = PACK[name]
        packed[0:parts, lo:lo + n] = value

    cols = lambda v: v.reshape(-1, P).T
    put("fbias", a["ab_f_bias"][0])
    put("qg", a["ab_q_gain"][0][:, None])
    put("kg", a["ab_k_gain"][0][:, None])
    put("convw", a["ab_conv_w"][0].reshape(CONV, 4, P).transpose(2, 1, 0).reshape(P, 4 * CONV))
    for name, key in (("convb", "ab_conv_b"), ("bab", "ab_ba"), ("bxb", "ab_bx"), ("lam", "ab_lambda"),
                      ("vg", "c_v_gain")):
        put(name, cols(a[key][0]))
    put("ub", cols(a["c_b_in"][0, 0:C_W]))
    for name, key in (("xqg", "x_q_gain"), ("xkg", "x_k_gain"), ("gcol", "norm_ffn")):
        put(name, np.concatenate([cols(a[key][l]) for l in range(LAYERS)], axis=1))
    put("rbias", np.concatenate([a["moe_bg"], a["moe_be"]], axis=1).reshape(1, -1))
    arrays["packed"] = packed
    blocks = np.zeros((P, 2, 4, P), np.float32)
    for j, key in enumerate(("ab_wa", "ab_wx")):
        for g in range(8):
            q = 64 * (g % 2)
            blocks[q:q + 64, j, g // 2, q:q + 64] = a[key][0, g]
    arrays["blocks"] = blocks.reshape(P, 8 * P)
    return arrays


def kernel(**inputs):
    import concourse.bacc as _bacc
    from concourse.bass_utils import run_bass_kernel_spmd as _run

    nc = _bacc.Bacc("TRN2", target_bir_lowering=False, num_devices=1)
    arrays = layout(inputs)
    aps = {n: nc.dram_tensor(f"in_{n}", v.shape, F32, kind="ExternalInput").ap() for n, v in arrays.items()}
    out = nc.dram_tensor("out_x", (1, T, D), F32, kind="ExternalOutput").ap()
    program(nc, aps, out)
    r = _run(nc, [{f"in_{n}": v for n, v in arrays.items()}], core_ids=[0])
    return r.results[0]["out_x"]
```

```python
from contextlib import ExitStack

import concourse.bass as bass
from concourse import mybir

F32 = mybir.dt.float32
F32R = mybir.dt.float32r
U32 = mybir.dt.uint32
I32 = mybir.dt.int32
ACT = mybir.ActivationFunctionType
ALU = mybir.AluOpType
AX = mybir.AxisListType

P = 128
D = 1024
KD = D // P
T = 512
TM = T // P
MEM = 256
MM = MEM // P
LAYERS = 2
EPS = 1e-6
A_HEADS, A_DIM = 8, 64
X_HEADS, X_DIM = 4, 256
A_W = A_HEADS * A_DIM
B_W = 512
CONV = 4
RG_C = 8.0
C_W = 2048
C_GROUPS, C_DIM = 8, 256
GROUPS, PER_GROUP = 4, 8
EXPERTS = GROUPS * PER_GROUP
FE = 512
KF = FE // P
SLOTS = 64
PASSES = T // SLOTS
NOWHERE = 4096.0
BIG = 1e30
PAIRS = EXPERTS // 2
OVER = 25

RING = 6
UNIT = 2048
STAGE = 3
THIN = (KD - 1) * (GROUPS + EXPERTS) + P
STEPS = 4


def dense_plan():
    plan, unit = {}, 0
    for layer in range(LAYERS):
        dense = ([("in", 10), ("out", 4)] if layer % 2 == 0 else [("cin", 16), ("cout", 8)])
        for name, units in dense + [("kv", 6), ("xq", 4), ("kv3", 2), ("xo", 4)]:
            plan[name, layer] = (unit, units)
            unit += units
        plan["moe", layer] = (unit, EXPERTS * 6)
        unit += EXPERTS * 6
    return plan


PLAN = dense_plan()
STEP0 = {}
_steps = 0
for _key, (_u, _n) in PLAN.items():
    if _key[0] != "moe":
        STEP0[_key] = _steps
        _steps += STEPS * _n


def first_step(name, layer, c):
    return STEP0["kv3", layer] if (name, c) == ("kv", 3) else STEP0[name, layer] + 8 * c


def round_plan():
    names = []
    for l in range(LAYERS):
        names += [] if l % 2 == 0 else [("wsT", l, 0)]
        names += [("nmix", l, m) for m in range(TM)]
        if l % 2 == 0:
            names += [("in", l, c) for c in range(3)] + [("f", l, 0)] + [("in", l, c) for c in (3, 4)]
            names += [("qT", l, 0), ("qT", l, 1), ("kT", l, 0), ("kT", l, 1)]
            names += [("rg", l, 0), ("rg", l, 1)]
            names += [("oT", l, m) for m in range(TM)] + [("nmem", l, m) for m in range(MM)]
            names += [("out", l, c) for c in range(2)]
        else:
            names += [("cin", l, c) for c in range(4)] + [("cin", l, c) for c in range(4, 8)]
            names += [("mix", l, c) for c in range(4)] + [("cout", l, 0)]
            names += [("nmem", l, m) for m in range(MM)] + [("cout", l, c) for c in range(1, 4)]
        names += [("kv", l, c) for c in range(3)]
        names += [("ncross", l, m) for m in range(TM)] + [("xkT", l, 0), ("xkT", l, 1)]
        names += [("xq", l, c) for c in range(2)] + [("kv", l, 3)]
        names += [("xqT", l, c) for c in range(2)] + [("xoT", l, m) for m in range(TM)]
        names += [("xo", l, c) for c in range(2)]
        names += [("nffn", l, m) for m in range(TM)] + [("route", l, 0), ("logits", l, 0), ("rank", l, 0)]
    return {name: i for i, name in enumerate(names)}


ROUND = round_plan()
DENSE = ("in", "out", "cin", "cout", "kv", "xq", "xo")
PLAIN = {}
for _name in ROUND:
    if _name[0] not in DENSE:
        PLAIN[_name] = len(PLAIN)
NORMS = [(kind, l) for l in range(LAYERS) for kind in ("mix", "mem", "cross", "ffn")]


PACK = {}
PACKED = 0
for _name, _parts, _shape in (("fbias", A_HEADS, (1,)), ("qg", A_DIM, (1,)), ("kg", A_DIM, (1,)),
                              ("convw", P, (4, CONV)), ("convb", P, (4,)), ("bab", P, (4,)), ("bxb", P, (4,)),
                              ("lam", P, (4,)), ("xqg", P, (LAYERS, 2)), ("xkg", P, (LAYERS, 2)),
                              ("gcol", P, (LAYERS, KD)), ("ub", P, (16,)), ("vg", P, (16,)),
                              ("rbias", P, (LAYERS, GROUPS + EXPERTS))):
    _n = 1
    for _s in _shape:
        _n *= _s
    PACK[_name] = (PACKED, _n, _parts, _shape)
    PACKED += _n


def program(nc, A, out):
    ctx = ExitStack()
    with ctx:
        at = [-(-nc.sbuf_base // 32) * 32]
        spot = {}

        def width(shape):
            n = 4
            for s in shape[1:]:
                n *= s
            return n

        def sb(name, shape, dt=F32, over=None, skip=0):
            if over is None:
                off = at[0]
                at[0] += -(-width(shape) // 32) * 32
            else:
                off = spot[over][0] + skip
                assert skip + width(shape) <= spot[over][1], (name, over)
            spot[name] = (off, width(shape))
            return nc.alloc_sbuf_tensor_at(name, shape, dt, offset=off)

        def sem(name):
            return ctx.enter_context(nc.semaphore(name))

        x = sb("x", [P, TM, D])
        ring = sb("ring", [P, RING, UNIT])
        wh = sb("wh", [P, STAGE, 512], F32R)
        wl = sb("wl", [P, STAGE, 512], F32R)
        acts = sb("acts", [P, 8192])
        ah = sb("ah", [P, KD, T], F32R, over="acts")
        al = sb("al", [P, KD, T], F32R, over="acts", skip=16384)
        nat = sb("nat", [P, 2, D])
        gain = sb("gain", [P, 2, D])
        ident = sb("ident", [P, P])
        before = sb("before", [P, P])
        ones = sb("ones", [P, P])
        causal = sb("causal", [P, P])
        iota = sb("iota", [P, SLOTS])
        halfp = sb("halfp", [P, 32])
        onecol = sb("onecol", [P, 1])
        big2 = sb("big2", [P, 1])
        tok2 = sb("tok2", [P, TM])
        rowid = sb("rowid", [P, 1])
        ss = sb("ss", [P, 32])
        rstd = sb("rstd", [P, 32])
        mean = sb("mean", [P, TM])
        rnorm = sb("rnorm", [P, TM])
        rx = sb("rx", [P, TM])
        nmax = sb("nmax", [P, 32])
        rsum = sb("rsum", [P, 32])
        rinv = sb("rinv", [P, 32])
        work = sb("work", [P, 2048])
        extra = sb("extra", [P, 16384])
        small = sb("small", [P, PACKED])
        assert at[0] <= nc.sbuf_usable_end, (at[0], nc.sbuf_usable_end)
        junk = sb("junk", [P, D], over="work")
        prob = sb("prob", [P, 2, 512], over="work")
        probT = sb("probT", [P, 2, 512], over="work", skip=4096)
        sq = sb("sq", [P, 2, 512], over="work", skip=4096)

        def sm(name):
            lo, n, parts, shape = PACK[name]
            v = small[0:parts, lo:lo + n]
            if len(shape) == 2:
                v = v.rearrange("p (a b) -> p a b", b=shape[1])
            return v

        fbias, qg, kg = sm("fbias"), sm("qg"), sm("kg")
        convw, convb, bab, bxb, lam = sm("convw"), sm("convb"), sm("bab"), sm("bxb"), sm("lam")
        xqg, xkg, gcol, ub, vg, rbias = sm("xqg"), sm("xkg"), sm("gcol"), sm("ub"), sm("vg"), sm("rbias")
        lam2 = sb("lam2", [P, 4])
        spl = sb("spl", [P, 4])
        wsmall = sb("wsmall", [P, KD, 36], over="work", skip=4096)
        whs = sb("whs", [P, THIN], F32R)
        wls = sb("wls", [P, THIN], F32R)
        assert at[0] <= nc.sbuf_usable_end, (at[0], nc.sbuf_usable_end)

        E = 1024
        qT = sb("qT", [A_DIM + 1, A_HEADS, T], over="extra", skip=0)
        kT = sb("kT", [A_DIM + 1, A_HEADS, T], over="extra", skip=16 * E)
        v0 = sb("v0", [P, TM, A_W], over="extra", skip=32 * E)
        xbT = sb("xbT", [P, 4, T], over="extra", skip=40 * E)
        gbT = sb("gbT", [P, 4, T], over="extra", skip=48 * E)
        kn = sb("kn", [P, TM, A_W], over="extra", skip=56 * E)
        on0 = sb("on0", [P, TM, A_W], over="extra", skip=56 * E)
        qn = sb("qn", [P, TM, A_W], over="nat")
        xcT = sb("xcT", [P, 4, T], over="gain")
        iT = sb("iT", [P, 4, T], over="nat")
        aT = sb("aT", [P, 4, T], over="gain")
        wblk = sb("wblk", [P, 2, 4, P])
        tanhs = sb("tanhs", [P, 2, T], over="wblk")
        negc = sb("negc", [A_HEADS, T], over="work")
        zf = sb("zf", [A_HEADS, T], over="work", skip=2048)
        ef = sb("ef", [A_HEADS, T], over="work", skip=4096)
        assert at[0] <= nc.sbuf_usable_end, (at[0], nc.sbuf_usable_end)
        v1 = sb("v1", [P, TM, C_W], over="extra", skip=0)
        uT = sb("uT", [P, 16, T], over="extra", skip=32 * E)
        gh = sb("gh", [P, 16, T], F32R, over="acts")
        gl = sb("gl", [P, 16, T], F32R, over="extra", skip=32 * E)
        vbias = sb("vbias", [P, 2048], over="nat")
        wsT = sb("wsT", [P, C_GROUPS, P], over="wblk")
        wsn = sb("wsn", [P, C_GROUPS, P], over="nat", skip=4 * E)
        bs = sb("bs", [P, C_GROUPS, P], over="work", skip=4096)
        gt = sb("gt", [P, 2, T], over="work")
        vjunk = sb("vjunk", [P, T], over="extra", skip=36 * E)
        mem = sb("mem", [P, MM, D], over="nat")
        mem_junk = sb("mem_junk", [P, D], over="wblk")
        mh = sb("mh", [P, KD, MEM], F32R, over="extra", skip=0)
        ml = sb("ml", [P, KD, MEM], F32R, over="extra", skip=8 * E)
        xkn = sb("xkn", [P, MM, D], over="extra", skip=24 * E)
        xkT = sb("xkT", [P, KD, MEM], over="extra", skip=32 * E)
        xv = sb("xv", [P, MM, D], over="extra", skip=40 * E)
        xqT = sb("xqT", [P, KD, T], over="extra", skip=48 * E)
        xqn = sb("xqn", [P, TM, D], over="extra", skip=16 * E)
        xon = sb("xon", [P, TM, D], over="extra", skip=0)
        lg = sb("lg", [P, TM, 36], over="extra", skip=0)
        gpad = sb("gpad", [P, TM, 8], over="extra", skip=1 * E)
        gm8 = sb("gm8", [P, TM, 8], over="extra", skip=1 * E + 128)
        gi8 = sb("gi8", [P, TM, 8], U32, over="extra", skip=1 * E + 256)
        gif = sb("gif", [P, TM, 1], over="extra", skip=1 * E + 384)
        ge = sb("ge", [P, TM, 4], over="extra", skip=1 * E + 448)
        gee = sb("gee", [P, TM, 4], over="extra", skip=1 * E + 512)
        gw = sb("gw", [P, TM, 1], over="extra", skip=1 * E + 576)
        oh4 = sb("oh4", [P, TM, 4], over="extra", skip=1 * E + 640)
        esel = sb("esel", [P, TM, 8], over="extra", skip=1 * E + 704)
        em8 = sb("em8", [P, TM, 8], over="extra", skip=1 * E + 832)
        ei8 = sb("ei8", [P, TM, 8], U32, over="extra", skip=2 * E)
        w01 = sb("w01", [P, TM, 2], over="extra", skip=2 * E + 128)
        ed = sb("ed", [P, TM, 1], over="extra", skip=2 * E + 192)
        ex = sb("ex", [P, TM, 1], over="extra", skip=2 * E + 256)
        eid = sb("eid", [P, TM, 2], over="extra", skip=2 * E + 320)
        etmp = sb("etmp", [P, TM, 8, 4], over="extra", skip=3 * E)
        sel0 = sb("sel0", [P, TM, EXPERTS], over="extra", skip=4 * E)
        sel1 = sb("sel1", [P, TM, EXPERTS], over="extra", skip=5 * E)
        cnt = sb("cnt", [P, TM, EXPERTS], over="extra", skip=6 * E)
        rt1 = sb("rt1", [P, TM, EXPERTS], over="extra", skip=7 * E)
        rt2 = sb("rt2", [P, TM, EXPERTS], over="extra", skip=8 * E)
        tab = sb("tab", [P, EXPERTS, TM, 3], over="extra", skip=9 * E)
        most = sb("most", [P, 1], over="extra", skip=11 * E)
        mosti = sb("mosti", [P, 1], I32, over="extra", skip=11 * E + 64)
        te = sb("te", [P, 2, TM, 3], over="extra", skip=11 * E + 128)
        oh = sb("oh", [P, TM, 2 * SLOTS], F32R, over="extra", skip=12 * E)
        xg = sb("xg", [P, KD, 2 * SLOTS], over="extra", skip=14 * E)
        sg = sb("sg", [P, FE], over="extra", skip=18 * E)
        hh = sb("hh", [P, FE], over="extra", skip=20 * E)
        hT = sb("hT", [P, KF, SLOTS], over="extra", skip=22 * E)
        yw = sb("yw", [P, 2, 512], over="extra", skip=23 * E)
        wcol = sb("wcol", [P, 2, 1], over="extra", skip=27 * E)
        idx = sb("idx", [P, 2, 1], U32, over="extra", skip=27 * E + 64)
        iotac = sb("iotac", [P, SLOTS], over="extra", skip=27 * E + 128)
        lgT = sb("lgT", [GROUPS + EXPERTS, T], over="extra", skip=28 * E)
        rows = sb("rows", [P, D], over="extra", skip=28 * E)
        xn = sb("xn", [P, TM, D], over="extra", skip=32 * E)
        xnl = sb("xnl", [P, TM, D], F32R, over="extra", skip=32 * E)
        xnh = sb("xnh", [P, TM, D], F32R, over="extra", skip=48 * E)
        yin = sb("yin", [P, TM, 2, D], over="extra", skip=32 * E)

        ps = ctx.enter_context(nc.psum_tensor("ps", [P, 8, 512], F32))
        ydram = [nc.dram_tensor(f"y_scratch{l}", [4 * T, 512], F32).ap() for l in range(LAYERS)]

        ring_full = [sem(f"ring_full{i}") for i in range(RING)]
        wh_ready, wl_ready, w_used = sem("wh_ready"), sem("wl_ready"), sem("w_used")
        acc_done = sem("acc_done")
        taken = [sem("taken0"), sem("taken1")]
        expert_used = sem("expert_used")
        consts_ready = sem("consts_ready")
        params = sem("params_loaded")
        x_loaded = [sem(f"x_loaded{m}") for m in range(TM)]
        gain_loaded = [sem("gain_loaded0"), sem("gain_loaded1")]
        squares = sem("squares")
        norm_rstd = sem("norm_rstd")
        var_ready, rstd_ready = sem("var_ready"), sem("rstd_ready")
        nat_ready = sem("nat_ready")
        hi_ready = sem("hi_ready")
        sq_ready, sq_used = sem("sq_ready"), sem("sq_used")
        heads_ready = sem("heads_ready")
        res_added = sem("res_added")
        out_stored = sem("out_stored")
        S = {n: sem(n) for n in (
            "small_loaded0 small_loaded1 small_loaded2 small_hi small_lo "
            "f_z f_e f_ln negc_ready c_row v_ready xb_ready sp_e sp_ln xc_ready rg_sig rg_l rg_exp rg_var "
            "rg_sqrt rec_ready rec_hi rec_lo gate_ready "
            "s_done mx_done p_done pt_done pt_copied o_done o_copied "
            "mem_loaded v_pre v_out vbias_loaded bs_loaded v_scaled ws_loaded ws_masked gt_ready gt_hi gt_lo "
            "g_sub g_exp e_sub e_exp cnt_ready tab_ready "
            "xn_hi xn_lo oh_ready x_gathered rows_ready rows_T xg_ready info_ready gu_done silu_done h_ready hT_done hT_ready y_done yw_ready"
        ).split()}
        y_stored = [[sem(f"y_stored{l}_{p}") for p in range(2)] for l in range(LAYERS)]
        y_in = [sem(f"y_in{m}") for m in range(TM)]
        over_full = [sem(f"over_full{l}") for l in range(LAYERS)]
        over_step = [sem(f"over_step{l}") for l in range(LAYERS)]
        over_stored = [sem(f"over_stored{l}") for l in range(LAYERS)]
        chain, achain, pchain = sem("dve_chain"), sem("act_chain"), sem("pool_chain")
        dve_loop = sem("dve_loop_chain")
        settled = sem("settled")

        block = ctx.enter_context(nc.Block())

        x_in = A["x"].rearrange("b (m p) d -> p (b m) d", p=P)
        x_out = out.rearrange("b (m p) d -> p (b m) d", p=P)
        mem_in = A["mem"].rearrange("b (m p) d -> p (b m) d", p=P)
        IN_COL = [0, A_W, 2 * A_W, 3 * A_W + A_HEADS, 3 * A_W + A_HEADS + B_W]

        def kcols(w, c0, n):
            return w[:, c0:c0 + n].rearrange("(k p) n -> p k n", p=P)

        def dense_unit(name, l, u):
            if name == "cout":
                c, half = divmod(u, 2)
                return kcols(A["c_w_out"][0], 256 * c, 256)[:, 8 * half:8 * half + 8], 256
            c = u // 2
            w, col = {"in": (A["ab_w_in"][0], IN_COL[c % 5]),
                      "out": (A["ab_w_out"][0], 512 * c),
                      "cin": (A["c_w_in"][0], 512 * ((c + 4) % 8)),
                      "kv": (A["x_wkv"][l], 512 * c),
                      "kv3": (A["x_wkv"][l], 512 * 3),
                      "xq": (A["x_wq"][l], 512 * c),
                      "xo": (A["x_wo"][l], 512 * c)}[name]
            return kcols(w, col, 512)[:, 4 * (u % 2):4 * (u % 2) + 4], 512

        def row_bcast(v, n):
            return v.rearrange("(a n) -> a n", a=1).to_broadcast([P, n])

        def expert_unit(l, e, j):
            w = A["moe_w_down"] if j >= 4 else A[("moe_w_gate", "moe_w_up")[j % 2]]
            src = w[l][bass.ds(e, 1)].rearrange("a (k p) f -> p (a k) f", p=P)
            return (src[:, 4 * (j // 2):4 * (j // 2) + 4], 512) if j < 4 else (src[:, 2 * (j - 4):2 * (j - 4) + 2], 1024)

        def units_before(unit):
            dense = sum(min(max(unit - u, 0), n) for (name, _), (u, n) in PLAN.items() if name != "moe")
            return dense, unit - dense

        def slot(unit, cols):
            return ring[:, unit % RING, :].rearrange("p (k n) -> p k n", n=cols)

        def thin_view(w):
            return w[:, 0:KD * 36].rearrange("p (k n) -> p k n", n=36)

        def after(eng, s, n):
            if not isinstance(n, int) or n > 0:
                eng.wait_ge(s, n)

        def nats_upto(kind, l):
            done = NORMS[:NORMS.index((kind, l)) + 1]
            return sum(MM if k == "mem" else TM for k, _ in done)

        def settle(eng):
            eng.sem_inc(settled, 1)

        def round_done(eng, name):
            if name[0] in DENSE:
                eng.wait_ge(w_used, first_step(*name) + 8)
            else:
                eng.wait_ge(acc_done, PLAIN[name] + 1)
            return 4 * (ROUND[name] % 2)

        def took(name):
            return taken[ROUND[name] % 2]

        def wait_taken(eng, name):
            eng.wait_ge(taken[ROUND[name] % 2], ROUND[name] // 2 + 1)

        def all_taken(eng, next_name):
            r = ROUND[next_name] if next_name in ROUND else len(ROUND)
            eng.wait_ge(taken[0], (r + 1) // 2)
            eng.wait_ge(taken[1], r // 2)

        def split_hi(act, pos, upto):
            for t in range(pos, upto):
                unit, s = unit_of_step(t)
                if s == 0:
                    act.wait_ge(ring_full[unit % RING], 16 * (unit // RING + 1))
                after(act, w_used, t - STAGE + 1)
                act.activation(wh[:, t % STAGE, :], ring[:, unit % RING, 512 * s:512 * (s + 1)],
                               ACT.Copy).then_inc(wh_ready, 1)
            return max(pos, upto)

        def split_lo(dve, pos, upto):
            for t in range(pos, upto):
                unit, s = unit_of_step(t)
                dve.wait_ge(wh_ready, t + 1)
                dve.tensor_tensor(wl[:, t % STAGE, :], ring[:, unit % RING, 512 * s:512 * (s + 1)],
                                  wh[:, t % STAGE, :].bitcast(F32), ALU.subtract).then_inc(wl_ready, 1)
            return max(pos, upto)

        def unit_of_step(t):
            for key, t0 in STEP0.items():
                if t0 <= t < t0 + STEPS * PLAN[key][1]:
                    return PLAN[key][0] + (t - t0) // STEPS, (t - t0) % STEPS
            raise AssertionError(t)

        N_STEPS = _steps
        items_a = [(h, i) for h in range(A_HEADS) for i in range(TM)]
        items_x = [(h, i) for h in range(X_HEADS) for i in range(TM)]
        ATT0 = {}
        n_att = 0
        for l in range(LAYERS):
            if l % 2 == 0:
                ATT0["a", l] = n_att
                n_att += len(items_a)
            ATT0["x", l] = n_att
            n_att += len(items_x)


        @block.sync
        def _(sp):
            for m in range(TM):
                sp.dma_start(x[:, m, :], x_in[:, m, :]).then_inc(x_loaded[m], 16)

            def expert_done_with(l, e, j):
                if j in (3, 5):
                    sp.wait_ge(S["gu_done" if j == 3 else "y_done"], e + EXPERTS * l)
                else:
                    sp.wait_ge(expert_used, e * 4 + (4 * (EXPERTS * l - 1) + (1, 2, 3, 0, 4)[j]))

            def free_slot(unit):
                if unit >= RING:
                    dense, moe = units_before(unit - RING + 1)
                    if dense > units_before(unit - RING)[0]:
                        sp.wait_ge(wl_ready, STEPS * dense)
                    else:
                        expert_done_with((moe - 1) // (6 * EXPERTS), EXPERTS, (moe - 1) % 6)

            for (name, l), (u0, n) in PLAN.items():
                if name != "moe":
                    for u in range(u0, u0 + n):
                        free_slot(u)
                        src, cols = dense_unit(name, l, u - u0)
                        sp.dma_start(slot(u, cols), src).then_inc(ring_full[u % RING], 16)
                    continue
                for j in range(6):
                    free_slot(u0 + j)
                    src, cols = expert_unit(l, 0, j)
                    sp.dma_start(slot(u0 + j, cols), src).then_inc(ring_full[(u0 + j) % RING], 16)
                with sp.Fori(1, EXPERTS) as e:
                    for j in range(6):
                        expert_done_with(l, e, j)
                        src, cols = expert_unit(l, e, j)
                        sp.dma_start(slot(u0 + j, cols), src).then_inc(ring_full[(u0 + j) % RING], 16)
                sp.wait_ge(S["tab_ready"], l + 1)
                n = sp.value_load(mosti[0:1, 0:1], min_val=0, max_val=T)
                with sp.Fori(1, PASSES) as c:
                    with sp.If(n > c * SLOTS):
                        expert_done_with(l, EXPERTS, 5)
                        with sp.Fori(0, PAIRS) as e:
                            for half in range(2):
                                sp.wait_ge(over_step[l], c * (OVER * PAIRS) + e * OVER + (1 - OVER * PAIRS + 17 * half))
                                for j in range(6):
                                    src, cols = expert_unit(l, e * 2 + half, j)
                                    sp.dma_start(slot(u0 + j, cols), src).then_inc(over_full[l], 16)
                        sp.wait_ge(over_step[l], c * (OVER * PAIRS) + 1)
                        settle(sp)
                    sp.nop()
                for p in range(2):
                    sp.wait_ge(y_stored[l][p], 16 * PAIRS)
                yv = ydram[l].rearrange("(k m p h) c -> p m k (h c)", k=2, m=TM, p=P)
                for m in range(TM):
                    sp.dma_start(yin[:, m, :, :], yv[:, m]).then_inc(y_in[m], 16)
            sp.wait_ge(out_stored, 16 * TM)

        @block.tensor
        def _(pe):
            pe.wait_ge(consts_ready, 1)

            def begin(name):
                r = ROUND[name]
                after(pe, taken[r % 2], r // 2)
                return 4 * (r % 2)

            def dense(name, l, c, hi, lo, cols=512, flip=False, rows=TM, ready=None):
                b = begin((name, l, c))
                per = 512 // cols
                for s in range(8):
                    t = first_step(name, l, c) + s
                    pe.wait_ge(wl_ready, t + 1)
                    for kk in range(per):
                        k = s * per + kk
                        if ready:
                            ready(k)
                        for m in range(rows):
                            for i, (w, a) in enumerate(((wh, hi), (wl, hi), (wh, lo))):
                                flags = dict(start=(k == 0 and i == 0), stop=(k == 8 * per - 1 and i == 2))
                                if flip:
                                    mm = pe.matmul(ps[:, b + m, 0:T], w[:, t % STAGE, m * P:(m + 1) * P],
                                                   a[:, k, :], **flags)
                                else:
                                    mm = pe.matmul(ps[:, b + m, 0:cols], a[:, k, m * P:(m + 1) * P],
                                                   w[:, t % STAGE, kk * cols:(kk + 1) * cols], **flags)
                    mm.then_inc(w_used, 1)

            nats = [0]

            def norm_T(kind, l, tiles):
                for m in tiles:
                    b = begin((kind, l, m))
                    nats[0] += 1
                    pe.wait_ge(nat_ready, nats[0])
                    for k in range(KD):
                        mm = pe.transpose(ps[:, b + k // 4, (k % 4) * P:(k % 4 + 1) * P],
                                          xn[:, m, k * P:(k + 1) * P] if kind == "nffn"
                                          else nat[:, m % 2, k * P:(k + 1) * P], ident[:, :])
                    mm.then_inc(acc_done, 1)

            def split_written(kind, l, tiles):
                for m in range(tiles - 2, tiles):
                    wait_taken(pe, (kind, l, m))

            def thin(name, l, which):
                b = begin((name, l, 0))
                pe.wait_ge(S["small_lo"], which + 1)
                for k in range(KD):
                    for i, (w, a) in enumerate(((whs, ah), (wls, ah), (whs, al))):
                        mm = pe.matmul(ps[:, b, 0:T], w[:, 36 * k:36 * k + P], a[:, k, :],
                                       start=(k == 0 and i == 0), stop=(k == KD - 1 and i == 2))
                mm.then_inc(acc_done, 1)

            def attention(kind, l, items, nk_of, score, v_of, ow, next_name):
                n0 = ATT0[kind, l]
                all_taken(pe, next_name)

                def scores(n):
                    if n >= 3:
                        pe.wait_ge(S["p_done"], n0 + n - 2)
                    score(*items[n], n % 3).then_inc(S["s_done"], 1)

                def transposes(n):
                    h, i = items[n]
                    pe.wait_ge(S["p_done"], n0 + n + 1)
                    if n >= 2:
                        pe.wait_ge(S["pt_copied"], n0 + n - 1)
                    for j in range(nk_of(i)):
                        mm = pe.transpose(ps[:, 3 + n % 2, j * P:(j + 1) * P],
                                          prob[:, n % 2, j * P:(j + 1) * P], ident[:, :])
                    mm.then_inc(S["pt_done"], 1)

                def values(n):
                    h, i = items[n]
                    pe.wait_ge(S["pt_copied"], n0 + n + 1)
                    if n >= 2:
                        pe.wait_ge(S["o_copied"], n0 + n - 1)
                    for j in range(nk_of(i)):
                        mm = pe.matmul(ps[:, 5 + n % 2, 0:ow], probT[:, n % 2, j * P:(j + 1) * P],
                                       v_of(j, h), start=(j == 0), stop=(j == nk_of(i) - 1))
                    mm.then_inc(S["o_done"], 1)

                scores(0)
                scores(1)
                for n in range(len(items)):
                    if n + 2 < len(items):
                        scores(n + 2)
                    transposes(n)
                    if n:
                        values(n - 1)
                values(len(items) - 1)
                pe.wait_ge(S["o_copied"], n0 + len(items))

            def fox(l):
                for c in range(3):
                    dense("in", l, c, ah, al)
                thin("f", l, 0)
                for c in (3, 4):
                    dense("in", l, c, ah, al, flip=True)
                for name, src, n in (("qT", qn, 1), ("kT", kn, 2)):
                    pe.wait_ge(heads_ready, n)
                    for r in range(2):
                        b = begin((name, l, r))
                        for j in range(4):
                            h = 4 * r + j
                            for m in range(TM):
                                mm = pe.transpose(ps[0:A_DIM, b + j, m * P:(m + 1) * P],
                                                  src[:, m, h * A_DIM:(h + 1) * A_DIM], ident[:, :])
                        mm.then_inc(acc_done, 1)
                pe.wait_ge(S["xc_ready"], 1)
                for g in range(2):
                    b = begin(("rg", l, g))
                    for m in range(4):
                        mm = pe.matmul(ps[:, b + m, :], wblk[:, g, m, :], xcT[:, m, :], start=True, stop=True)
                    mm.then_inc(acc_done, 1)
                pe.wait_ge(S["c_row"], 16)
                wait_taken(pe, ("in", l, 2))

                def score(h, i, bank):
                    n = (i + 1) * P
                    pe.matmul(ps[:, bank, 0:n], qT[:, h, i * P:(i + 1) * P], kT[:, h, 0:n], start=True, stop=False)
                    return pe.matmul(ps[:, bank, i * P:n], ident[:, :], causal[:, :], start=False, stop=True)

                attention("a", l, items_a, lambda i: i + 1, score,
                          lambda j, h: v0[:, j, h * A_DIM:(h + 1) * A_DIM], A_DIM, ("oT", l, 0))
                for m in range(TM):
                    b = begin(("oT", l, m))
                    for k in range(4):
                        mm = pe.transpose(ps[:, b, k * P:(k + 1) * P], on0[:, m, k * P:(k + 1) * P], ident[:, :])
                    mm.then_inc(acc_done, 1)
                norm_T("nmem", l, range(MM))
                split_written("oT", l, TM)
                pe.wait_ge(S["rec_lo"], 4)
                for c in range(2):
                    dense("out", l, c, ah, al)

            def gmlp(l):
                for c in range(4):
                    dense("cin", l, c, ah, al)
                for c in range(4, 8):
                    dense("cin", l, c, ah, al, flip=True)
                pe.wait_ge(S["v_scaled"], TM)
                for r in range(4):
                    b = begin(("mix", l, r))
                    for j in range(4):
                        kt = 4 * r + j
                        for n in range(TM):
                            mm = pe.matmul(ps[:, b + j, n * P:(n + 1) * P], v1[:, n, kt * P:(kt + 1) * P],
                                           wsT[:, kt // 2, :], start=True, stop=True)
                    mm.then_inc(acc_done, 1)
                for c in range(4):
                    dense("cout", l, c, gh, gl, cols=256,
                          ready=(lambda k: pe.wait_ge(S["gt_lo"], k + 1)) if c == 0 else None)
                    if c == 0:
                        norm_T("nmem", l, range(MM))

            def cross(l):
                split_written("nmem", l, MM)
                for c in range(3):
                    dense("kv", l, c, mh, ml, rows=MM)
                norm_T("ncross", l, range(TM))
                n0 = (2 if l == 0 else 6)
                pe.wait_ge(heads_ready, n0 + 2)
                for r in range(2):
                    b = begin(("xkT", l, r))
                    for j in range(4):
                        for m in range(MM):
                            mm = pe.transpose(ps[:, b + j, m * P:(m + 1) * P],
                                              xkn[:, m, (4 * r + j) * P:(4 * r + j + 1) * P], ident[:, :])
                    mm.then_inc(acc_done, 1)
                split_written("ncross", l, TM)
                for c in range(2):
                    dense("xq", l, c, ah, al)
                dense("kv", l, 3, mh, ml, rows=MM)
                for r in range(2):
                    b = begin(("xqT", l, r))
                    pe.wait_ge(heads_ready, n0 + 3 + r)
                    for j in range(4):
                        for m in range(TM):
                            mm = pe.transpose(ps[:, b + j, m * P:(m + 1) * P],
                                              xqn[:, m, (4 * r + j) * P:(4 * r + j + 1) * P], ident[:, :])
                    mm.then_inc(acc_done, 1)

                def score(h, i, bank):
                    for kk in range(2):
                        mm = pe.matmul(ps[:, bank, 0:MEM], xqT[:, 2 * h + kk, i * P:(i + 1) * P],
                                       xkT[:, 2 * h + kk, :], start=(kk == 0), stop=(kk == 1))
                    return mm

                attention("x", l, items_x, lambda i: MM, score,
                          lambda j, h: xv[:, j, h * X_DIM:(h + 1) * X_DIM], X_DIM, ("xoT", l, 0))
                for m in range(TM):
                    b = begin(("xoT", l, m))
                    for k in range(KD):
                        mm = pe.transpose(ps[:, b + k // 4, (k % 4) * P:(k % 4 + 1) * P],
                                          xon[:, m, k * P:(k + 1) * P], ident[:, :])
                    mm.then_inc(acc_done, 1)
                split_written("xoT", l, TM)
                for c in range(2):
                    dense("xo", l, c, ah, al)

            def gather():
                for half in range(2):
                    for m in range(TM):
                        for i, a in enumerate((xnh, xnl)):
                            mm = pe.matmul(ps[:, half, :], oh[:, m, :], a[:, m, 512 * half:512 * (half + 1)],
                                           start=(m == 0 and i == 0), stop=(m == TM - 1 and i == 1))
                return mm

            def slots_T():
                for e in range(2):
                    for half in range(2):
                        for m in range(TM):
                            pe.matmul(ps[half * SLOTS:(half + 1) * SLOTS, 7, 2 * e:2 * e + 2],
                                      oh[:, m, e * SLOTS:(e + 1) * SLOTS].bitcast(F32), te[:, e, m, 1:3],
                                      start=(m == 0), stop=(m == TM - 1))
                for k in range(KD):
                    mm = pe.transpose(ps[:, k // 4, (k % 4) * P:(k % 4 + 1) * P], rows[:, k * P:(k + 1) * P], ident[:, :])
                return mm

            def gate_up(u0, p, full, used):
                for k in range(KD):
                    if k % 4 == 0:
                        full(k // 2)
                        full(k // 2 + 1)
                    for half in range(2):
                        w = slot(u0 + 2 * (k // 4) + half, 512)
                        mm = pe.matmul(ps[half * SLOTS:(half + 1) * SLOTS, 2 + p, :],
                                       xg[:, k, p * SLOTS:(p + 1) * SLOTS], w[:, k % 4, :],
                                       start=(k == 0), stop=(k == KD - 1))
                        if k % 4 == 3 and used and k < KD - 1:
                            mm.then_inc(expert_used, 1)
                        if k == KD - 1 and half == 0 and used:
                            mm.then_inc(expert_used, 1)
                return mm

            def hidden_T():
                for k in range(KF):
                    mm = pe.transpose(ps[:, 4, k * P:(k + 1) * P], hh[:, k * P:(k + 1) * P],
                                      ident[:, :])
                return mm

            def down(u0, p, full, used):
                for k in range(KF):
                    if k % 2 == 0:
                        full(4 + k // 2)
                    w = slot(u0 + 4 + k // 2, 1024)
                    for half in range(2):
                        mm = pe.matmul(ps[half * SLOTS:(half + 1) * SLOTS, 5 + p, :], hT[:, k, :],
                                       w[:, k % 2, 512 * half:512 * (half + 1)], start=(k == 0), stop=(k == KF - 1))
                    if k == 1 and used:
                        mm.then_inc(expert_used, 1)
                return mm

            def experts(l):
                u0 = PLAN["moe", l][0]
                e0 = EXPERTS * l
                all_taken(pe, ("wsT", l + 1, 0))

                q0 = PAIRS * l

                def do_gather(q):
                    pe.wait_ge(S["oh_ready"], q + (q0 + 1))
                    gather().then_inc(S["x_gathered"], 1)

                def do_slots_T(q):
                    pe.wait_ge(S["rows_ready"], q + (q0 + 1))
                    after(pe, S["info_ready"], q + q0)
                    slots_T().then_inc(S["rows_T"], 1)

                def expert(e, p, q, last=False):
                    def full(j):
                        pe.wait_ge(ring_full[(u0 + j) % RING], (e + ((u0 + j) // RING + 1)) * 16)
                    if p == 0:
                        pe.wait_ge(S["xg_ready"], q + (q0 + 1))
                    after(pe, S["h_ready"], e + (e0 - 1))
                    gate_up(u0, p, full, True).then_inc(S["gu_done"], 1)
                    if not last:
                        if p == 0:
                            do_gather(q + 1)
                        else:
                            do_slots_T(q + 1)
                    pe.wait_ge(S["h_ready"], e + (e0 + 1))
                    after(pe, S["hT_ready"], e + e0)
                    hidden_T().then_inc(S["hT_done"], 1)
                    pe.wait_ge(S["hT_ready"], e + (e0 + 1))
                    after(pe, S["yw_ready"], e + (e0 - 1))
                    down(u0, p, full, True).then_inc(S["y_done"], 1)

                pe.wait_ge(S["xn_lo"], l + 1)
                do_gather(0)
                do_slots_T(0)
                expert(0, 0, 0)
                expert(1, 1, 0)
                with pe.Fori(1, PAIRS - 1) as i:
                    for p in range(2):
                        expert(i * 2 + p, p, i)
                expert(EXPERTS - 2, 0, PAIRS - 1, last=True)
                expert(EXPERTS - 1, 1, PAIRS - 1, last=True)
                n = pe.value_load(mosti[0:1, 0:1], min_val=0, max_val=T)
                with pe.Fori(1, PASSES) as c:
                    with pe.If(n > c * SLOTS):
                        with pe.Fori(0, PAIRS) as e:
                            at_ = lambda k: c * (OVER * PAIRS) + e * OVER + (1 - OVER * PAIRS + k)
                            pe.wait_ge(over_step[l], at_(3))
                            gather().then_inc(over_step[l], 1)
                            pe.wait_ge(over_step[l], at_(5))
                            slots_T().then_inc(over_step[l], 1)
                            for p in range(2):
                                pe.wait_ge(over_step[l], at_(9 + 8 * p))
                                pe.wait_ge(over_full[l], c * (96 * EXPERTS) + e * 192 + (96 * (p + 1) - 96 * EXPERTS))
                                gate_up(u0, p, lambda j: None, False).then_inc(over_step[l], 1)
                                pe.wait_ge(over_step[l], at_(12 + 8 * p))
                                hidden_T().then_inc(over_step[l], 1)
                                pe.wait_ge(over_step[l], at_(14 + 8 * p))
                                down(u0, p, lambda j: None, False).then_inc(over_step[l], 1)
                        pe.wait_ge(over_step[l], c * (OVER * PAIRS) + 1)
                        settle(pe)
                    pe.nop()

            def position_weights(l):
                b = begin(("wsT", l, 0))
                pe.wait_ge(S["ws_masked"], 1)
                for g in range(C_GROUPS):
                    mm = pe.transpose(ps[:, b + g // 4, (g % 4) * P:(g % 4 + 1) * P], wsn[:, g, :], ident[:, :])
                mm.then_inc(acc_done, 1)

            for l in range(LAYERS):
                if l % 2:
                    position_weights(l)
                norm_T("nmix", l, range(TM))
                split_written("nmix", l, TM)
                fox(l) if l % 2 == 0 else gmlp(l)
                cross(l)
                norm_T("nffn", l, range(TM))
                split_written("nffn", l, TM)
                thin("route", l, l + 1)
                wait_taken(pe, ("route", l, 0))
                b = begin(("logits", l, 0))
                for m in range(TM):
                    mm = pe.transpose(ps[:, b, m * 64:m * 64 + 36], lgT[:, m * P:(m + 1) * P], ident[0:36, 0:36])
                mm.then_inc(acc_done, 1)
                b = begin(("rank", l, 0))
                pe.wait_ge(S["cnt_ready"], l + 1)
                flat = cnt[:, :, :].rearrange("p m e -> p (m e)")
                pe.matmul(ps[:, b, 0:TM * EXPERTS], before[:, :], flat, start=True, stop=False)
                for m in range(1, TM):
                    pe.matmul(ps[:, b, m * EXPERTS:TM * EXPERTS], ones[:, :], flat[:, 0:(TM - m) * EXPERTS],
                              start=False, stop=(m == TM - 1))
                for m in range(TM):
                    mm = pe.matmul(ps[:, b, TM * EXPERTS:(TM + 1) * EXPERTS], ones[:, :], cnt[:, m, :],
                                   start=(m == 0), stop=(m == TM - 1))
                mm.then_inc(acc_done, 1)
                experts(l)

        @block.scalar
        def _(act):
            pos = [0]
            links = [0]

            def link(ins):
                links[0] += 1
                ins.then_inc(achain, 1)
                act.wait_ge(achain, links[0])

            def split(key, c, between=None):
                first = first_step(*key, c)
                for s in sorted(between or {}):
                    pos[0] = split_hi(act, pos[0], first + s)
                    between[s]()
                pos[0] = split_hi(act, pos[0], first + 8)

            def split_next():
                pos[0] = split_hi(act, pos[0], min(pos[0] + STAGE, N_STEPS))

            nsq = [0]

            def tile_square(src, m, throwaway):
                after(act, squares, nsq[0])
                nsq[0] += 1
                act.activation(throwaway[:, :], src[:, m, :], ACT.Square, scale=float(D) ** -0.5,
                               accum_out=mean[:, m:m + 1]).then_inc(squares, 1)

            def x_square(event, m):
                act.wait_ge(res_added, TM * event + m + 1)
                tile_square(x, m, junk)

            def tile_hi(name, dst, m, kts, k0=0):
                b = round_done(act, name)
                src = ps[:, b:b + -(-kts // 4), :].rearrange("p a (k n) -> p (a k) n", n=P)
                act.activation(dst[:, k0:k0 + kts, m * P:(m + 1) * P], src, ACT.Copy).then_inc(hi_ready, 1)

            def norm(kind, l, square):
                for m in range(3):
                    square(m)
                tile_hi((kind, l, 0), ah, 0, KD)
                square(3)
                for m in range(1, TM):
                    tile_hi((kind, l, m), ah, m, KD)

            def mem_squares(l):
                act.wait_ge(S["mem_loaded"], 16 * (l + 1))
                for m in range(MM):
                    tile_square(mem, m, mem_junk if l % 2 == 0 else junk)

            sqs = [0]

            def head_squares(name, tiles, dim):
                b = round_done(act, name)
                for m in range(tiles):
                    after(act, sq_used, sqs[0] - 1)
                    act.activation(sq[:, sqs[0] % 2, :], ps[:, b + m, :], ACT.Square,
                                   scale=float(dim) ** -0.5).then_inc(sq_ready, 1)
                    sqs[0] += 1

            def copy_out(name, dst, tiles, func=ACT.Copy, bias=None):
                b = round_done(act, name)
                for m in tiles:
                    kw = {} if bias is None else dict(bias=bias(m))
                    ins = act.activation(dst(m), ps[:, b + m, :], func, **kw)
                    if m == tiles[-1] and m == (MM if name[0] == "kv" else TM) - 1:
                        ins.then_inc(took(name), 1)

            def attention(kind, l, items, nk_of, hooks):
                n0 = ATT0[kind, l]

                def exps(n):
                    h, i = items[n]
                    w = nk_of(i) * P
                    act.wait_ge(S["mx_done"], n0 + n + 1)
                    if n >= 2:
                        act.wait_ge(S["pt_done"], n0 + n - 1)
                    act.activation(prob[:, n % 2, 0:w], ps[:, n % 3, 0:w], ACT.Exp, bias=nmax[:, n:n + 1],
                                   accum_out=rsum[:, n:n + 1]).then_inc(S["p_done"], 1)

                def copies(n):
                    w = nk_of(items[n][1]) * P
                    act.wait_ge(S["pt_done"], n0 + n + 1)
                    if n >= 2:
                        act.wait_ge(S["o_done"], n0 + n - 1)
                    act.activation(probT[:, n % 2, 0:w], ps[:, 3 + n % 2, 0:w], ACT.Copy).then_inc(S["pt_copied"], 1)

                exps(0)
                for n in range(len(items)):
                    if n + 1 < len(items):
                        exps(n + 1)
                    copies(n)
                    if n in hooks:
                        hooks[n]()

            def fox(l):
                split(("in", l), 0)
                act.wait_ge(consts_ready, 2)
                act.wait_ge(S["small_loaded0"], 16)
                act.activation(thin_view(whs)[:, :, 0:A_HEADS], wsmall[:, :, 0:A_HEADS], ACT.Copy)\
                   .then_inc(S["small_hi"], 1)

                def squares0():
                    act.wait_ge(S["small_lo"], 1)
                    head_squares(("in", l, 0), TM, A_DIM)
                split(("in", l), 1, {3: squares0})
                split(("in", l), 2, {3: lambda: head_squares(("in", l, 1), TM, A_DIM)})
                split(("in", l), 3, {3: lambda: copy_out(("in", l, 2), lambda m: v0[:, m, :], range(TM))})
                act.wait_ge(S["f_z"], 2)
                act.activation(ef[:, :], ef[:, :], ACT.Exp).then_inc(S["f_e"], 1)
                act.activation(spl[:, :], spl[:, :], ACT.Exp).then_inc(S["f_e"], 1)
                act.wait_ge(S["f_e"], 2)
                act.activation(ef[:, :], ef[:, :], ACT.Ln, bias=onecol[0:A_HEADS, :]).then_inc(S["f_ln"], 1)
                act.activation(spl[:, :], spl[:, :], ACT.Ln, bias=onecol[:, :]).then_inc(S["f_ln"], 1)
                split(("in", l), 4, {3: lambda: copy_out(("in", l, 3), lambda m: xbT[:, m, :], range(4))})
                split_next()
                copy_out(("in", l, 4), lambda m: gbT[:, m, :], range(4), ACT.Gelu_apprx_tanh)
                act.wait_ge(S["negc_ready"], 1)
                act.dma_start(kT[A_DIM:A_DIM + 1, :, :], negc[:, :]).then_inc(S["c_row"], 16)
                for r in range(2):
                    b = round_done(act, ("qT", l, r))
                    for j in range(4):
                        ins = act.activation(qT[0:A_DIM, 4 * r + j, :], ps[0:A_DIM, b + j, :], ACT.Copy, scale=qg[:, :])
                    ins.then_inc(took(("qT", l, r)), 1)
                for g, (dst, bias) in enumerate(((xbT, bab), (iT, bxb))):
                    b = round_done(act, ("rg", l, g))
                    if g == 1:
                        wait_taken(act, ("qT", l, 1))
                    for m in range(4):
                        ins = act.activation(dst[:, m, :], ps[:, b + m, :], ACT.Sigmoid, bias=bias[:, m:m + 1])
                    ins.then_inc(took(("rg", l, g)), 1)

                def decay(m):
                    def run():
                        act.wait_ge(S["rg_l"], m + 1)
                        if m >= 2:
                            act.wait_ge(S["rg_var"], m - 1)
                        act.activation(aT[:, m, :], xbT[:, m, :], ACT.Exp)
                        act.activation(tanhs[:, m % 2, :], xbT[:, m, :], ACT.Tanh, scale=-1.0).then_inc(S["rg_exp"], 1)
                    return run

                def roots():
                    act.wait_ge(S["rg_var"], 4)
                    for m in range(4):
                        act.activation(xbT[:, m, :], xbT[:, m, :], ACT.Sqrt).then_inc(S["rg_sqrt"], 1)

                def rec_his():
                    for m in range(4):
                        act.wait_ge(S["rec_ready"], m + 1)
                        act.activation(ah[:, 4 + m, :], gbT[:, m, :], ACT.Copy).then_inc(S["rec_hi"], 1)

                attention("a", l, items_a, lambda i: i + 1,
                          {2: decay(0), 5: decay(1), 9: decay(2), 13: decay(3), 17: roots, 28: lambda: mem_squares(l),
                           30: rec_his})
                for m in range(TM):
                    tile_hi(("oT", l, m), ah, m, 4)
                for m in range(MM):
                    tile_hi(("nmem", l, m), mh, m, KD)
                split(("out", l), 0)
                split(("out", l), 1)

            def gmlp(l):
                def v_part(c, m):
                    def run():
                        n = c * TM + m
                        act.wait_ge(S["v_pre"], n + 1)
                        link(act.activation(v1[:, m, c * 512:(c + 1) * 512], gt[:, n % 2, :], ACT.Gelu_apprx_tanh))
                        act.activation(vjunk[:, :], v1[:, m, c * 512:(c + 1) * 512], ACT.Square,
                                       accum_out=ss[:, 4 * m + c:4 * m + c + 1]).then_inc(S["v_out"], 1)
                    return run

                def u_part(c, m):
                    return lambda: copy_out(("cin", l, c), lambda m: uT[:, 4 * (c - 4) + m, :], [m], ACT.Gelu_apprx_tanh,
                                            lambda m: ub[:, 4 * (c - 4) + m:4 * (c - 4) + m + 1])

                split(("cin", l), 0)
                for c in range(1, 4):
                    split(("cin", l), c, {3 + m: v_part(c - 1, m) for m in range(TM)})
                split_next()
                for m in range(TM):
                    v_part(3, m)()
                split(("cin", l), 4)
                for c in range(5, 8):
                    split(("cin", l), c, {3 + m: u_part(c - 1, m) for m in range(4)})
                split_next()
                for m in range(4):
                    u_part(7, m)()
                mem_squares(l)
                for kt in range(16):
                    act.wait_ge(S["gt_ready"], kt + 1)
                    act.activation(gh[:, kt, :], gt[:, kt % 2, :], ACT.Copy).then_inc(S["gt_hi"], 1)
                for c in range(4):
                    split(("cout", l), c, {} if c != 1 else
                          {3 + m: (lambda m=m: tile_hi(("nmem", l, m), mh, m, KD)) for m in range(MM)})

            def cross(l):
                split(("kv", l), 0, {3 + m: (lambda m=m: x_square(3 * l, m)) for m in range(TM)})
                split(("kv", l), 1, {4: lambda: head_squares(("kv", l, 0), MM, X_DIM)})
                split(("kv", l), 2, {4: lambda: head_squares(("kv", l, 1), MM, X_DIM)})
                split_next()
                copy_out(("kv", l, 2), lambda m: xv[:, m, 0:512], range(MM))
                for m in range(TM):
                    tile_hi(("ncross", l, m), ah, m, KD)
                split(("xq", l), 0)
                split(("xq", l), 1, {3: lambda: head_squares(("xq", l, 0), TM, X_DIM)})
                split(("kv", l), 3, {3: lambda: head_squares(("xq", l, 1), TM, X_DIM)})
                split_next()
                copy_out(("kv", l, 3), lambda m: xv[:, m, 512:1024], range(MM))
                for r in range(2):
                    b = round_done(act, ("xqT", l, r))
                    for j in range(4):
                        ins = act.activation(xqT[:, 4 * r + j, :], ps[:, b + j, :], ACT.Copy,
                                             scale=xqg[:, l, j % 2:j % 2 + 1])
                    ins.then_inc(took(("xqT", l, r)), 1)
                attention("x", l, items_x, lambda i: MM, {})
                for m in range(TM):
                    tile_hi(("xoT", l, m), ah, m, KD)
                split(("xo", l), 0)
                split(("xo", l), 1)

            def silu(p):
                return act.activation(sg[SLOTS:P, :], ps[0:SLOTS, 2 + p, :], ACT.Silu)

            def hidden_copy():
                return act.activation(hT[:, :, :], ps[:, 4, :].rearrange("p (k n) -> p k n", n=P)[:, :, 0:SLOTS], ACT.Copy)

            def weigh(p):
                return act.activation(yw[:, p, :], ps[:, 5 + p, :], ACT.Copy, scale=wcol[:, p, :])

            def rows_copy():
                return act.activation(rows[:, :], ps[:, 0:2, :].rearrange("p a n -> p (a n)"), ACT.Copy)

            def experts(l):
                e0, q0 = EXPERTS * l, PAIRS * l
                for m in range(TM):
                    act.activation(xnh[:, m, :], xn[:, m, :], ACT.Copy).then_inc(S["xn_hi"], 1)
                b = round_done(act, ("route", l, 0))
                act.activation(lgT[:, :], ps[0:GROUPS + EXPERTS, b, :], ACT.Copy).then_inc(took(("route", l, 0)), 1)
                act.wait_ge(S["g_sub"], l + 1)
                act.activation(gee[:, :, :], ge[:, :, :], ACT.Exp).then_inc(S["g_exp"], 1)
                act.wait_ge(S["e_sub"], l + 1)
                act.activation(ex[:, :, :], ed[:, :, :], ACT.Exp).then_inc(S["e_exp"], 1)

                def do_rows(q):
                    act.wait_ge(S["x_gathered"], q + (q0 + 1))
                    after(act, S["rows_T"], q + q0)
                    rows_copy().then_inc(S["rows_ready"], 1)

                def expert(e, p, q, stored, last=False):
                    act.wait_ge(S["gu_done"], e + (e0 + 1))
                    after(act, S["h_ready"], e + e0)
                    silu(p).then_inc(S["silu_done"], 1)
                    act.wait_ge(S["hT_done"], e + (e0 + 1))
                    after(act, S["y_done"], e + e0)
                    hidden_copy().then_inc(S["hT_ready"], 1)
                    if p == 0 and not last:
                        do_rows(q + 1)
                    act.wait_ge(S["y_done"], e + (e0 + 1))
                    act.wait_ge(S["info_ready"], q + (q0 + 1))
                    after(act, y_stored[l][p], stored)
                    weigh(p).then_inc(S["yw_ready"], 1)

                do_rows(0)
                expert(0, 0, 0, 0)
                expert(1, 1, 0, 0)
                with act.Fori(1, PAIRS - 1) as i:
                    for p in range(2):
                        expert(i * 2 + p, p, i, i * 16)
                for p in range(2):
                    expert(EXPERTS - 2 + p, p, PAIRS - 1, 16 * (PAIRS - 1), last=True)
                n = act.value_load(mosti[0:1, 0:1], min_val=0, max_val=T)
                with act.Fori(1, PASSES) as c:
                    with act.If(n > c * SLOTS):
                        with act.Fori(0, PAIRS) as e:
                            at_ = lambda k: c * (OVER * PAIRS) + e * OVER + (1 - OVER * PAIRS + k)
                            act.wait_ge(over_step[l], at_(4))
                            rows_copy().then_inc(over_step[l], 1)
                            for p in range(2):
                                act.wait_ge(over_step[l], at_(10 + 8 * p))
                                silu(p).then_inc(over_step[l], 1)
                                act.wait_ge(over_step[l], at_(13 + 8 * p))
                                hidden_copy().then_inc(over_step[l], 1)
                                act.wait_ge(over_step[l], at_(15 + 8 * p))
                                weigh(p).then_inc(over_step[l], 1)
                        act.wait_ge(over_step[l], c * (OVER * PAIRS) + 1)
                        settle(act)
                    act.nop()

            for l in range(LAYERS):
                def x_tile(m):
                    if l == 0:
                        act.wait_ge(x_loaded[m], 16)
                        tile_square(x, m, junk)
                    else:
                        x_square(3 * l - 1, m)
                if l % 2:
                    b = round_done(act, ("wsT", l, 0))
                    act.activation(wsT[:, :, :], ps[:, b:b + 2, :].rearrange("p a (g n) -> p (a g) n", n=P),
                                   ACT.Copy).then_inc(took(("wsT", l, 0)), 1)
                norm("nmix", l, x_tile)
                fox(l) if l % 2 == 0 else gmlp(l)
                cross(l)
                act.wait_ge(S[f"small_loaded{l + 1}"], 32)
                act.activation(thin_view(whs), wsmall[:, :, :], ACT.Copy).then_inc(S["small_hi"], 1)
                norm("nffn", l, lambda m: x_square(3 * l + 1, m))
                experts(l)
            for m in range(TM):
                act.wait_ge(res_added, TM * (3 * LAYERS - 1) + m + 1)
                act.dma_start(x_out[:, m, :], x[:, m, :]).then_inc(out_stored, 16)
            act.wait_ge(out_stored, 16 * TM)

        @block.vector
        def _(dve):
            pos = [0]
            links = [0]

            def link(ins):
                links[0] += 1
                ins.then_inc(chain, 1)
                dve.wait_ge(chain, links[0])

            def split(key, c, between=None):
                first = first_step(*key, c)
                for s in sorted(between or {}):
                    pos[0] = split_lo(dve, pos[0], first + s)
                    between[s]()
                pos[0] = split_lo(dve, pos[0], first + 8)

            def split_next():
                pos[0] = split_lo(dve, pos[0], min(pos[0] + STAGE, N_STEPS))

            rstds, sqs = [0], [0]

            def scale(kind, l, m, src):
                n = NORMS.index((kind[1:], l))
                if m == 0:
                    dve.wait_ge(gain_loaded[n % 2], 16 * (n // 2 + 1))
                tiles = MM if kind == "nmem" else TM
                dve.wait_ge(norm_rstd, nats_upto(kind[1:], l) - tiles + m + 1)
                if kind == "ncross" or kind == "nmix" and m >= 2:
                    round_done(dve, (kind, l, m - 2) if m >= 2 else ("nmem", l, m))
                if (kind, m) == ("nmix", 1) and l % 2:
                    round_done(dve, ("wsT", l, 0))
                out_ = {"nffn": xn, "nmem": mem}.get(kind)
                dve.scalar_tensor_tensor(out=nat[:, m % 2, :] if out_ is None else out_[:, m, :], in0=src[:, m, :],
                                         scalar=rnorm[:, m:m + 1], in1=gain[:, n % 2, :],
                                         op0=ALU.mult, op1=ALU.mult).then_inc(nat_ready, 1)

            def norm(kind, l, feed=lambda m: None):
                feed(0)
                feed(1)
                scale(kind, l, 0, x)
                feed(2)
                scale(kind, l, 1, x)
                for m in range(TM):
                    tile_lo((kind, l, m), ah, al, m, KD)
                    if m == 0:
                        feed(3)
                    if m + 2 < TM:
                        scale(kind, l, m + 2, x)

            his = [0]

            def tile_lo(name, hi, lo, m, kts):
                his[0] += 1
                dve.wait_ge(hi_ready, his[0])
                b = 4 * (ROUND[name] % 2)
                src = ps[:, b:b + -(-kts // 4), :].rearrange("p a (k n) -> p (a k) n", n=P)
                dve.tensor_tensor(lo[:, 0:kts, m * P:(m + 1) * P], src,
                                  hi[:, 0:kts, m * P:(m + 1) * P].bitcast(F32), ALU.subtract).then_inc(took(name), 1)

            def head_means(name, tiles, nh, dim):
                for m in range(tiles):
                    dve.wait_ge(sq_ready, sqs[0] + 1)
                    sqs[0] += 1
                    dve.tensor_reduce(ss[:, m * nh:(m + 1) * nh],
                                      sq[:, (sqs[0] - 1) % 2, :].rearrange("p (h d) -> p h d", d=dim), AX.X, ALU.add)\
                       .then_inc(sq_used, 1)
                dve.wait_ge(sq_used, sqs[0])
                dve.engine_nop().then_inc(var_ready, 1)

            def head_scales(name, tiles, nh, dim, dst):
                rstds[0] += 1
                dve.wait_ge(rstd_ready, rstds[0])
                b = 4 * (ROUND[name] % 2)
                for m in range(tiles):
                    ins = dve.tensor_tensor(dst(m).rearrange("p (h d) -> p h d", d=dim),
                                            ps[:, b + m, :].rearrange("p (h d) -> p h d", d=dim),
                                            rstd[:, m * nh:(m + 1) * nh].unsqueeze(2).to_broadcast([P, nh, dim]), ALU.mult)
                ins.then_inc(took(name), 1)
                wait_taken(dve, name)
                dve.engine_nop().then_inc(heads_ready, 1)

            def residual(name, cols, last):
                b = round_done(dve, name)
                c = name[2]
                for m in range(TM):
                    xs = x[:, m, c * cols:(c + 1) * cols]
                    ins = dve.tensor_tensor(xs, ps[:, b + m, 0:cols], xs, ALU.add)
                    if last:
                        ins.then_inc(res_added, 1)
                if last:
                    dve.engine_nop().then_inc(took(name), 1)
                else:
                    ins.then_inc(took(name), 1)

            def attention(kind, l, items, nk_of, ow, dst, hooks):
                n0 = ATT0[kind, l]

                def maxima(n):
                    w = nk_of(items[n][1]) * P
                    dve.wait_ge(S["s_done"], n0 + n + 1)
                    dve.tensor_reduce(nmax[:, n:n + 1], ps[:, n % 3, 0:w], AX.X, ALU.max, negate=True)\
                       .then_inc(S["mx_done"], 1)

                def outputs(n):
                    h, i = items[n]
                    dve.wait_ge(S["p_done"], n0 + n + 1)
                    link(dve.reciprocal(rinv[:, n:n + 1], rsum[:, n:n + 1]))
                    dve.wait_ge(S["o_done"], n0 + n + 1)
                    dve.tensor_scalar(dst[:, i, h * ow:(h + 1) * ow], ps[:, 5 + n % 2, 0:ow], rinv[:, n:n + 1], None,
                                      ALU.mult).then_inc(S["o_copied"], 1)

                maxima(0)
                maxima(1)
                for n in range(len(items)):
                    if n + 2 < len(items):
                        maxima(n + 2)
                    if n:
                        outputs(n - 1)
                    if n in hooks:
                        hooks[n]()
                outputs(len(items) - 1)

            def fox(l):
                split(("in", l), 0)
                dve.wait_ge(S["small_hi"], 1)
                dve.tensor_tensor(thin_view(wls)[:, :, 0:A_HEADS], wsmall[:, :, 0:A_HEADS],
                                  thin_view(whs)[:, :, 0:A_HEADS].bitcast(F32), ALU.subtract).then_inc(S["small_lo"], 1)
                dve.wait_ge(params, 32)
                link(dve.tensor_scalar(qg[:, :], qg[:, :], float(A_DIM) ** -0.5, None, ALU.mult))
                link(dve.tensor_scalar(xqg[:, :, :], xqg[:, :, :], float(X_DIM) ** -0.5, None, ALU.mult))
                args = (TM, A_HEADS, A_DIM)
                split(("in", l), 1, {3: lambda: head_means(("in", l, 0), *args),
                                     6: lambda: head_scales(("in", l, 0), *args, lambda m: qn[:, m, :])})
                split(("in", l), 2, {3: lambda: head_means(("in", l, 1), *args),
                                     6: lambda: head_scales(("in", l, 1), *args, lambda m: kn[:, m, :])})
                split(("in", l), 3)
                b = round_done(dve, ("f", l, 0))
                dve.tensor_scalar(zf[:, :], ps[0:A_HEADS, b, :], fbias[:, :], None, ALU.add)\
                   .then_inc(took(("f", l, 0)), 1)
                wait_taken(dve, ("f", l, 0))
                for dst, src in ((ef[:, :], zf[:, :]), (spl[:, :], lam[:, :])):
                    link(dve.tensor_scalar(dst, src, -1.0, None, ALU.mult))
                    dve.tensor_tensor(dst, dst, src, ALU.min).then_inc(S["f_z"], 1)
                link(dve.tensor_scalar(zf[:, :], zf[:, :], 0.0, None, ALU.min))
                link(dve.tensor_scalar(lam2[:, :], lam[:, :], 0.0, None, ALU.min))
                dve.wait_ge(S["f_ln"], 2)
                link(dve.tensor_tensor(zf[:, :], zf[:, :], ef[:, :], ALU.subtract))
                dve.tensor_tensor_scan(negc[:, :], onecol[0:A_HEADS, :].to_broadcast([A_HEADS, T]), zf[:, :], 0.0,
                                       ALU.mult, ALU.subtract).then_inc(S["negc_ready"], 1)
                link(dve.tensor_tensor(spl[:, :], lam2[:, :], spl[:, :], ALU.subtract))
                link(dve.tensor_scalar(spl[:, :], spl[:, :], RG_C, None, ALU.mult))
                split(("in", l), 4)
                wait_taken(dve, ("in", l, 3))
                wait_taken(dve, ("nmix", l, TM - 1))
                for m in range(4):
                    link(dve.tensor_scalar(xcT[:, m, :], xbT[:, m, :], convw[:, m, CONV - 1:CONV], convb[:, m:m + 1],
                                           ALU.mult, ALU.add))
                    for k in range(CONV - 1):
                        s = CONV - 1 - k
                        ins = dve.scalar_tensor_tensor(out=xcT[:, m, s:T], in0=xbT[:, m, 0:T - s],
                                                       scalar=convw[:, m, k:k + 1], in1=xcT[:, m, s:T],
                                                       op0=ALU.mult, op1=ALU.add)
                        if m == 3 and k == CONV - 2:
                            ins.then_inc(S["xc_ready"], 1)
                        else:
                            link(ins)
                split_next()
                for r in range(2):
                    b = round_done(dve, ("kT", l, r))
                    ins = dve.tensor_scalar(kT[0:A_DIM, 4 * r:4 * r + 4, :], ps[0:A_DIM, b:b + 4, :], kg[:, :], None,
                                            ALU.mult)
                    ins.then_inc(took(("kT", l, r)), 1)
                wait_taken(dve, ("rg", l, 0))
                wait_taken(dve, ("rg", l, 1))
                for m in range(4):
                    dve.tensor_tensor(iT[:, m, :], iT[:, m, :], xcT[:, m, :], ALU.mult)
                    dve.tensor_scalar(xbT[:, m, :], xbT[:, m, :], spl[:, m:m + 1], None, ALU.mult).then_inc(S["rg_l"], 1)

                def variance(m):
                    def run():
                        dve.wait_ge(S["rg_exp"], m + 1)
                        link(dve.tensor_tensor(xbT[:, m, :], aT[:, m, :], aT[:, m, :], ALU.mult))
                        dve.scalar_tensor_tensor(out=xbT[:, m, :], in0=xbT[:, m, :], scalar=1.0, in1=tanhs[:, m % 2, :],
                                                 op0=ALU.add, op1=ALU.mult).then_inc(S["rg_var"], 1)
                    return run

                def recur(m):
                    def run():
                        dve.wait_ge(S["rg_sqrt"], m + 1)
                        link(dve.tensor_tensor(iT[:, m, :], iT[:, m, :], xbT[:, m, :], ALU.mult))
                        link(dve.tensor_tensor_scan(xbT[:, m, :], aT[:, m, :], iT[:, m, :], 0.0, ALU.mult, ALU.add))
                        dve.tensor_tensor(gbT[:, m, :], gbT[:, m, :], xbT[:, m, :], ALU.mult).then_inc(S["rec_ready"], 1)
                    return run

                attention("a", l, items_a, lambda i: i + 1, A_DIM, on0,
                          {3: variance(0), 6: variance(1), 10: variance(2), 14: variance(3),
                           19: recur(0), 21: recur(1), 23: recur(2), 25: recur(3),
                           30: lambda: (scale("nmem", l, 0, mem), scale("nmem", l, 1, mem))})
                for m in range(4):
                    dve.wait_ge(S["rec_hi"], m + 1)
                    dve.tensor_tensor(al[:, 4 + m, :], gbT[:, m, :], ah[:, 4 + m, :].bitcast(F32),
                                      ALU.subtract).then_inc(S["rec_lo"], 1)
                for m in range(TM):
                    tile_lo(("oT", l, m), ah, al, m, 4)
                for m in range(MM):
                    tile_lo(("nmem", l, m), mh, ml, m, KD)
                split(("out", l), 0)
                split(("out", l), 1, {3: lambda: residual(("out", l, 0), 512, False)})

            def gmlp(l):
                def v_part(c, m):
                    def run():
                        n = c * TM + m
                        if n == 0:
                            dve.wait_ge(S["vbias_loaded"], 16)
                        b = round_done(dve, ("cin", l, c))
                        after(dve, S["v_out"], n - 1)
                        dve.tensor_tensor(gt[:, n % 2, :], ps[:, b + m, :], vbias[:, c * 512:(c + 1) * 512], ALU.add)\
                           .then_inc(S["v_pre"], 1)
                        if m == TM - 1:
                            dve.wait_ge(S["v_pre"], n + 1)
                            dve.engine_nop().then_inc(took(("cin", l, c)), 1)
                    return run

                split(("cin", l), 0)
                for c in range(1, 4):
                    split(("cin", l), c, {3 + m: v_part(c - 1, m) for m in range(TM)})
                split_next()
                for m in range(TM):
                    v_part(3, m)()
                split(("cin", l), 4)
                dve.wait_ge(S["v_out"], 16)
                link(dve.tensor_reduce(rinv[:, 0:TM], ss[:, 0:16].rearrange("p (m c) -> p m c", c=4), AX.X, ALU.add))
                dve.tensor_scalar(ss[:, 0:TM], rinv[:, 0:TM], 1.0 / C_W, None, ALU.mult).then_inc(var_ready, 1)
                rstds[0] += 1
                dve.wait_ge(rstd_ready, rstds[0])
                link(dve.tensor_copy(rx[:, :], rstd[:, 0:TM]))
                for c in range(5, 8):
                    split(("cin", l), c)
                    dve.tensor_scalar(v1[:, c - 5, :], v1[:, c - 5, :], rx[:, c - 5:c - 4], None, ALU.mult)\
                       .then_inc(S["v_scaled"], 1)
                split_next()
                dve.tensor_scalar(v1[:, 3, :], v1[:, 3, :], rx[:, 3:4], None, ALU.mult).then_inc(S["v_scaled"], 1)
                dve.wait_ge(S["bs_loaded"], 16)
                wait_taken(dve, ("cin", l, 7))
                dve.wait_ge(squares, nats_upto("mem", l))

                for kt in range(16):
                    name = ("mix", l, kt // 4)
                    b = round_done(dve, name)
                    after(dve, S["gt_lo"], kt - 1)
                    ins = dve.scalar_tensor_tensor(
                        out=gt[:, kt % 2, :].rearrange("p (n t) -> p n t", t=P),
                        in0=ps[:, b + kt % 4, :].rearrange("p (n t) -> p n t", t=P), scalar=vg[:, kt:kt + 1],
                        in1=bs[:, kt // 2, :].unsqueeze(1).to_broadcast([P, TM, P]), op0=ALU.mult, op1=ALU.add)
                    link(ins)
                    if kt % 4 == 3:
                        dve.engine_nop().then_inc(took(name), 1)
                    dve.tensor_tensor(gt[:, kt % 2, :], gt[:, kt % 2, :], uT[:, kt, :], ALU.mult).then_inc(S["gt_ready"], 1)
                    if kt == 7:
                        scale("nmem", l, 0, mem)
                        scale("nmem", l, 1, mem)
                split(("cout", l), 0)
                for c in range(1, 4):
                    between = {3: lambda c=c: residual(("cout", l, c - 1), 256, False)}
                    if c == 1:
                        between[3] = lambda: (residual(("cout", l, 0), 256, False),
                                              tile_lo(("nmem", l, 0), mh, ml, 0, KD))
                        between[4] = lambda: tile_lo(("nmem", l, 1), mh, ml, 1, KD)
                    split(("cout", l), c, between)

            def cross(l):
                last = ("out", l, 1, 512) if l % 2 == 0 else ("cout", l, 3, 256)
                args = (MM, 2, X_DIM)
                xkh = lambda c: lambda: head_scales(("kv", l, c), *args, lambda m: xkn[:, m, 512 * c:512 * (c + 1)])
                split(("kv", l), 0, {3: lambda: residual(last[:3], last[3], True)})
                split(("kv", l), 1, {2: lambda: scale("ncross", l, 0, x), 3: lambda: scale("ncross", l, 1, x),
                                     4: lambda: head_means(("kv", l, 0), *args), 6: xkh(0)})
                split(("kv", l), 2, {4: lambda: head_means(("kv", l, 1), *args), 6: xkh(1)})
                split_next()
                for m in range(TM):
                    tile_lo(("ncross", l, m), ah, al, m, KD)
                    if m + 2 < TM:
                        scale("ncross", l, m + 2, x)
                for r in range(2):
                    b = round_done(dve, ("xkT", l, r))
                    for j in range(4):
                        ins = dve.tensor_scalar(xkT[:, 4 * r + j, :], ps[:, b + j, 0:MEM], xkg[:, l, j % 2:j % 2 + 1],
                                                None, ALU.mult)
                    ins.then_inc(took(("xkT", l, r)), 1)
                args = (TM, 2, X_DIM)
                xqh = lambda c: lambda: head_scales(("xq", l, c), *args, lambda m: xqn[:, m, 512 * c:512 * (c + 1)])
                split(("xq", l), 0)
                split(("xq", l), 1, {3: lambda: head_means(("xq", l, 0), *args), 5: xqh(0)})
                split(("kv", l), 3, {3: lambda: head_means(("xq", l, 1), *args), 7: xqh(1)})
                split_next()
                attention("x", l, items_x, lambda i: MM, X_DIM, xon, {})
                for m in range(TM):
                    tile_lo(("xoT", l, m), ah, al, m, KD)
                split(("xo", l), 0)
                split(("xo", l), 1, {3: lambda: residual(("xo", l, 0), 512, False)})
                residual(("xo", l, 1), 512, True)

            def route(l):
                link(dve.memset(gpad[:, :, :], -3.0e38))
                b = round_done(dve, ("logits", l, 0))
                lv = ps[:, b, 0:TM * 64].rearrange("p (m n) -> p m n", n=64)[:, :, 0:36]
                dve.tensor_tensor(lg[:, :, :], lv, rbias[:, l, :].unsqueeze(1).to_broadcast([P, TM, 36]),
                                  ALU.add).then_inc(took(("logits", l, 0)), 1)
                wait_taken(dve, ("logits", l, 0))
                link(dve.tensor_copy(gpad[:, :, 0:GROUPS], lg[:, :, 0:GROUPS]))
                for m in range(TM):
                    ins = dve.max(gm8[:, m, :], gpad[:, m, :])
                link(ins)
                for m in range(TM):
                    ins = dve.max_index(gi8[:, m, :], gm8[:, m, :], gpad[:, m, :])
                link(ins)
                link(dve.tensor_copy(gif[:, :, :], gi8[:, :, 0:1]))
                dve.tensor_tensor(ge[:, :, :], lg[:, :, 0:GROUPS], gm8[:, :, 0:1].to_broadcast([P, TM, GROUPS]),
                                  ALU.subtract).then_inc(S["g_sub"], 1)
                link(dve.tensor_tensor(oh4[:, :, :], iota[:, 0:GROUPS].unsqueeze(1).to_broadcast([P, TM, GROUPS]),
                                       gif[:, :, :].to_broadcast([P, TM, GROUPS]), ALU.is_equal))
                link(dve.tensor_tensor(etmp[:, :, :, :],
                                       lg[:, :, GROUPS:36].rearrange("p m (g j) -> p m j g", g=GROUPS),
                                       oh4[:, :, :].unsqueeze(2).to_broadcast([P, TM, PER_GROUP, GROUPS]), ALU.mult))
                link(dve.tensor_reduce(esel[:, :, :], etmp[:, :, :, :], AX.X, ALU.add))
                for m in range(TM):
                    ins = dve.max(em8[:, m, :], esel[:, m, :])
                link(ins)
                for m in range(TM):
                    ins = dve.max_index(ei8[:, m, :], em8[:, m, :], esel[:, m, :])
                link(ins)
                dve.tensor_tensor(ed[:, :, :], em8[:, :, 1:2], em8[:, :, 0:1], ALU.subtract).then_inc(S["e_sub"], 1)
                link(dve.tensor_copy(eid[:, :, :], ei8[:, :, 0:2]))
                link(dve.scalar_tensor_tensor(out=eid[:, :, :], in0=gif[:, :, :].to_broadcast([P, TM, 2]),
                                              scalar=float(PER_GROUP), in1=eid[:, :, :], op0=ALU.mult, op1=ALU.add))
                ids = iota[:, 0:EXPERTS].unsqueeze(1).to_broadcast([P, TM, EXPERTS])
                link(dve.tensor_tensor(sel0[:, :, :], ids, eid[:, :, 0:1].to_broadcast([P, TM, EXPERTS]), ALU.is_equal))
                link(dve.tensor_tensor(sel1[:, :, :], ids, eid[:, :, 1:2].to_broadcast([P, TM, EXPERTS]), ALU.is_equal))
                dve.tensor_tensor(cnt[:, :, :], sel0[:, :, :], sel1[:, :, :], ALU.add).then_inc(S["cnt_ready"], 1)
                dve.wait_ge(S["g_exp"], l + 1)
                link(dve.tensor_reduce(gw[:, :, 0], gee[:, :, :], AX.X, ALU.add))
                link(dve.reciprocal(gw[:, :, :], gw[:, :, :]))
                dve.wait_ge(S["e_exp"], l + 1)
                link(dve.tensor_scalar(w01[:, :, 0:1], ex[:, :, :], 1.0, None, ALU.add))
                link(dve.reciprocal(w01[:, :, 0:1], w01[:, :, 0:1]))
                link(dve.tensor_tensor(w01[:, :, 0:1], w01[:, :, 0:1], gw[:, :, :], ALU.mult))
                link(dve.tensor_tensor(w01[:, :, 1:2], w01[:, :, 0:1], ex[:, :, :], ALU.mult))
                full = [P, TM, EXPERTS]
                link(dve.tensor_tensor(rt1[:, :, :], sel0[:, :, :], w01[:, :, 0:1].to_broadcast(full), ALU.mult))
                link(dve.tensor_tensor(rt2[:, :, :], sel1[:, :, :], w01[:, :, 1:2].to_broadcast(full), ALU.mult))
                tb = lambda j: tab[:, :, :, j].rearrange("p e m -> p m e")
                link(dve.tensor_tensor(tb(1), rt1[:, :, :], rt2[:, :, :], ALU.add))
                tk = tok2[:, :].unsqueeze(2).to_broadcast(full)
                link(dve.scalar_tensor_tensor(out=rt1[:, :, :], in0=tk, scalar=-NOWHERE, in1=sel0[:, :, :],
                                              op0=ALU.add, op1=ALU.mult))
                link(dve.scalar_tensor_tensor(out=rt2[:, :, :], in0=tk, scalar=2.0 * T - NOWHERE, in1=sel1[:, :, :],
                                              op0=ALU.add, op1=ALU.mult))
                link(dve.tensor_tensor(tb(2), rt1[:, :, :], rt2[:, :, :], ALU.add))
                b = round_done(dve, ("rank", l, 0))
                link(dve.scalar_tensor_tensor(out=rt1[:, :, :], in0=ps[:, b, 0:TM * EXPERTS].rearrange("p (m e) -> p m e", e=EXPERTS),
                                              scalar=1.0, in1=cnt[:, :, :], op0=ALU.add, op1=ALU.mult))
                link(dve.tensor_scalar(tb(0), rt1[:, :, :], -1.0, None, ALU.add))
                link(dve.tensor_reduce(most[:, :], ps[:, b, TM * EXPERTS:(TM + 1) * EXPERTS], AX.X, ALU.max))
                link(dve.tensor_copy(mosti[:, :], most[:, :]))
                link(dve.tensor_copy(iotac[:, :], iota[:, :]))
                link(dve.memset(hh[:, :], 0.0))
                dve.engine_nop().then_inc(took(("rank", l, 0)), 1)
                dve.engine_nop().then_inc(over_step[l], 1)
                dve.engine_nop().then_inc(S["tab_ready"], 1)

            def columns(src, q, stage):
                stage(dve.tensor_copy(te[:, :, :, :], tab[:, bass.ds(q * 2, 2), :, :]))
                for e in range(2):
                    ins = dve.tensor_tensor(oh[:, :, e * SLOTS:(e + 1) * SLOTS],
                                            src[:, :].unsqueeze(1).to_broadcast([P, TM, SLOTS]),
                                            te[:, e, :, 0:1].to_broadcast([P, TM, SLOTS]), ALU.is_equal)
                    if e == 0:
                        stage(ins)
                return ins

            def tokens_out():
                return dve.tensor_copy(xg[:, :, :].rearrange("p (a k) n -> p a (k n)", a=2), ps[:, 0:2, :])

            def info_out():
                pair = ps[:, 7, 0:4].rearrange("p (e c) -> p e c", c=2)
                return (dve.tensor_copy(wcol[:, :, :], pair[:, :, 0:1]),
                        dve.tensor_scalar(idx[:, :, :], pair[:, :, 1:2], big2[:, :], None, ALU.add))

            def hidden(p):
                return dve.tensor_tensor(hh[0:SLOTS, :], ps[SLOTS:P, 2 + p, :], sg[SLOTS:P, :], ALU.mult)

            def xn_los(l):
                all_taken(dve, ("route", l, 0))
                for m in range(TM):
                    dve.wait_ge(S["xn_hi"], TM * l + m + 1)
                    ins = dve.tensor_tensor(xnl[:, m, :], xn[:, m, :], xnh[:, m, :].bitcast(F32), ALU.subtract)
                ins.then_inc(S["xn_lo"], 1)

            def experts(l):
                e0, q0 = EXPERTS * l, PAIRS * l

                def prepare(q):
                    after(dve, S["rows_T"], q + q0)
                    n = [0]

                    def stage(ins):
                        n[0] += 1
                        ins.then_inc(dve_loop, 1)
                        dve.wait_ge(dve_loop, q * 2 + (2 * q0 + n[0]))
                    columns(iota, q, stage).then_inc(S["oh_ready"], 1)

                def take(q):
                    dve.wait_ge(S["rows_T"], q + (q0 + 1))
                    after(dve, S["gu_done"], q * 2 + e0)
                    tokens_out().then_inc(S["xg_ready"], 1)

                def info(q, stored):
                    after(dve, S["yw_ready"], q * 2 + e0)
                    after(dve, y_stored[l][0], stored)
                    after(dve, y_stored[l][1], stored)
                    info_out()[1].then_inc(S["info_ready"], 1)

                def hide(e, p):
                    dve.wait_ge(S["silu_done"], e + (e0 + 1))
                    after(dve, S["hT_done"], e + e0)
                    hidden(p).then_inc(S["h_ready"], 1)

                prepare(0)
                take(0)
                prepare(1)
                hide(0, 0)
                info(0, 0)
                hide(1, 1)
                take(1)
                with dve.Fori(1, PAIRS - 1) as i:
                    prepare(i + 1)
                    hide(i * 2, 0)
                    info(i, i * 16)
                    hide(i * 2 + 1, 1)
                    take(i + 1)
                hide(EXPERTS - 2, 0)
                info(PAIRS - 1, (PAIRS - 1) * 16)
                hide(EXPERTS - 1, 1)
                n = dve.value_load(mosti[0:1, 0:1], min_val=0, max_val=T)
                with dve.Fori(1, PASSES) as c:
                    with dve.If(n > c * SLOTS):
                        dve.wait_ge(S["yw_ready"], e0 + EXPERTS)
                        for p in range(2):
                            dve.wait_ge(y_stored[l][p], 16 * (EXPERTS // 2))
                        dve.tensor_scalar(iotac[:, :], iotac[:, :], float(SLOTS), None, ALU.add)
                        dve.drain()
                        with dve.Fori(0, PAIRS) as e:
                            at_ = lambda k: c * (OVER * PAIRS) + e * OVER + (1 - OVER * PAIRS + k)
                            dve.wait_ge(over_step[l], at_(0))
                            n_ = [0]

                            def stage(ins):
                                n_[0] += 1
                                ins.then_inc(over_step[l], 1)
                                dve.wait_ge(over_step[l], at_(n_[0]))
                            columns(iotac, e, stage).then_inc(over_step[l], 1)
                            dve.wait_ge(over_step[l], at_(6))
                            tokens_out().then_inc(over_step[l], 1)
                            for ins in info_out():
                                ins.then_inc(over_step[l], 1)
                            for p in range(2):
                                dve.wait_ge(over_step[l], at_(11 + 8 * p))
                                hidden(p).then_inc(over_step[l], 1)
                        dve.wait_ge(over_step[l], c * (OVER * PAIRS) + 1)
                        settle(dve)
                    dve.nop()

            def add_y(l):
                def run(m):
                    dve.wait_ge(y_in[m], 16 * (l + 1))
                    link(dve.tensor_tensor(x[:, m, :], x[:, m, :], yin[:, m, 0, :], ALU.add))
                    dve.tensor_tensor(x[:, m, :], x[:, m, :], yin[:, m, 1, :], ALU.add).then_inc(res_added, 1)
                return run

            for l in range(LAYERS):
                norm("nmix", l, add_y(l - 1) if l else lambda m: None)
                fox(l) if l % 2 == 0 else gmlp(l)
                cross(l)
                dve.wait_ge(S["small_hi"], l + 2)
                dve.tensor_tensor(thin_view(wls), wsmall[:, :, :], thin_view(whs).bitcast(F32),
                                  ALU.subtract).then_inc(S["small_lo"], 1)
                norm("nffn", l)
                xn_los(l)
                route(l)
                experts(l)
            for m in range(TM):
                add_y(LAYERS - 1)(m)

        @block.gpsimd
        def _(pool):
            links = [0]

            def link(ins):
                links[0] += 1
                ins.then_inc(pchain, 1)
                pool.wait_ge(pchain, links[0])

            def load_gain(kind, l):
                n = NORMS.index((kind, l))
                if n >= 2:
                    pool.wait_ge(nat_ready, nats_upto(*NORMS[n - 2]))
                pool.dma_start(gain[:, n % 2, :], row_bcast(A["norm_" + kind][l], D)).then_inc(gain_loaded[n % 2], 16)

            load_gain("mix", 0)
            pool.dma_start(wsmall[:, :, 0:A_HEADS], kcols(A["ab_w_in"][0], 3 * A_W, A_HEADS)).then_inc(S["small_loaded0"], 16)
            link(pool.memset(halfp[:, :], -0.5))
            link(pool.memset(ident[:, :], 0.0))
            link(pool.affine_select(out=ident[:, :], in_=ident[:, :], compare_op=ALU.not_equal, fill=1.0, base=0,
                               pattern=[[-1, P]], channel_multiplier=1))
            pool.engine_nop().then_inc(consts_ready, 1)

            powers, nsq = [0], [0]

            def power(n):
                powers[0] += 1
                pool.wait_ge(var_ready, powers[0])
                link(pool.tensor_scalar(rstd[:, 0:n], ss[:, 0:n], EPS, None, ALU.add))
                pool.tensor_tensor(rstd[:, 0:n], rstd[:, 0:n], halfp[:, 0:n], ALU.pow).then_inc(rstd_ready, 1)

            def norm_power(tiles):
                for m in range(tiles):
                    nsq[0] += 1
                    pool.wait_ge(squares, nsq[0])
                    link(pool.tensor_scalar(rnorm[:, m:m + 1], mean[:, m:m + 1], EPS, None, ALU.add))
                    pool.tensor_tensor(rnorm[:, m:m + 1], rnorm[:, m:m + 1], halfp[:, 0:1], ALU.pow)\
                        .then_inc(norm_rstd, 1)

            def constants():
                link(pool.memset(whs[:, :].bitcast(F32), 0.0))
                link(pool.memset(wls[:, :].bitcast(F32), 0.0))
                link(pool.memset(onecol[:, :], 1.0))
                link(pool.memset(ones[:, :], 1.0))
                link(pool.memset(qT[A_DIM:A_DIM + 1, :, :], 1.0))
                link(pool.memset(causal[:, :], 0.0))
                link(pool.affine_select(out=causal[:, :], in_=causal[:, :], compare_op=ALU.is_ge, fill=-BIG, base=0,
                                        pattern=[[-1, P]], channel_multiplier=1))
                link(pool.affine_select(out=before[:, :], in_=ones[:, :], compare_op=ALU.is_ge, fill=0.0, base=-1,
                                        pattern=[[1, P]], channel_multiplier=-1))
                link(pool.iota(iota[:, :], pattern=[[1, SLOTS]], base=0, channel_multiplier=0,
                               allow_small_or_imprecise_dtypes=True))
                link(pool.iota(tok2[:, :], pattern=[[2 * P, TM]], base=0, channel_multiplier=2,
                               allow_small_or_imprecise_dtypes=True))
                link(pool.memset(big2[0:SLOTS, :], NOWHERE))
                link(pool.memset(big2[SLOTS:P, :], NOWHERE + 1))
                pool.engine_nop().then_inc(consts_ready, 1)

            pool.dma_start(small[:, 0:PACKED], A["packed"]).then_inc(params, 16)
            pool.dma_start(wblk[:, :, :, :].rearrange("p a m n -> p (a m n)"), A["blocks"]).then_inc(params, 16)
            for l in range(LAYERS):
                norm_power(TM)
                if l % 2 == 0:
                    constants()
                    power(TM * A_HEADS)
                    power(TM * A_HEADS)
                    pool.wait_ge(S["rec_ready"], 4)
                    pool.wait_ge(heads_ready, 1)
                else:
                    round_done(pool, ("nmix", l, TM - 1))
                    pool.dma_start(vbias[:, :], row_bcast(A["c_b_in"][0, C_W:2 * C_W], C_W)).then_inc(S["vbias_loaded"], 16)
                    pool.dma_start(bs[:, :, :], A["c_b_s"][0].rearrange("(a g) t -> a g t", a=1)
                                   .to_broadcast([P, C_GROUPS, P])).then_inc(S["bs_loaded"], 16)
                    power(TM)
                    pool.wait_ge(S["v_pre"], 4 * TM)
                pool.dma_start(mem[:, :, :], mem_in).then_inc(S["mem_loaded"], 16)
                load_gain("mem", l)
                load_gain("cross", l)
                norm_power(MM)
                if l % 2:
                    for kt in range(16):
                        pool.wait_ge(S["gt_hi"], kt + 1)
                        pool.tensor_tensor(gl[:, kt, :], gt[:, kt % 2, :], gh[:, kt, :].bitcast(F32),
                                           ALU.subtract).then_inc(S["gt_lo"], 1)
                norm_power(TM)
                load_gain("ffn", l)
                power(2 * MM)
                power(2 * MM)
                power(2 * TM)
                power(2 * TM)
                round_done(pool, ("xoT", l, TM - 1))
                pool.dma_start(wsmall[:, :, 0:GROUPS], A["moe_wg"][l].rearrange("(k p) n -> p k n", p=P))\
                    .then_inc(S[f"small_loaded{l + 1}"], 16)
                pool.dma_start(wsmall[:, :, GROUPS:36], A["moe_we"][l].rearrange("(k p) n -> p k n", p=P))\
                    .then_inc(S[f"small_loaded{l + 1}"], 16)
                norm_power(TM)
                if l + 1 < LAYERS:
                    load_gain("mix", l + 1)
                    pool.dma_start(wsn[:, :, :], A["c_w_s"][0].rearrange("g t s -> t g s")).then_inc(S["ws_loaded"], 16)
                    pool.wait_ge(S["ws_loaded"], 16)
                    pool.affine_select(out=wsn[:, :, :], in_=wsn[:, :, :], compare_op=ALU.is_ge, fill=0.0, base=0,
                                       pattern=[[0, C_GROUPS], [-1, P]], channel_multiplier=1).then_inc(S["ws_masked"], 1)

                e0 = EXPERTS * l

                def scatter(p):
                    return pool.indirect_dma_start(
                        out=ydram[l], out_offset=bass.IndirectOffsetOnAxis(ap=idx[:, p, :], axis=0),
                        in_=yw[:, p, :], in_offset=None, bounds_check=4 * T - 1, oob_is_err=False)

                with pool.Fori(0, EXPERTS // 2) as i:
                    for p in range(2):
                        pool.wait_ge(S["yw_ready"], i * 2 + (e0 + p + 1))
                        settle(pool)
                        scatter(p).then_inc(y_stored[l][p], 16)
                nn = pool.value_load(mosti[0:1, 0:1], min_val=0, max_val=T)
                with pool.Fori(1, PASSES) as c:
                    with pool.If(nn > c * SLOTS):
                        with pool.Fori(0, PAIRS) as e:
                            for p in range(2):
                                pool.wait_ge(over_step[l], c * (OVER * PAIRS) + e * OVER + (17 + 8 * p - OVER * PAIRS))
                                settle(pool)
                                scatter(p).then_inc(over_stored[l], 16)
                                pool.wait_ge(over_stored[l], c * (16 * EXPERTS) + e * 32 + (16 * (p + 1) - 16 * EXPERTS))
                                pool.sem_inc(over_step[l], 1)
                        pool.wait_ge(over_step[l], c * (OVER * PAIRS) + 1)
                        settle(pool)
                    pool.nop()


_BIG = ["x", "mem", "norm_mix", "norm_cross", "norm_mem", "norm_ffn", "ab_w_in", "ab_w_out", "c_w_in", "c_b_in",
        "c_w_s", "c_b_s", "c_w_out", "x_wq", "x_wkv", "x_wo", "moe_wg", "moe_we", "moe_w_gate", "moe_w_up", "moe_w_down"]


def layout(inputs):
    import numpy as np
    a = {n: np.asarray(inputs[n]) for n in inputs}
    arrays = {n: np.ascontiguousarray(a[n]) for n in _BIG}
    packed = np.zeros((P, PACKED), np.float32)

    def put(name, value):
        lo, n, parts, _ = PACK[name]
        packed[0:parts, lo:lo + n] = value

    cols = lambda v: v.reshape(-1, P).T
    put("fbias", a["ab_f_bias"][0][:, None])
    put("qg", a["ab_q_gain"][0][:, None])
    put("kg", a["ab_k_gain"][0][:, None])
    put("convw", a["ab_conv_w"][0].reshape(CONV, 4, P).transpose(2, 1, 0).reshape(P, 4 * CONV))
    for name, key in (("convb", "ab_conv_b"), ("bab", "ab_ba"), ("bxb", "ab_bx"), ("lam", "ab_lambda"),
                      ("vg", "c_v_gain")):
        put(name, cols(a[key][0]))
    put("ub", cols(a["c_b_in"][0, 0:C_W]))
    for name, key in (("xqg", "x_q_gain"), ("xkg", "x_k_gain"), ("gcol", "norm_ffn")):
        put(name, np.concatenate([cols(a[key][l]) for l in range(LAYERS)], axis=1))
    put("rbias", np.concatenate([a["moe_bg"], a["moe_be"]], axis=1).reshape(1, -1))
    arrays["packed"] = packed
    blocks = np.zeros((P, 2, 4, P), np.float32)
    for j, key in enumerate(("ab_wa", "ab_wx")):
        for g in range(8):
            q = 64 * (g % 2)
            blocks[q:q + 64, j, g // 2, q:q + 64] = a[key][0, g]
    arrays["blocks"] = blocks.reshape(P, 8 * P)
    return arrays


def kernel(**inputs):
    import concourse.bacc as _bacc
    from concourse.bass_utils import run_bass_kernel_spmd as _run

    nc = _bacc.Bacc("TRN2", target_bir_lowering=False, num_devices=1)
    arrays = layout(inputs)
    aps = {n: nc.dram_tensor(f"in_{n}", v.shape, F32, kind="ExternalInput").ap() for n, v in arrays.items()}
    out = nc.dram_tensor("out_x", (1, T, D), F32, kind="ExternalOutput").ap()
    program(nc, aps, out)
    r = _run(nc, [{f"in_{n}": v for n, v in arrays.items()}], core_ids=[0])
    return r.results[0]["out_x"]
```

```python
from contextlib import ExitStack

import concourse.bass as bass
from concourse import mybir

F32 = mybir.dt.float32
F32R = mybir.dt.float32r
U32 = mybir.dt.uint32
I32 = mybir.dt.int32
ACT = mybir.ActivationFunctionType
ALU = mybir.AluOpType
AX = mybir.AxisListType

P = 128
D = 1024
KD = D // P
T = 512
TM = T // P
MEM = 256
MM = MEM // P
LAYERS = 2
EPS = 1e-6
A_HEADS, A_DIM = 8, 64
X_HEADS, X_DIM = 4, 256
A_W = A_HEADS * A_DIM
B_W = 512
CONV = 4
RG_C = 8.0
C_W = 2048
C_GROUPS, C_DIM = 8, 256
GROUPS, PER_GROUP = 4, 8
EXPERTS = GROUPS * PER_GROUP
FE = 512
KF = FE // P
SLOTS = 64
PASSES = T // SLOTS
BIG = 1e30
PAIRS = EXPERTS // 2
OVER = 35

RING = 6
UNIT = 2048
STAGE = 3
THIN = (KD - 1) * (GROUPS + EXPERTS) + P
STEPS = 4


def dense_plan():
    plan, unit = {}, 0
    for layer in range(LAYERS):
        dense = ([("in", 10), ("out", 4)] if layer % 2 == 0 else [("cin", 16), ("cout", 8)])
        for name, units in dense + [("kv", 6), ("xq", 4), ("kv3", 2), ("xo", 4)]:
            plan[name, layer] = (unit, units)
            unit += units
        plan["moe", layer] = (unit, EXPERTS * 6)
        unit += EXPERTS * 6
    return plan


PLAN = dense_plan()
STEP0 = {}
_steps = 0
for _key, (_u, _n) in PLAN.items():
    if _key[0] != "moe":
        STEP0[_key] = _steps
        _steps += STEPS * _n


def first_step(name, layer, c):
    return STEP0["kv3", layer] if (name, c) == ("kv", 3) else STEP0[name, layer] + 8 * c


def round_plan():
    names = []
    for l in range(LAYERS):
        names += [] if l % 2 == 0 else [("wsT", l, 0)]
        names += [("nmix", l, m) for m in range(TM)]
        if l % 2 == 0:
            names += [("in", l, c) for c in range(3)] + [("f", l, 0)] + [("in", l, c) for c in (3, 4)]
            names += [("qT", l, 0), ("qT", l, 1), ("kT", l, 0), ("kT", l, 1)]
            names += [("rg", l, 0), ("rg", l, 1)]
            names += [("out", l, 0)]
            names += [("nmem", l, m) for m in range(MM)] + [("out", l, 1)]
        else:
            names += [("cin", l, c) for c in range(4)] + [("cin", l, c) for c in range(4, 8)]
            names += [("mix", l, c) for c in range(4)] + [("cout", l, 0)]
            names += [("nmem", l, m) for m in range(MM)] + [("cout", l, c) for c in range(1, 4)]
        names += [("kv", l, c) for c in range(3)]
        names += [("ncross", l, m) for m in range(TM)] + [("xkT", l, 0), ("xkT", l, 1)]
        names += [("xq", l, c) for c in range(2)] + [("kv", l, 3)]
        names += [("xqT", l, c) for c in range(2)]
        names += [("xo", l, c) for c in range(2)]
        names += [("nffn", l, m) for m in range(TM)] + [("route", l, 0), ("logits", l, 0), ("rank", l, 0)]
    return {name: i for i, name in enumerate(names)}


ROUND = round_plan()
DENSE = ("in", "out", "cin", "cout", "kv", "xq", "xo")
PLAIN = {}
for _name in ROUND:
    if _name[0] not in DENSE:
        PLAIN[_name] = len(PLAIN)
NORMS = [(kind, l) for l in range(LAYERS) for kind in ("mix", "mem", "cross", "ffn")]


PACK = {}
PACKED = 0
for _name, _parts, _shape in (("fbias", A_HEADS, (1,)), ("qg", A_DIM, (1,)), ("kg", A_DIM, (1,)),
                              ("convw", P, (4, CONV)), ("convb", P, (4,)), ("bab", P, (4,)), ("bxb", P, (4,)),
                              ("lam", P, (4,)), ("xqg", P, (LAYERS, 2)), ("xkg", P, (LAYERS, 2)),
                              ("ub", P, (16,)), ("vg", P, (16,)),
                              ("rbias", P, (LAYERS, GROUPS + EXPERTS))):
    _n = 1
    for _s in _shape:
        _n *= _s
    PACK[_name] = (PACKED, _n, _parts, _shape)
    PACKED += _n


def program(nc, A, out):
    ctx = ExitStack()
    with ctx:
        at = [-(-nc.sbuf_base // 32) * 32]
        spot = {}

        def width(shape):
            n = 4
            for s in shape[1:]:
                n *= s
            return n

        def sb(name, shape, dt=F32, over=None, skip=0):
            if over is None:
                off = at[0]
                at[0] += -(-width(shape) // 32) * 32
            else:
                off = spot[over][0] + skip
                assert skip + width(shape) <= spot[over][1], (name, over)
            spot[name] = (off, width(shape))
            return nc.alloc_sbuf_tensor_at(name, shape, dt, offset=off)

        def sem(name):
            return ctx.enter_context(nc.semaphore(name))

        x = sb("x", [P, TM, D])
        ring = sb("ring", [P, RING, UNIT])
        wh = sb("wh", [P, STAGE, 512], F32R)
        wl = sb("wl", [P, STAGE, 512], F32R)
        acts = sb("acts", [P, 8192])
        ah = sb("ah", [P, KD, T], F32R, over="acts")
        al = sb("al", [P, KD, T], F32R, over="acts", skip=16384)
        nat = sb("nat", [P, 2, D])
        gain = sb("gain", [P, 2, D])
        ident = sb("ident", [P, P])
        before = sb("before", [P, P])
        ones = sb("ones", [P, P])
        causal = sb("causal", [P, P])
        iota = sb("iota", [P, SLOTS])
        halfp = sb("halfp", [P, 32])
        onecol = sb("onecol", [P, 1])
        ss = sb("ss", [P, 32])
        rstd = sb("rstd", [P, 32])
        mean = sb("mean", [P, TM])
        rnorm = sb("rnorm", [P, TM])
        rx = sb("rx", [P, TM])
        nmax = sb("nmax", [P, 32])
        rsum = sb("rsum", [P, 32])
        rinv = sb("rinv", [P, 32])
        work = sb("work", [P, 2048])
        extra = sb("extra", [P, 16384])
        small = sb("small", [P, PACKED])
        assert at[0] <= nc.sbuf_usable_end, (at[0], nc.sbuf_usable_end)
        junk = sb("junk", [P, D], over="work")
        prob = sb("prob", [P, 2, 512], over="work")
        sq = sb("sq", [P, 2, 512], over="work", skip=4096)

        def sm(name):
            lo, n, parts, shape = PACK[name]
            v = small[0:parts, lo:lo + n]
            if len(shape) == 2:
                v = v.rearrange("p (a b) -> p a b", b=shape[1])
            return v

        fbias, qg, kg = sm("fbias"), sm("qg"), sm("kg")
        convw, convb, bab, bxb, lam = sm("convw"), sm("convb"), sm("bab"), sm("bxb"), sm("lam")
        xqg, xkg, ub, vg, rbias = sm("xqg"), sm("xkg"), sm("ub"), sm("vg"), sm("rbias")
        lam2 = sb("lam2", [P, 4])
        spl = sb("spl", [P, 4])
        wsmall = sb("wsmall", [P, KD, 36], over="work", skip=4096)
        whs = sb("whs", [P, THIN], F32R)
        wls = sb("wls", [P, THIN], F32R)
        assert at[0] <= nc.sbuf_usable_end, (at[0], nc.sbuf_usable_end)

        E = 1024
        qT = sb("qT", [A_DIM + 1, A_HEADS, T], over="extra", skip=0)
        kT = sb("kT", [A_DIM + 1, A_HEADS, T], over="extra", skip=16 * E)
        v0 = sb("v0", [P, TM, A_W], over="extra", skip=32 * E)
        xbT = sb("xbT", [P, 4, T], over="extra", skip=40 * E)
        gbT = sb("gbT", [P, 4, T], over="extra", skip=48 * E)
        kn = sb("kn", [P, TM, A_W], over="extra", skip=56 * E)
        ptA = [sb(f"ptA{h}", [P, TM, T], over="acts", skip=(8 + 16 * h) * E) for h in range(2)]
        qn = sb("qn", [P, TM, A_W], over="nat")
        xcT = sb("xcT", [P, 4, T], over="gain")
        iT = sb("iT", [P, 4, T], over="nat")
        aT = sb("aT", [P, 4, T], over="gain")
        wblk = sb("wblk", [P, 2, 4, P])
        tanhs = sb("tanhs", [P, 2, T], over="wblk")
        negc = sb("negc", [A_HEADS, T], over="work")
        zf = sb("zf", [A_HEADS, T], over="work", skip=2048)
        ef = sb("ef", [A_HEADS, T], over="work", skip=4096)
        assert at[0] <= nc.sbuf_usable_end, (at[0], nc.sbuf_usable_end)
        v1 = sb("v1", [P, TM, C_W], over="extra", skip=0)
        uT = sb("uT", [P, 16, T], over="extra", skip=32 * E)
        gh = sb("gh", [P, 16, T], F32R, over="acts")
        gl = sb("gl", [P, 16, T], F32R, over="extra", skip=32 * E)
        vbias = sb("vbias", [P, 2048], over="nat")
        wsT = sb("wsT", [P, C_GROUPS, P], over="wblk")
        wsn = sb("wsn", [P, C_GROUPS, P], over="nat", skip=4 * E)
        bs = sb("bs", [P, C_GROUPS, P], over="work", skip=4096)
        gt = sb("gt", [P, 2, T], over="work")
        vjunk = sb("vjunk", [P, T], over="extra", skip=36 * E)
        mem = sb("mem", [P, MM, D], over="nat")
        mem_junk = sb("mem_junk", [P, D], over="wblk")
        mh = sb("mh", [P, KD, MEM], F32R, over="extra", skip=0)
        ml = sb("ml", [P, KD, MEM], F32R, over="extra", skip=8 * E)
        xkn = sb("xkn", [P, MM, D], over="extra", skip=24 * E)
        xkT = sb("xkT", [P, KD, MEM], over="extra", skip=32 * E)
        xv = sb("xv", [P, MM, D], over="extra", skip=40 * E)
        xqT = sb("xqT", [P, KD, T], over="extra", skip=48 * E)
        xqn = sb("xqn", [P, TM, D], over="extra", skip=16 * E)
        ptX = [sb(f"ptX{h}", [P, MM, T], over="extra", skip=(16 + 4 * h) * E) for h in range(2)]
        lg = sb("lg", [P, TM, 36], over="extra", skip=0)
        gpad = sb("gpad", [P, TM, 8], over="extra", skip=1 * E)
        gm8 = sb("gm8", [P, TM, 8], over="extra", skip=1 * E + 128)
        gi8 = sb("gi8", [P, TM, 8], U32, over="extra", skip=1 * E + 256)
        gif = sb("gif", [P, TM, 1], over="extra", skip=1 * E + 384)
        ge = sb("ge", [P, TM, 4], over="extra", skip=1 * E + 448)
        gee = sb("gee", [P, TM, 4], over="extra", skip=1 * E + 512)
        gw = sb("gw", [P, TM, 1], over="extra", skip=1 * E + 576)
        oh4 = sb("oh4", [P, TM, 4], over="extra", skip=1 * E + 640)
        esel = sb("esel", [P, TM, 8], over="extra", skip=1 * E + 704)
        em8 = sb("em8", [P, TM, 8], over="extra", skip=1 * E + 832)
        ei8 = sb("ei8", [P, TM, 8], U32, over="extra", skip=2 * E)
        w01 = sb("w01", [P, TM, 2], over="extra", skip=2 * E + 128)
        ed = sb("ed", [P, TM, 1], over="extra", skip=2 * E + 192)
        ex = sb("ex", [P, TM, 1], over="extra", skip=2 * E + 256)
        eid = sb("eid", [P, TM, 2], over="extra", skip=2 * E + 320)
        etmp = sb("etmp", [P, TM, 8, 4], over="extra", skip=3 * E)
        sel0 = sb("sel0", [P, TM, EXPERTS], over="extra", skip=4 * E)
        sel1 = sb("sel1", [P, TM, EXPERTS], over="extra", skip=5 * E)
        cnt = sb("cnt", [P, TM, EXPERTS], over="extra", skip=6 * E)
        rt1 = sb("rt1", [P, TM, EXPERTS], over="extra", skip=7 * E)
        rt2 = sb("rt2", [P, TM, EXPERTS], over="extra", skip=8 * E)
        tab = sb("tab", [P, EXPERTS, TM, 2], over="extra", skip=9 * E)
        most = sb("most", [P, 1], over="extra", skip=11 * E)
        mosti = sb("mosti", [P, 1], I32, over="extra", skip=11 * E + 64)
        te = sb("te", [P, 2, TM, 2], over="extra", skip=11 * E + 128)
        oh = sb("oh", [P, TM, 2 * SLOTS], F32R, over="extra", skip=12 * E)
        xg = sb("xg", [P, KD, 2 * SLOTS], over="extra", skip=14 * E)
        sg = sb("sg", [P, FE], over="extra", skip=18 * E)
        hh = sb("hh", [P, FE], over="extra", skip=20 * E)
        hT = sb("hT", [P, KF, SLOTS], over="extra", skip=22 * E)
        wcol = sb("wcol", [P, 2, 1], over="extra", skip=27 * E)
        yh = sb("yh", [P, D], F32R, over="acts", skip=0)
        yl = sb("yl", [P, D], F32R, over="acts", skip=4 * E)
        yw = sb("yw", [P, D], over="acts", skip=8 * E)
        selT = sb("selT", [P, T], F32R, over="acts", skip=12 * E)
        iotac = sb("iotac", [P, SLOTS], over="extra", skip=27 * E + 128)
        lgT = sb("lgT", [GROUPS + EXPERTS, T], over="extra", skip=28 * E)
        rows = sb("rows", [P, D], over="extra", skip=28 * E)
        xn = sb("xn", [P, TM, D], over="extra", skip=32 * E)
        xnl = sb("xnl", [P, TM, D], F32R, over="extra", skip=32 * E)
        xnh = sb("xnh", [P, TM, D], F32R, over="extra", skip=48 * E)

        ps = ctx.enter_context(nc.psum_tensor("ps", [P, 8, 512], F32))

        ring_full = [sem(f"ring_full{i}") for i in range(RING)]
        wh_ready, wl_ready, w_used = sem("wh_ready"), sem("wl_ready"), sem("w_used")
        acc_done = sem("acc_done")
        taken = [sem("taken0"), sem("taken1")]
        expert_used = sem("expert_used")
        consts_ready = sem("consts_ready")
        params = sem("params_loaded")
        x_loaded = [sem(f"x_loaded{m}") for m in range(TM)]
        gain_loaded = [sem("gain_loaded0"), sem("gain_loaded1")]
        squares = sem("squares")
        norm_rstd = sem("norm_rstd")
        var_ready, rstd_ready = sem("var_ready"), sem("rstd_ready")
        nat_ready = sem("nat_ready")
        hi_ready = sem("hi_ready")
        sq_ready, sq_used = sem("sq_ready"), sem("sq_used")
        heads_ready = sem("heads_ready")
        res_added = sem("res_added")
        out_stored = sem("out_stored")
        S = {n: sem(n) for n in (
            "small_loaded0 small_loaded1 small_loaded2 small_hi small_lo "
            "f_z f_e f_ln negc_ready c_row xc_ready rg_l rg_exp rg_var "
            "rg_sqrt rec_ready rec_hi rec_lo "
            "s_done mx_done p_done pn_done pt_done pt_copied o_done o_hi o_copied "
            "mem_loaded v_pre v_out vbias_loaded bs_loaded v_scaled ws_loaded ws_masked gt_ready gt_hi gt_lo "
            "g_sub g_exp e_sub e_exp cnt_ready tab_ready "
            "xn_hi xn_lo oh_ready x_gathered rows_ready rows_T slots_done xg_ready info_ready gu_done silu_done "
            "h_ready hT_done hT_ready y_done yw_ready yh_ready y_split mixed y_added"
        ).split()}
        over_full = [sem(f"over_full{l}") for l in range(LAYERS)]
        over_step = [sem(f"over_step{l}") for l in range(LAYERS)]
        chain, achain, pchain = sem("dve_chain"), sem("act_chain"), sem("pool_chain")
        dve_loop = sem("dve_loop_chain")
        settled = sem("settled")

        block = ctx.enter_context(nc.Block())

        x_in = A["x"].rearrange("b (m p) d -> p (b m) d", p=P)
        x_out = out.rearrange("b (m p) d -> p (b m) d", p=P)
        mem_in = A["mem"].rearrange("b (m p) d -> p (b m) d", p=P)
        IN_COL = [0, A_W, 2 * A_W, 3 * A_W + A_HEADS, 3 * A_W + A_HEADS + B_W]

        def kcols(w, c0, n):
            return w[:, c0:c0 + n].rearrange("(k p) n -> p k n", p=P)

        def dense_unit(name, l, u):
            if name == "cout":
                c, half = divmod(u, 2)
                return kcols(A["c_w_out"][0], 256 * c, 256)[:, 8 * half:8 * half + 8], 256
            c = u // 2
            w, col = {"in": (A["ab_w_in"][0], IN_COL[c % 5]),
                      "out": (A["ab_w_out"][0], 512 * c),
                      "cin": (A["c_w_in"][0], 512 * ((c + 4) % 8)),
                      "kv": (A["x_wkv"][l], 512 * c),
                      "kv3": (A["x_wkv"][l], 512 * 3),
                      "xq": (A["x_wq"][l], 512 * c),
                      "xo": (A["x_wo"][l], 512 * c)}[name]
            return kcols(w, col, 512)[:, 4 * (u % 2):4 * (u % 2) + 4], 512

        def row_bcast(v, n):
            return v.rearrange("(a n) -> a n", a=1).to_broadcast([P, n])

        def expert_unit(l, e, j):
            w = A["moe_w_down"] if j >= 4 else A[("moe_w_gate", "moe_w_up")[j % 2]]
            src = w[l][bass.ds(e, 1)].rearrange("a (k p) f -> p (a k) f", p=P)
            return (src[:, 4 * (j // 2):4 * (j // 2) + 4], 512) if j < 4 else (src[:, 2 * (j - 4):2 * (j - 4) + 2], 1024)

        def units_before(unit):
            dense = sum(min(max(unit - u, 0), n) for (name, _), (u, n) in PLAN.items() if name != "moe")
            return dense, unit - dense

        def slot(unit, cols):
            return ring[:, unit % RING, :].rearrange("p (k n) -> p k n", n=cols)

        def thin_view(w):
            return w[:, 0:KD * 36].rearrange("p (k n) -> p k n", n=36)

        def after(eng, s, n):
            if not isinstance(n, int) or n > 0:
                eng.wait_ge(s, n)

        def nats_upto(kind, l):
            done = NORMS[:NORMS.index((kind, l)) + 1]
            return sum(MM if k == "mem" else TM for k, _ in done)

        def settle(eng):
            eng.sem_inc(settled, 1)

        def round_done(eng, name):
            if name[0] in DENSE:
                eng.wait_ge(w_used, first_step(*name) + 8)
            else:
                eng.wait_ge(acc_done, PLAIN[name] + 1)
            return 4 * (ROUND[name] % 2)

        def took(name):
            return taken[ROUND[name] % 2]

        def wait_taken(eng, name):
            eng.wait_ge(taken[ROUND[name] % 2], ROUND[name] // 2 + 1)

        def all_taken(eng, next_name):
            r = ROUND[next_name] if next_name in ROUND else len(ROUND)
            eng.wait_ge(taken[0], (r + 1) // 2)
            eng.wait_ge(taken[1], r // 2)

        def split_hi(act, pos, upto):
            for t in range(pos, upto):
                unit, s = unit_of_step(t)
                if s == 0:
                    act.wait_ge(ring_full[unit % RING], 16 * (unit // RING + 1))
                after(act, w_used, t - STAGE + 1)
                act.activation(wh[:, t % STAGE, :], ring[:, unit % RING, 512 * s:512 * (s + 1)],
                               ACT.Copy).then_inc(wh_ready, 1)
            return max(pos, upto)

        def split_lo(dve, pos, upto):
            for t in range(pos, upto):
                unit, s = unit_of_step(t)
                dve.wait_ge(wh_ready, t + 1)
                dve.tensor_tensor(wl[:, t % STAGE, :], ring[:, unit % RING, 512 * s:512 * (s + 1)],
                                  wh[:, t % STAGE, :].bitcast(F32), ALU.subtract).then_inc(wl_ready, 1)
            return max(pos, upto)

        def unit_of_step(t):
            for key, t0 in STEP0.items():
                if t0 <= t < t0 + STEPS * PLAN[key][1]:
                    return PLAN[key][0] + (t - t0) // STEPS, (t - t0) % STEPS
            raise AssertionError(t)

        N_STEPS = _steps
        items_a = [(h, i) for h in range(A_HEADS) for i in range(TM)]
        items_x = [(h, i) for h in range(X_HEADS) for i in range(TM)]
        SCORES, T_BANK, O_BANK = 3, 3, 5
        SHAPE = {"a": (1, 2, 2), "x": (2, 1, 1)}
        PT = {"a": ptA, "x": ptX}
        HEAD0 = {("a", 0): 0, ("x", 0): A_HEADS, ("x", 1): A_HEADS + X_HEADS}
        GROUP0 = {("a", 0): 0, ("x", 0): A_HEADS // 2, ("x", 1): A_HEADS // 2 + X_HEADS}
        ATT0 = {}
        n_att = 0
        for l in range(LAYERS):
            if l % 2 == 0:
                ATT0["a", l] = n_att
                n_att += len(items_a)
            ATT0["x", l] = n_att
            n_att += len(items_x)


        @block.sync
        def _(sp):
            for m in range(TM):
                sp.dma_start(x[:, m, :], x_in[:, m, :]).then_inc(x_loaded[m], 16)

            def expert_done_with(l, e, j):
                if j in (3, 5):
                    sp.wait_ge(S["gu_done" if j == 3 else "y_done"], e + EXPERTS * l)
                else:
                    sp.wait_ge(expert_used, e * 4 + (4 * (EXPERTS * l - 1) + (1, 2, 3, 0, 4)[j]))

            def free_slot(unit):
                if unit >= RING:
                    dense, moe = units_before(unit - RING + 1)
                    if dense > units_before(unit - RING)[0]:
                        sp.wait_ge(wl_ready, STEPS * dense)
                    else:
                        expert_done_with((moe - 1) // (6 * EXPERTS), EXPERTS, (moe - 1) % 6)

            for (name, l), (u0, n) in PLAN.items():
                if name != "moe":
                    for u in range(u0, u0 + n):
                        free_slot(u)
                        src, cols = dense_unit(name, l, u - u0)
                        sp.dma_start(slot(u, cols), src).then_inc(ring_full[u % RING], 16)
                    continue
                for j in range(6):
                    free_slot(u0 + j)
                    src, cols = expert_unit(l, 0, j)
                    sp.dma_start(slot(u0 + j, cols), src).then_inc(ring_full[(u0 + j) % RING], 16)
                with sp.Fori(1, EXPERTS) as e:
                    for j in range(6):
                        expert_done_with(l, e, j)
                        src, cols = expert_unit(l, e, j)
                        sp.dma_start(slot(u0 + j, cols), src).then_inc(ring_full[(u0 + j) % RING], 16)
                sp.wait_ge(S["tab_ready"], l + 1)
                n = sp.value_load(mosti[0:1, 0:1], min_val=0, max_val=T)
                with sp.If(n > SLOTS):
                    with sp.Fori(1, PASSES) as c:
                        with sp.If(n > c * SLOTS):
                            expert_done_with(l, EXPERTS, 5)
                            with sp.Fori(0, PAIRS) as e:
                                for half in range(2):
                                    sp.wait_ge(over_step[l], c * (OVER * PAIRS) + e * OVER + (1 - OVER * PAIRS + 18 * half))
                                    for j in range(6):
                                        src, cols = expert_unit(l, e * 2 + half, j)
                                        sp.dma_start(slot(u0 + j, cols), src).then_inc(over_full[l], 16)
                            sp.wait_ge(over_step[l], c * (OVER * PAIRS) + 1)
                            settle(sp)
                        sp.nop()
                sp.nop()
            sp.wait_ge(out_stored, 16 * TM)

        @block.tensor
        def _(pe):
            pe.wait_ge(consts_ready, 1)

            def begin(name):
                r = ROUND[name]
                after(pe, taken[r % 2], r // 2)
                return 4 * (r % 2)

            def dense(name, l, c, hi, lo, cols=512, flip=False, rows=TM, ready=None):
                b = begin((name, l, c))
                per = 512 // cols
                for s in range(8):
                    t = first_step(name, l, c) + s
                    pe.wait_ge(wl_ready, t + 1)
                    for kk in range(per):
                        k = s * per + kk
                        if ready:
                            ready(k)
                        for m in range(rows):
                            for i, (w, a) in enumerate(((wh, hi), (wl, hi), (wh, lo))):
                                flags = dict(start=(k == 0 and i == 0), stop=(k == 8 * per - 1 and i == 2))
                                if flip:
                                    mm = pe.matmul(ps[:, b + m, 0:T], w[:, t % STAGE, m * P:(m + 1) * P],
                                                   a[:, k, :], **flags)
                                else:
                                    mm = pe.matmul(ps[:, b + m, 0:cols], a[:, k, m * P:(m + 1) * P],
                                                   w[:, t % STAGE, kk * cols:(kk + 1) * cols], **flags)
                    mm.then_inc(w_used, 1)

            nats = [0]

            def norm_T(kind, l, tiles):
                for m in tiles:
                    b = begin((kind, l, m))
                    nats[0] += 1
                    pe.wait_ge(nat_ready, nats[0])
                    for k in range(KD):
                        mm = pe.transpose(ps[:, b + k // 4, (k % 4) * P:(k % 4 + 1) * P],
                                          xn[:, m, k * P:(k + 1) * P] if kind == "nffn"
                                          else nat[:, m % 2, k * P:(k + 1) * P], ident[:, :])
                    mm.then_inc(acc_done, 1)

            def split_written(kind, l, tiles):
                for m in range(tiles - 2, tiles):
                    wait_taken(pe, (kind, l, m))

            def thin(name, l, which):
                b = begin((name, l, 0))
                pe.wait_ge(S["small_lo"], which + 1)
                for k in range(KD):
                    for i, (w, a) in enumerate(((whs, ah), (wls, ah), (whs, al))):
                        mm = pe.matmul(ps[:, b, 0:T], w[:, 36 * k:36 * k + P], a[:, k, :],
                                       start=(k == 0 and i == 0), stop=(k == KD - 1 and i == 2))
                mm.then_inc(acc_done, 1)

            def attention(kind, l, items, nk_of, score, head_values, next_name):
                n0, g0 = ATT0[kind, l], GROUP0[kind, l]
                o_banks, o_buffers, heads = SHAPE[kind]
                all_taken(pe, next_name)

                def scores(n):
                    if n >= SCORES:
                        pe.wait_ge(S["p_done"], n0 + n - SCORES + 1)
                    score(*items[n], n % SCORES).then_inc(S["s_done"], 1)

                def transposes(n):
                    h, i = items[n]
                    pe.wait_ge(S["pn_done"], n0 + n + 1)
                    if n >= 2:
                        pe.wait_ge(S["pt_copied"], n0 + n - 1)
                    for j in range(nk_of(i)):
                        mm = pe.transpose(ps[:, T_BANK + n % 2, j * P:(j + 1) * P],
                                          prob[:, n % 2, j * P:(j + 1) * P], ident[:, :])
                    mm.then_inc(S["pt_done"], 1)

                def values(h):
                    g = h // heads
                    pe.wait_ge(S["pt_copied"], n0 + TM * (h + 1))
                    if g >= o_buffers and h % heads == 0:
                        pe.wait_ge(S["o_copied"], g0 + g - o_buffers + 1)
                    head_values(h, O_BANK + o_banks * (g % o_buffers), PT[kind][h % 2]).then_inc(S["o_done"], 1)

                for n in range(SCORES - 1):
                    scores(n)
                for n in range(len(items)):
                    if n + SCORES - 1 < len(items):
                        scores(n + SCORES - 1)
                    transposes(n)
                    if n % TM == 0 and n:
                        values(n // TM - 1)
                values(len(items) // TM - 1)
                pe.wait_ge(S["o_copied"], g0 + len(items) // TM // heads)

            def fox(l):
                for c in range(3):
                    dense("in", l, c, ah, al)
                thin("f", l, 0)
                for c in (3, 4):
                    dense("in", l, c, ah, al, flip=True)
                for name, src, n in (("qT", qn, 1), ("kT", kn, 2)):
                    pe.wait_ge(heads_ready, n)
                    for r in range(2):
                        b = begin((name, l, r))
                        for j in range(4):
                            h = 4 * r + j
                            for m in range(TM):
                                mm = pe.transpose(ps[0:A_DIM, b + j, m * P:(m + 1) * P],
                                                  src[:, m, h * A_DIM:(h + 1) * A_DIM], ident[:, :])
                        mm.then_inc(acc_done, 1)
                pe.wait_ge(S["xc_ready"], 1)
                for g in range(2):
                    b = begin(("rg", l, g))
                    for m in range(4):
                        mm = pe.matmul(ps[:, b + m, :], wblk[:, g, m, :], xcT[:, m, :], start=True, stop=True)
                    mm.then_inc(acc_done, 1)
                pe.wait_ge(S["c_row"], 16)
                wait_taken(pe, ("in", l, 2))

                def score(h, i, bank):
                    n = (i + 1) * P
                    pe.matmul(ps[:, bank, 0:n], qT[:, h, i * P:(i + 1) * P], kT[:, h, 0:n], start=True, stop=False)
                    return pe.matmul(ps[:, bank, i * P:n], ident[:, :], causal[:, :], start=False, stop=True)

                def head_values(h, bank, pt):
                    for j in range(TM):
                        mm = pe.matmul(ps[h % 2 * A_DIM:(h % 2 + 1) * A_DIM, bank, j * P:T],
                                       v0[:, j, h * A_DIM:(h + 1) * A_DIM], pt[:, j, j * P:T],
                                       start=(j == 0), stop=(j == TM - 1))
                    return mm

                attention("a", l, items_a, lambda i: i + 1, score, head_values, ("out", l, 0))
                dense("out", l, 0, ah, al, ready=lambda k: after(pe, S["rec_lo"], k - 3))
                norm_T("nmem", l, range(MM))
                dense("out", l, 1, ah, al)

            def gmlp(l):
                for c in range(4):
                    dense("cin", l, c, ah, al)
                for c in range(4, 8):
                    dense("cin", l, c, ah, al, flip=True)
                pe.wait_ge(S["v_scaled"], TM)
                for r in range(4):
                    b = begin(("mix", l, r))
                    for j in range(4):
                        kt = 4 * r + j
                        for n in range(TM):
                            mm = pe.matmul(ps[:, b + j, n * P:(n + 1) * P], v1[:, n, kt * P:(kt + 1) * P],
                                           wsT[:, kt // 2, :], start=True, stop=True)
                    mm.then_inc(acc_done, 1)
                for c in range(4):
                    dense("cout", l, c, gh, gl, cols=256,
                          ready=(lambda k: pe.wait_ge(S["gt_lo"], k + 1)) if c == 0 else None)
                    if c == 0:
                        norm_T("nmem", l, range(MM))

            def cross(l):
                split_written("nmem", l, MM)
                for c in range(3):
                    dense("kv", l, c, mh, ml, rows=MM)
                norm_T("ncross", l, range(TM))
                n0 = (2 if l == 0 else 6)
                pe.wait_ge(heads_ready, n0 + 2)
                for r in range(2):
                    b = begin(("xkT", l, r))
                    for j in range(4):
                        for m in range(MM):
                            mm = pe.transpose(ps[:, b + j, m * P:(m + 1) * P],
                                              xkn[:, m, (4 * r + j) * P:(4 * r + j + 1) * P], ident[:, :])
                    mm.then_inc(acc_done, 1)
                split_written("ncross", l, TM)
                for c in range(2):
                    dense("xq", l, c, ah, al)
                dense("kv", l, 3, mh, ml, rows=MM)
                for r in range(2):
                    b = begin(("xqT", l, r))
                    pe.wait_ge(heads_ready, n0 + 3 + r)
                    for j in range(4):
                        for m in range(TM):
                            mm = pe.transpose(ps[:, b + j, m * P:(m + 1) * P],
                                              xqn[:, m, (4 * r + j) * P:(4 * r + j + 1) * P], ident[:, :])
                    mm.then_inc(acc_done, 1)

                def score(h, i, bank):
                    for kk in range(2):
                        mm = pe.matmul(ps[:, bank, 0:MEM], xqT[:, 2 * h + kk, i * P:(i + 1) * P],
                                       xkT[:, 2 * h + kk, :], start=(kk == 0), stop=(kk == 1))
                    return mm

                def head_values(h, bank, pt):
                    for half in range(2):
                        for j in range(MM):
                            mm = pe.matmul(ps[:, bank + half, :],
                                           xv[:, j, h * X_DIM + half * P:h * X_DIM + (half + 1) * P], pt[:, j, :],
                                           start=(j == 0), stop=(j == MM - 1))
                    return mm

                attention("x", l, items_x, lambda i: MM, score, head_values, ("xo", l, 0))
                for c in range(2):
                    dense("xo", l, c, ah, al)

            def gather():
                for half in range(2):
                    for m in range(TM):
                        for i, a in enumerate((xnh, xnl)):
                            mm = pe.matmul(ps[:, half, :], oh[:, m, :], a[:, m, 512 * half:512 * (half + 1)],
                                           start=(m == 0 and i == 0), stop=(m == TM - 1 and i == 1))
                return mm

            def slots_T():
                for e in range(2):
                    for half in range(2):
                        for m in range(TM):
                            pe.matmul(ps[half * SLOTS:(half + 1) * SLOTS, 7, e:e + 1],
                                      oh[:, m, e * SLOTS:(e + 1) * SLOTS].bitcast(F32), te[:, e, m, 1:2],
                                      start=(m == 0), stop=(m == TM - 1))
                for m in range(TM):
                    mm = pe.transpose(ps[:, 3, m * P:(m + 1) * P], oh[:, m, :].bitcast(F32), ident[:, :])
                return mm

            def tokens_T():
                for k in range(KD):
                    mm = pe.transpose(ps[:, k // 4, (k % 4) * P:(k % 4 + 1) * P], rows[:, k * P:(k + 1) * P], ident[:, :])
                return mm

            def mix(m):
                b = 0 if m % 2 == 0 else 5
                for half in range(2):
                    for i, a in enumerate((yh, yl)):
                        mm = pe.matmul(ps[:, b + half, :], selT[:, m * P:(m + 1) * P],
                                       a[:, 512 * half:512 * (half + 1)], start=(i == 0), stop=(i == 1))
                return mm

            def gate_up(u0, p, full, used, halfway=None):
                for k in range(KD):
                    if halfway and k >= KD - TM:
                        halfway(k - (KD - TM))
                    if k % 4 == 0:
                        full(k // 2)
                        full(k // 2 + 1)
                    for half in range(2):
                        w = slot(u0 + 2 * (k // 4) + half, 512)
                        mm = pe.matmul(ps[half * SLOTS:(half + 1) * SLOTS, 2, :],
                                       xg[:, k, p * SLOTS:(p + 1) * SLOTS], w[:, k % 4, :],
                                       start=(k == 0), stop=(k == KD - 1))
                        if k % 4 == 3 and used and k < KD - 1:
                            mm.then_inc(expert_used, 1)
                        if k == KD - 1 and half == 0 and used:
                            mm.then_inc(expert_used, 1)
                return mm

            def hidden_T():
                for k in range(KF):
                    mm = pe.transpose(ps[:, 4, k * P:(k + 1) * P], hh[:, k * P:(k + 1) * P],
                                      ident[:, :])
                return mm

            def down(u0, full, used):
                for k in range(KF):
                    if k % 2 == 0:
                        full(4 + k // 2)
                    w = slot(u0 + 4 + k // 2, 1024)
                    for half in range(2):
                        mm = pe.matmul(ps[half * SLOTS:(half + 1) * SLOTS, 5, :], hT[:, k, :],
                                       w[:, k % 2, 512 * half:512 * (half + 1)], start=(k == 0), stop=(k == KF - 1))
                    if k == 1 and used:
                        mm.then_inc(expert_used, 1)
                return mm

            def experts(l):
                u0 = PLAN["moe", l][0]
                e0 = EXPERTS * l
                all_taken(pe, ("wsT", l + 1, 0))

                q0 = PAIRS * l

                def do_mix(q, m):
                    if m == 0:
                        pe.wait_ge(S["y_split"], q * 2 + (e0 + 2))
                        pe.wait_ge(S["info_ready"], q + (q0 + 1))
                    if m:
                        after(pe, S["y_added"], q * 4 + (4 * q0 + m - 1))
                    mix(m).then_inc(S["mixed"], 1)

                def do_gather(q):
                    pe.wait_ge(S["oh_ready"], q + (q0 + 1))
                    after(pe, S["y_added"], q * 4 + (4 * q0 - 5))
                    gather().then_inc(S["x_gathered"], 1)

                def do_slots_T(q):
                    pe.wait_ge(S["rows_ready"], q + (q0 + 1))
                    tokens_T().then_inc(S["rows_T"], 1)
                    after(pe, S["info_ready"], q + q0)
                    slots_T().then_inc(S["slots_done"], 1)

                def expert(e, p, q, first=False, last=False):
                    def full(j):
                        pe.wait_ge(ring_full[(u0 + j) % RING], (e + ((u0 + j) // RING + 1)) * 16)
                    if p == 0:
                        pe.wait_ge(S["xg_ready"], q + (q0 + 1))
                    halfway = (lambda m: do_mix(q - 1, m)) if p == 0 and not first else None
                    gate_up(u0, p, full, True, halfway).then_inc(S["gu_done"], 1)
                    if not last:
                        if p == 0:
                            do_gather(q + 1)
                        else:
                            do_slots_T(q + 1)
                    pe.wait_ge(S["h_ready"], e + (e0 + 1))
                    after(pe, S["hT_ready"], e + e0)
                    hidden_T().then_inc(S["hT_done"], 1)
                    pe.wait_ge(S["hT_ready"], e + (e0 + 1))
                    after(pe, S["yw_ready"], e + e0)
                    down(u0, full, True).then_inc(S["y_done"], 1)

                pe.wait_ge(S["xn_lo"], l + 1)
                do_gather(0)
                do_slots_T(0)
                expert(0, 0, 0, first=True)
                expert(1, 1, 0)
                with pe.Fori(1, PAIRS - 1) as i:
                    for p in range(2):
                        expert(i * 2 + p, p, i)
                expert(EXPERTS - 2, 0, PAIRS - 1, last=True)
                expert(EXPERTS - 1, 1, PAIRS - 1, last=True)
                for m in range(TM):
                    do_mix(PAIRS - 1, m)
                pe.wait_ge(S["y_added"], TM * PAIRS * (l + 1))
                n = pe.value_load(mosti[0:1, 0:1], min_val=0, max_val=T)
                with pe.If(n > SLOTS):
                    with pe.Fori(1, PASSES) as c:
                        with pe.If(n > c * SLOTS):
                            with pe.Fori(0, PAIRS) as e:
                                at_ = lambda k: c * (OVER * PAIRS) + e * OVER + (1 - OVER * PAIRS + k)
                                pe.wait_ge(over_step[l], at_(3))
                                gather().then_inc(over_step[l], 1)
                                pe.wait_ge(over_step[l], at_(5))
                                tokens_T()
                                slots_T().then_inc(over_step[l], 1)
                                for p in range(2):
                                    pe.wait_ge(over_step[l], at_(9 + 9 * p))
                                    pe.wait_ge(over_full[l], c * (96 * EXPERTS) + e * 192 + (96 * (p + 1) - 96 * EXPERTS))
                                    gate_up(u0, p, lambda j: None, False).then_inc(over_step[l], 1)
                                    pe.wait_ge(over_step[l], at_(12 + 9 * p))
                                    hidden_T().then_inc(over_step[l], 1)
                                    pe.wait_ge(over_step[l], at_(14 + 9 * p))
                                    down(u0, lambda j: None, False).then_inc(over_step[l], 1)
                                for m in range(TM):
                                    pe.wait_ge(over_step[l], at_(27 + 2 * m))
                                    mix(m).then_inc(over_step[l], 1)
                            pe.wait_ge(over_step[l], c * (OVER * PAIRS) + 1)
                            settle(pe)
                        pe.nop()
                pe.nop()

            def position_weights(l):
                b = begin(("wsT", l, 0))
                pe.wait_ge(S["ws_masked"], 1)
                for g in range(C_GROUPS):
                    mm = pe.transpose(ps[:, b + g // 4, (g % 4) * P:(g % 4 + 1) * P], wsn[:, g, :], ident[:, :])
                mm.then_inc(acc_done, 1)

            for l in range(LAYERS):
                if l % 2:
                    position_weights(l)
                norm_T("nmix", l, range(TM))
                split_written("nmix", l, TM)
                fox(l) if l % 2 == 0 else gmlp(l)
                cross(l)
                norm_T("nffn", l, range(TM))
                split_written("nffn", l, TM)
                thin("route", l, l + 1)
                wait_taken(pe, ("route", l, 0))
                b = begin(("logits", l, 0))
                for m in range(TM):
                    mm = pe.transpose(ps[:, b, m * 64:m * 64 + 36], lgT[:, m * P:(m + 1) * P], ident[0:36, 0:36])
                mm.then_inc(acc_done, 1)
                b = begin(("rank", l, 0))
                pe.wait_ge(S["cnt_ready"], l + 1)
                flat = cnt[:, :, :].rearrange("p m e -> p (m e)")
                pe.matmul(ps[:, b, 0:TM * EXPERTS], before[:, :], flat, start=True, stop=False)
                for m in range(1, TM):
                    pe.matmul(ps[:, b, m * EXPERTS:TM * EXPERTS], ones[:, :], flat[:, 0:(TM - m) * EXPERTS],
                              start=False, stop=(m == TM - 1))
                for m in range(TM):
                    mm = pe.matmul(ps[:, b, TM * EXPERTS:(TM + 1) * EXPERTS], ones[:, :], cnt[:, m, :],
                                   start=(m == 0), stop=(m == TM - 1))
                mm.then_inc(acc_done, 1)
                experts(l)

        @block.scalar
        def _(act):
            pos = [0]
            links = [0]

            def link(ins):
                links[0] += 1
                ins.then_inc(achain, 1)
                act.wait_ge(achain, links[0])

            def split(key, c, between=None):
                first = first_step(*key, c)
                for s in sorted(between or {}):
                    pos[0] = split_hi(act, pos[0], first + s)
                    between[s]()
                pos[0] = split_hi(act, pos[0], first + 8)

            def split_next():
                pos[0] = split_hi(act, pos[0], min(pos[0] + STAGE, N_STEPS))

            nsq = [0]

            def tile_square(src, m, throwaway):
                after(act, squares, nsq[0])
                nsq[0] += 1
                act.activation(throwaway[:, :], src[:, m, :], ACT.Square, scale=float(D) ** -0.5,
                               accum_out=mean[:, m:m + 1]).then_inc(squares, 1)

            def x_square(event, m):
                act.wait_ge(res_added, TM * event + m + 1)
                tile_square(x, m, junk)

            def tile_hi(name, dst, m, kts, k0=0):
                b = round_done(act, name)
                src = ps[:, b:b + -(-kts // 4), :].rearrange("p a (k n) -> p (a k) n", n=P)
                act.activation(dst[:, k0:k0 + kts, m * P:(m + 1) * P], src, ACT.Copy).then_inc(hi_ready, 1)

            def norm(kind, l, square):
                for m in range(3):
                    square(m)
                tile_hi((kind, l, 0), ah, 0, KD)
                square(3)
                for m in range(1, TM):
                    tile_hi((kind, l, m), ah, m, KD)

            def mem_squares(l):
                act.wait_ge(S["mem_loaded"], 16 * (l + 1))
                for m in range(MM):
                    tile_square(mem, m, mem_junk if l % 2 == 0 else junk)

            sqs = [0]

            def head_squares(name, tiles, dim):
                b = round_done(act, name)
                for m in range(tiles):
                    after(act, sq_used, sqs[0] - 1)
                    act.activation(sq[:, sqs[0] % 2, :], ps[:, b + m, :], ACT.Square,
                                   scale=float(dim) ** -0.5).then_inc(sq_ready, 1)
                    sqs[0] += 1

            def copy_out(name, dst, tiles, func=ACT.Copy, bias=None):
                b = round_done(act, name)
                for m in tiles:
                    kw = {} if bias is None else dict(bias=bias(m))
                    ins = act.activation(dst(m), ps[:, b + m, :], func, **kw)
                    if m == tiles[-1] and m == (MM if name[0] == "kv" else TM) - 1:
                        ins.then_inc(took(name), 1)

            def attention(kind, l, items, nk_of, hooks):
                n0, g0 = ATT0[kind, l], GROUP0[kind, l]
                o_banks, o_buffers, heads = SHAPE[kind]
                h0 = HEAD0[kind, l]

                def exps(n):
                    h, i = items[n]
                    w = nk_of(i) * P
                    act.wait_ge(S["mx_done"], n0 + n + 1)
                    if n >= 2:
                        act.wait_ge(S["pt_done"], n0 + n - 1)
                    act.activation(prob[:, n % 2, 0:w], ps[:, n % SCORES, 0:w], ACT.Exp, bias=nmax[:, n:n + 1],
                                   accum_out=rsum[:, n:n + 1]).then_inc(S["p_done"], 1)

                def copies(n):
                    h, i = items[n]
                    act.wait_ge(S["pt_done"], n0 + n + 1)
                    if h >= 2:
                        act.wait_ge(S["o_done"], h0 + h - 1)
                    act.activation(PT[kind][h % 2][:, 0:nk_of(i), i * P:(i + 1) * P],
                                   ps[:, T_BANK + n % 2, 0:nk_of(i) * P].rearrange("p (j n) -> p j n", n=P),
                                   ACT.Copy).then_inc(S["pt_copied"], 1)

                def output_hi(g):
                    act.wait_ge(S["o_done"], h0 + heads * (g + 1))
                    b = O_BANK + o_banks * (g % o_buffers)
                    act.activation(ah[:, o_banks * g:o_banks * (g + 1), :], ps[:, b:b + o_banks, :],
                                   ACT.Copy).then_inc(S["o_hi"], 1)

                exps(0)
                for n in range(len(items)):
                    if n + 1 < len(items):
                        exps(n + 1)
                    copies(n)
                    if n in hooks:
                        hooks[n]()
                    if n % (TM * heads) == 1 and n > 1:
                        output_hi(n // (TM * heads) - 1)
                output_hi(len(items) // TM // heads - 1)

            def fox(l):
                split(("in", l), 0)
                act.wait_ge(consts_ready, 2)
                act.wait_ge(S["small_loaded0"], 16)
                act.activation(thin_view(whs)[:, :, 0:A_HEADS], wsmall[:, :, 0:A_HEADS], ACT.Copy)\
                   .then_inc(S["small_hi"], 1)

                def squares0():
                    act.wait_ge(S["small_lo"], 1)
                    head_squares(("in", l, 0), TM, A_DIM)
                split(("in", l), 1, {3: squares0})
                split(("in", l), 2, {3: lambda: head_squares(("in", l, 1), TM, A_DIM)})
                split(("in", l), 3, {3: lambda: copy_out(("in", l, 2), lambda m: v0[:, m, :], range(TM))})
                act.wait_ge(S["f_z"], 2)
                act.activation(ef[:, :], ef[:, :], ACT.Exp).then_inc(S["f_e"], 1)
                act.activation(spl[:, :], spl[:, :], ACT.Exp).then_inc(S["f_e"], 1)
                act.wait_ge(S["f_e"], 2)
                act.activation(ef[:, :], ef[:, :], ACT.Ln, bias=onecol[0:A_HEADS, :]).then_inc(S["f_ln"], 1)
                act.activation(spl[:, :], spl[:, :], ACT.Ln, bias=onecol[:, :]).then_inc(S["f_ln"], 1)
                split(("in", l), 4, {3: lambda: copy_out(("in", l, 3), lambda m: xbT[:, m, :], range(4))})
                split_next()
                copy_out(("in", l, 4), lambda m: gbT[:, m, :], range(4), ACT.Gelu_apprx_tanh)
                act.wait_ge(S["negc_ready"], 1)
                act.dma_start(kT[A_DIM:A_DIM + 1, :, :], negc[:, :]).then_inc(S["c_row"], 16)
                for r in range(2):
                    b = round_done(act, ("qT", l, r))
                    for j in range(4):
                        ins = act.activation(qT[0:A_DIM, 4 * r + j, :], ps[0:A_DIM, b + j, :], ACT.Copy, scale=qg[:, :])
                    ins.then_inc(took(("qT", l, r)), 1)
                for g, (dst, bias) in enumerate(((xbT, bab), (iT, bxb))):
                    b = round_done(act, ("rg", l, g))
                    if g == 1:
                        wait_taken(act, ("qT", l, 1))
                    for m in range(4):
                        ins = act.activation(dst[:, m, :], ps[:, b + m, :], ACT.Sigmoid, bias=bias[:, m:m + 1])
                    ins.then_inc(took(("rg", l, g)), 1)

                def decay(m):
                    def run():
                        act.wait_ge(S["rg_l"], m + 1)
                        if m >= 2:
                            act.wait_ge(S["rg_var"], m - 1)
                        act.activation(aT[:, m, :], xbT[:, m, :], ACT.Exp)
                        act.activation(tanhs[:, m % 2, :], xbT[:, m, :], ACT.Tanh, scale=-1.0).then_inc(S["rg_exp"], 1)
                    return run

                def roots():
                    act.wait_ge(S["rg_var"], 4)
                    for m in range(4):
                        act.activation(xbT[:, m, :], xbT[:, m, :], ACT.Sqrt).then_inc(S["rg_sqrt"], 1)

                def rec_his():
                    for m in range(4):
                        act.wait_ge(S["rec_ready"], m + 1)
                        act.activation(ah[:, 4 + m, :], gbT[:, m, :], ACT.Copy).then_inc(S["rec_hi"], 1)

                attention("a", l, items_a, lambda i: i + 1,
                          {2: decay(0), 5: decay(1), 8: decay(2), 11: decay(3), 16: roots})
                rec_his()
                split(("out", l), 0, {5: lambda: mem_squares(l)})
                split(("out", l), 1, {3 + m: (lambda m=m: tile_hi(("nmem", l, m), mh, m, KD)) for m in range(MM)})

            def gmlp(l):
                def v_part(c, m):
                    def run():
                        n = c * TM + m
                        act.wait_ge(S["v_pre"], n + 1)
                        link(act.activation(v1[:, m, c * 512:(c + 1) * 512], gt[:, n % 2, :], ACT.Gelu_apprx_tanh))
                        act.activation(vjunk[:, :], v1[:, m, c * 512:(c + 1) * 512], ACT.Square,
                                       accum_out=ss[:, 4 * m + c:4 * m + c + 1]).then_inc(S["v_out"], 1)
                    return run

                def u_part(c, m):
                    return lambda: copy_out(("cin", l, c), lambda m: uT[:, 4 * (c - 4) + m, :], [m], ACT.Gelu_apprx_tanh,
                                            lambda m: ub[:, 4 * (c - 4) + m:4 * (c - 4) + m + 1])

                split(("cin", l), 0)
                for c in range(1, 4):
                    split(("cin", l), c, {3 + m: v_part(c - 1, m) for m in range(TM)})
                split_next()
                for m in range(TM):
                    v_part(3, m)()
                split(("cin", l), 4)
                for c in range(5, 8):
                    split(("cin", l), c, {3 + m: u_part(c - 1, m) for m in range(4)})
                split_next()
                for m in range(4):
                    u_part(7, m)()
                mem_squares(l)
                for kt in range(16):
                    act.wait_ge(S["gt_ready"], kt + 1)
                    act.activation(gh[:, kt, :], gt[:, kt % 2, :], ACT.Copy).then_inc(S["gt_hi"], 1)
                for c in range(4):
                    split(("cout", l), c, {} if c != 1 else
                          {3 + m: (lambda m=m: tile_hi(("nmem", l, m), mh, m, KD)) for m in range(MM)})

            def cross(l):
                split(("kv", l), 0, {3 + m: (lambda m=m: x_square(3 * l, m)) for m in range(TM)})
                split(("kv", l), 1, {4: lambda: head_squares(("kv", l, 0), MM, X_DIM)})
                split(("kv", l), 2, {4: lambda: head_squares(("kv", l, 1), MM, X_DIM)})
                split_next()
                copy_out(("kv", l, 2), lambda m: xv[:, m, 0:512], range(MM))
                for m in range(TM):
                    tile_hi(("ncross", l, m), ah, m, KD)
                split(("xq", l), 0)
                split(("xq", l), 1, {3: lambda: head_squares(("xq", l, 0), TM, X_DIM)})
                split(("kv", l), 3, {3: lambda: head_squares(("xq", l, 1), TM, X_DIM)})
                split_next()
                copy_out(("kv", l, 3), lambda m: xv[:, m, 512:1024], range(MM))
                for r in range(2):
                    b = round_done(act, ("xqT", l, r))
                    for j in range(4):
                        ins = act.activation(xqT[:, 4 * r + j, :], ps[:, b + j, :], ACT.Copy,
                                             scale=xqg[:, l, j % 2:j % 2 + 1])
                    ins.then_inc(took(("xqT", l, r)), 1)
                attention("x", l, items_x, lambda i: MM, {})
                split(("xo", l), 0)
                split(("xo", l), 1)

            def silu():
                return act.activation(sg[SLOTS:P, :], ps[0:SLOTS, 2, :], ACT.Silu)

            def hidden_copy():
                return act.activation(hT[:, :, :], ps[:, 4, :].rearrange("p (k n) -> p k n", n=P)[:, :, 0:SLOTS], ACT.Copy)

            def weigh(p):
                for half in range(2):
                    q = slice(half * SLOTS, (half + 1) * SLOTS)
                    ins = act.activation(yw[p * SLOTS:(p + 1) * SLOTS, 512 * half:512 * (half + 1)], ps[q, 5, :],
                                         ACT.Copy, scale=wcol[q, p, :])
                return ins

            def results_hi(p):
                return act.activation(yh[p * SLOTS:(p + 1) * SLOTS, :], yw[p * SLOTS:(p + 1) * SLOTS, :], ACT.Copy)

            def rows_copy():
                return act.activation(rows[:, :], ps[:, 0:2, :].rearrange("p a n -> p (a n)"), ACT.Copy)

            def experts(l):
                e0, q0 = EXPERTS * l, PAIRS * l
                for m in range(TM):
                    act.activation(xnh[:, m, :], xn[:, m, :], ACT.Copy).then_inc(S["xn_hi"], 1)
                b = round_done(act, ("route", l, 0))
                act.activation(lgT[:, :], ps[0:GROUPS + EXPERTS, b, :], ACT.Copy).then_inc(took(("route", l, 0)), 1)
                act.wait_ge(S["g_sub"], l + 1)
                act.activation(gee[:, :, :], ge[:, :, :], ACT.Exp).then_inc(S["g_exp"], 1)
                act.wait_ge(S["e_sub"], l + 1)
                act.activation(ex[:, :, :], ed[:, :, :], ACT.Exp).then_inc(S["e_exp"], 1)

                def do_rows(q):
                    act.wait_ge(S["x_gathered"], q + (q0 + 1))
                    after(act, S["rows_T"], q + q0)
                    rows_copy().then_inc(S["rows_ready"], 1)

                def expert(e, p, q, last=False):
                    act.wait_ge(S["gu_done"], e + (e0 + 1))
                    after(act, S["h_ready"], e + e0)
                    silu().then_inc(S["silu_done"], 1)
                    act.wait_ge(S["hT_done"], e + (e0 + 1))
                    after(act, S["y_done"], e + e0)
                    hidden_copy().then_inc(S["hT_ready"], 1)
                    if p == 0 and not last:
                        do_rows(q + 1)
                    act.wait_ge(S["y_done"], e + (e0 + 1))
                    act.wait_ge(S["info_ready"], q + (q0 + 1))
                    after(act, S["y_split"], e + (e0 - 1))
                    weigh(p).then_inc(S["yw_ready"], 1)
                    act.wait_ge(S["yw_ready"], e + (e0 + 1))
                    after(act, S["mixed"], q * 4 + 4 * q0)
                    results_hi(p).then_inc(S["yh_ready"], 1)

                do_rows(0)
                expert(0, 0, 0)
                expert(1, 1, 0)
                with act.Fori(1, PAIRS - 1) as i:
                    for p in range(2):
                        expert(i * 2 + p, p, i)
                for p in range(2):
                    expert(EXPERTS - 2 + p, p, PAIRS - 1, last=True)
                n = act.value_load(mosti[0:1, 0:1], min_val=0, max_val=T)
                with act.If(n > SLOTS):
                    with act.Fori(1, PASSES) as c:
                        with act.If(n > c * SLOTS):
                            with act.Fori(0, PAIRS) as e:
                                at_ = lambda k: c * (OVER * PAIRS) + e * OVER + (1 - OVER * PAIRS + k)
                                act.wait_ge(over_step[l], at_(4))
                                rows_copy().then_inc(over_step[l], 1)
                                for p in range(2):
                                    act.wait_ge(over_step[l], at_(10 + 9 * p))
                                    silu().then_inc(over_step[l], 1)
                                    act.wait_ge(over_step[l], at_(13 + 9 * p))
                                    hidden_copy().then_inc(over_step[l], 1)
                                    act.wait_ge(over_step[l], at_(15 + 9 * p))
                                    weigh(p).then_inc(over_step[l], 1)
                                    act.wait_ge(over_step[l], at_(16 + 9 * p))
                                    results_hi(p).then_inc(over_step[l], 1)
                            act.wait_ge(over_step[l], c * (OVER * PAIRS) + 1)
                            settle(act)
                        act.nop()
                act.nop()

            for l in range(LAYERS):
                def x_tile(m):
                    if l == 0:
                        act.wait_ge(x_loaded[m], 16)
                        tile_square(x, m, junk)
                    else:
                        x_square(3 * l - 1, m)
                if l % 2:
                    b = round_done(act, ("wsT", l, 0))
                    act.activation(wsT[:, :, :], ps[:, b:b + 2, :].rearrange("p a (g n) -> p (a g) n", n=P),
                                   ACT.Copy).then_inc(took(("wsT", l, 0)), 1)
                norm("nmix", l, x_tile)
                fox(l) if l % 2 == 0 else gmlp(l)
                cross(l)
                act.wait_ge(S[f"small_loaded{l + 1}"], 32)
                act.activation(thin_view(whs), wsmall[:, :, :], ACT.Copy).then_inc(S["small_hi"], 1)
                norm("nffn", l, lambda m: x_square(3 * l + 1, m))
                experts(l)
            for m in range(TM):
                act.wait_ge(res_added, TM * (3 * LAYERS - 1) + m + 1)
                act.dma_start(x_out[:, m, :], x[:, m, :]).then_inc(out_stored, 16)
            act.wait_ge(out_stored, 16 * TM)

        @block.vector
        def _(dve):
            pos = [0]
            links = [0]

            def link(ins):
                links[0] += 1
                ins.then_inc(chain, 1)
                dve.wait_ge(chain, links[0])

            def split(key, c, between=None):
                first = first_step(*key, c)
                for s in sorted(between or {}):
                    pos[0] = split_lo(dve, pos[0], first + s)
                    between[s]()
                pos[0] = split_lo(dve, pos[0], first + 8)

            def split_next():
                pos[0] = split_lo(dve, pos[0], min(pos[0] + STAGE, N_STEPS))

            rstds, sqs = [0], [0]

            def scale(kind, l, m, src):
                n = NORMS.index((kind[1:], l))
                if m == 0:
                    dve.wait_ge(gain_loaded[n % 2], 16 * (n // 2 + 1))
                tiles = MM if kind == "nmem" else TM
                dve.wait_ge(norm_rstd, nats_upto(kind[1:], l) - tiles + m + 1)
                if kind == "ncross" or kind == "nmix" and m >= 2:
                    round_done(dve, (kind, l, m - 2) if m >= 2 else ("nmem", l, m))
                if (kind, m) == ("nmix", 1) and l % 2:
                    round_done(dve, ("wsT", l, 0))
                out_ = {"nffn": xn, "nmem": mem}.get(kind)
                dve.scalar_tensor_tensor(out=nat[:, m % 2, :] if out_ is None else out_[:, m, :], in0=src[:, m, :],
                                         scalar=rnorm[:, m:m + 1], in1=gain[:, n % 2, :],
                                         op0=ALU.mult, op1=ALU.mult).then_inc(nat_ready, 1)

            def norm(kind, l, feed=lambda m: None):
                feed(0)
                feed(1)
                scale(kind, l, 0, x)
                feed(2)
                scale(kind, l, 1, x)
                for m in range(TM):
                    tile_lo((kind, l, m), ah, al, m, KD)
                    if m == 0:
                        feed(3)
                    if m + 2 < TM:
                        scale(kind, l, m + 2, x)

            his = [0]

            def tile_lo(name, hi, lo, m, kts):
                his[0] += 1
                dve.wait_ge(hi_ready, his[0])
                b = 4 * (ROUND[name] % 2)
                src = ps[:, b:b + -(-kts // 4), :].rearrange("p a (k n) -> p (a k) n", n=P)
                dve.tensor_tensor(lo[:, 0:kts, m * P:(m + 1) * P], src,
                                  hi[:, 0:kts, m * P:(m + 1) * P].bitcast(F32), ALU.subtract).then_inc(took(name), 1)

            def head_means(name, tiles, nh, dim):
                for m in range(tiles):
                    dve.wait_ge(sq_ready, sqs[0] + 1)
                    sqs[0] += 1
                    dve.tensor_reduce(ss[:, m * nh:(m + 1) * nh],
                                      sq[:, (sqs[0] - 1) % 2, :].rearrange("p (h d) -> p h d", d=dim), AX.X, ALU.add)\
                       .then_inc(sq_used, 1)
                dve.wait_ge(sq_used, sqs[0])
                dve.engine_nop().then_inc(var_ready, 1)

            def head_scales(name, tiles, nh, dim, dst):
                rstds[0] += 1
                dve.wait_ge(rstd_ready, rstds[0])
                b = 4 * (ROUND[name] % 2)
                for m in range(tiles):
                    ins = dve.tensor_tensor(dst(m).rearrange("p (h d) -> p h d", d=dim),
                                            ps[:, b + m, :].rearrange("p (h d) -> p h d", d=dim),
                                            rstd[:, m * nh:(m + 1) * nh].unsqueeze(2).to_broadcast([P, nh, dim]), ALU.mult)
                ins.then_inc(took(name), 1)
                wait_taken(dve, name)
                dve.engine_nop().then_inc(heads_ready, 1)

            def residual(name, cols, last):
                b = round_done(dve, name)
                c = name[2]
                for m in range(TM):
                    xs = x[:, m, c * cols:(c + 1) * cols]
                    ins = dve.tensor_tensor(xs, ps[:, b + m, 0:cols], xs, ALU.add)
                    if last:
                        ins.then_inc(res_added, 1)
                if last:
                    dve.engine_nop().then_inc(took(name), 1)
                else:
                    ins.then_inc(took(name), 1)

            def attention(kind, l, items, nk_of, hooks):
                n0, g0 = ATT0[kind, l], GROUP0[kind, l]
                o_banks, o_buffers, heads = SHAPE[kind]

                def maxima(n):
                    w = nk_of(items[n][1]) * P
                    dve.wait_ge(S["s_done"], n0 + n + 1)
                    dve.tensor_reduce(nmax[:, n:n + 1], ps[:, n % SCORES, 0:w], AX.X, ALU.max, negate=True)\
                       .then_inc(S["mx_done"], 1)

                def normalise(n):
                    w = nk_of(items[n][1]) * P
                    dve.wait_ge(S["p_done"], n0 + n + 1)
                    link(dve.reciprocal(rinv[:, n:n + 1], rsum[:, n:n + 1]))
                    dve.tensor_scalar(prob[:, n % 2, 0:w], prob[:, n % 2, 0:w], rinv[:, n:n + 1], None,
                                      ALU.mult).then_inc(S["pn_done"], 1)

                def output_lo(g):
                    dve.wait_ge(S["o_hi"], g0 + g + 1)
                    b = O_BANK + o_banks * (g % o_buffers)
                    k = slice(o_banks * g, o_banks * (g + 1))
                    dve.tensor_tensor(al[:, k, :], ps[:, b:b + o_banks, :], ah[:, k, :].bitcast(F32),
                                      ALU.subtract).then_inc(S["o_copied"], 1)

                for n in range(SCORES - 1):
                    maxima(n)
                for n in range(len(items)):
                    normalise(n)
                    if n + SCORES - 1 < len(items):
                        maxima(n + SCORES - 1)
                    if n in hooks:
                        hooks[n]()
                    if n % (TM * heads) == 2 and n > 2:
                        output_lo(n // (TM * heads) - 1)
                output_lo(len(items) // TM // heads - 1)

            def fox(l):
                split(("in", l), 0)
                dve.wait_ge(S["small_hi"], 1)
                dve.tensor_tensor(thin_view(wls)[:, :, 0:A_HEADS], wsmall[:, :, 0:A_HEADS],
                                  thin_view(whs)[:, :, 0:A_HEADS].bitcast(F32), ALU.subtract).then_inc(S["small_lo"], 1)
                dve.wait_ge(params, 32)
                link(dve.tensor_scalar(qg[:, :], qg[:, :], float(A_DIM) ** -0.5, None, ALU.mult))
                link(dve.tensor_scalar(xqg[:, :, :], xqg[:, :, :], float(X_DIM) ** -0.5, None, ALU.mult))
                args = (TM, A_HEADS, A_DIM)
                split(("in", l), 1, {3: lambda: head_means(("in", l, 0), *args),
                                     6: lambda: head_scales(("in", l, 0), *args, lambda m: qn[:, m, :])})
                split(("in", l), 2, {3: lambda: head_means(("in", l, 1), *args),
                                     6: lambda: head_scales(("in", l, 1), *args, lambda m: kn[:, m, :])})
                split(("in", l), 3)
                b = round_done(dve, ("f", l, 0))
                dve.tensor_scalar(zf[:, :], ps[0:A_HEADS, b, :], fbias[:, :], None, ALU.add)\
                   .then_inc(took(("f", l, 0)), 1)
                wait_taken(dve, ("f", l, 0))
                for dst, src in ((ef[:, :], zf[:, :]), (spl[:, :], lam[:, :])):
                    link(dve.tensor_scalar(dst, src, -1.0, None, ALU.mult))
                    dve.tensor_tensor(dst, dst, src, ALU.min).then_inc(S["f_z"], 1)
                link(dve.tensor_scalar(zf[:, :], zf[:, :], 0.0, None, ALU.min))
                link(dve.tensor_scalar(lam2[:, :], lam[:, :], 0.0, None, ALU.min))
                dve.wait_ge(S["f_ln"], 2)
                link(dve.tensor_tensor(zf[:, :], zf[:, :], ef[:, :], ALU.subtract))
                dve.tensor_tensor_scan(negc[:, :], onecol[0:A_HEADS, :].to_broadcast([A_HEADS, T]), zf[:, :], 0.0,
                                       ALU.mult, ALU.subtract).then_inc(S["negc_ready"], 1)
                link(dve.tensor_tensor(spl[:, :], lam2[:, :], spl[:, :], ALU.subtract))
                link(dve.tensor_scalar(spl[:, :], spl[:, :], RG_C, None, ALU.mult))
                split(("in", l), 4)
                wait_taken(dve, ("in", l, 3))
                wait_taken(dve, ("nmix", l, TM - 1))
                for m in range(4):
                    link(dve.tensor_scalar(xcT[:, m, :], xbT[:, m, :], convw[:, m, CONV - 1:CONV], convb[:, m:m + 1],
                                           ALU.mult, ALU.add))
                    for k in range(CONV - 1):
                        s = CONV - 1 - k
                        ins = dve.scalar_tensor_tensor(out=xcT[:, m, s:T], in0=xbT[:, m, 0:T - s],
                                                       scalar=convw[:, m, k:k + 1], in1=xcT[:, m, s:T],
                                                       op0=ALU.mult, op1=ALU.add)
                        if m == 3 and k == CONV - 2:
                            ins.then_inc(S["xc_ready"], 1)
                        else:
                            link(ins)
                split_next()
                for r in range(2):
                    b = round_done(dve, ("kT", l, r))
                    ins = dve.tensor_scalar(kT[0:A_DIM, 4 * r:4 * r + 4, :], ps[0:A_DIM, b:b + 4, :], kg[:, :], None,
                                            ALU.mult)
                    ins.then_inc(took(("kT", l, r)), 1)
                wait_taken(dve, ("rg", l, 0))
                wait_taken(dve, ("rg", l, 1))
                for m in range(4):
                    dve.tensor_tensor(iT[:, m, :], iT[:, m, :], xcT[:, m, :], ALU.mult)
                    dve.tensor_scalar(xbT[:, m, :], xbT[:, m, :], spl[:, m:m + 1], None, ALU.mult).then_inc(S["rg_l"], 1)

                def mark(ins):
                    links[0] += 1
                    ins.then_inc(chain, 1)
                    return links[0]

                done = {}

                def a_squared(m):
                    dve.wait_ge(S["rg_exp"], m + 1)
                    done["a2", m] = mark(dve.tensor_tensor(xbT[:, m, :], aT[:, m, :], aT[:, m, :], ALU.mult))

                def variance(m):
                    dve.wait_ge(chain, done["a2", m])
                    dve.scalar_tensor_tensor(out=xbT[:, m, :], in0=xbT[:, m, :], scalar=1.0, in1=tanhs[:, m % 2, :],
                                             op0=ALU.add, op1=ALU.mult).then_inc(S["rg_var"], 1)

                def drive(m):
                    dve.wait_ge(S["rg_sqrt"], m + 1)
                    done["in", m] = mark(dve.tensor_tensor(iT[:, m, :], iT[:, m, :], xbT[:, m, :], ALU.mult))

                def scan(m):
                    dve.wait_ge(chain, done["in", m])
                    done["h", m] = mark(dve.tensor_tensor_scan(xbT[:, m, :], aT[:, m, :], iT[:, m, :], 0.0,
                                                               ALU.mult, ALU.add))

                def gate(m):
                    dve.wait_ge(chain, done["h", m])
                    dve.tensor_tensor(gbT[:, m, :], gbT[:, m, :], xbT[:, m, :], ALU.mult).then_inc(S["rec_ready"], 1)

                hooks = {}
                for m in range(4):
                    for j, step in enumerate((a_squared, variance)):
                        hooks[4 + 3 * m + j] = lambda step=step, m=m: step(m)
                    for j, step in enumerate((drive, scan, gate)):
                        hooks[18 + 3 * m + j] = lambda step=step, m=m: step(m)
                attention("a", l, items_a, lambda i: i + 1,
                          hooks)
                for m in range(4):
                    dve.wait_ge(S["rec_hi"], m + 1)
                    dve.tensor_tensor(al[:, 4 + m, :], gbT[:, m, :], ah[:, 4 + m, :].bitcast(F32),
                                      ALU.subtract).then_inc(S["rec_lo"], 1)
                split(("out", l), 0, {6: lambda: scale("nmem", l, 0, mem), 7: lambda: scale("nmem", l, 1, mem)})
                split(("out", l), 1, {3: lambda: (residual(("out", l, 0), 512, False),
                                                  tile_lo(("nmem", l, 0), mh, ml, 0, KD)),
                                      4: lambda: tile_lo(("nmem", l, 1), mh, ml, 1, KD)})

            def gmlp(l):
                def v_part(c, m):
                    def run():
                        n = c * TM + m
                        if n == 0:
                            dve.wait_ge(S["vbias_loaded"], 16)
                        b = round_done(dve, ("cin", l, c))
                        after(dve, S["v_out"], n - 1)
                        dve.tensor_tensor(gt[:, n % 2, :], ps[:, b + m, :], vbias[:, c * 512:(c + 1) * 512], ALU.add)\
                           .then_inc(S["v_pre"], 1)
                        if m == TM - 1:
                            dve.wait_ge(S["v_pre"], n + 1)
                            dve.engine_nop().then_inc(took(("cin", l, c)), 1)
                    return run

                split(("cin", l), 0)
                for c in range(1, 4):
                    split(("cin", l), c, {3 + m: v_part(c - 1, m) for m in range(TM)})
                split_next()
                for m in range(TM):
                    v_part(3, m)()
                split(("cin", l), 4)
                dve.wait_ge(S["v_out"], 16)
                link(dve.tensor_reduce(rinv[:, 0:TM], ss[:, 0:16].rearrange("p (m c) -> p m c", c=4), AX.X, ALU.add))
                dve.tensor_scalar(ss[:, 0:TM], rinv[:, 0:TM], 1.0 / C_W, None, ALU.mult).then_inc(var_ready, 1)
                rstds[0] += 1
                dve.wait_ge(rstd_ready, rstds[0])
                link(dve.tensor_copy(rx[:, :], rstd[:, 0:TM]))
                for c in range(5, 8):
                    split(("cin", l), c)
                    dve.tensor_scalar(v1[:, c - 5, :], v1[:, c - 5, :], rx[:, c - 5:c - 4], None, ALU.mult)\
                       .then_inc(S["v_scaled"], 1)
                split_next()
                dve.tensor_scalar(v1[:, 3, :], v1[:, 3, :], rx[:, 3:4], None, ALU.mult).then_inc(S["v_scaled"], 1)
                dve.wait_ge(S["bs_loaded"], 16)
                wait_taken(dve, ("cin", l, 7))
                dve.wait_ge(squares, nats_upto("mem", l))

                for kt in range(16):
                    name = ("mix", l, kt // 4)
                    b = round_done(dve, name)
                    after(dve, S["gt_lo"], kt - 1)
                    ins = dve.scalar_tensor_tensor(
                        out=gt[:, kt % 2, :].rearrange("p (n t) -> p n t", t=P),
                        in0=ps[:, b + kt % 4, :].rearrange("p (n t) -> p n t", t=P), scalar=vg[:, kt:kt + 1],
                        in1=bs[:, kt // 2, :].unsqueeze(1).to_broadcast([P, TM, P]), op0=ALU.mult, op1=ALU.add)
                    link(ins)
                    if kt % 4 == 3:
                        dve.engine_nop().then_inc(took(name), 1)
                    dve.tensor_tensor(gt[:, kt % 2, :], gt[:, kt % 2, :], uT[:, kt, :], ALU.mult).then_inc(S["gt_ready"], 1)
                    if kt == 7:
                        scale("nmem", l, 0, mem)
                        scale("nmem", l, 1, mem)
                split(("cout", l), 0)
                for c in range(1, 4):
                    between = {3: lambda c=c: residual(("cout", l, c - 1), 256, False)}
                    if c == 1:
                        between[3] = lambda: (residual(("cout", l, 0), 256, False),
                                              tile_lo(("nmem", l, 0), mh, ml, 0, KD))
                        between[4] = lambda: tile_lo(("nmem", l, 1), mh, ml, 1, KD)
                    split(("cout", l), c, between)

            def cross(l):
                last = ("out", l, 1, 512) if l % 2 == 0 else ("cout", l, 3, 256)
                args = (MM, 2, X_DIM)
                xkh = lambda c: lambda: head_scales(("kv", l, c), *args, lambda m: xkn[:, m, 512 * c:512 * (c + 1)])
                split(("kv", l), 0, {3: lambda: residual(last[:3], last[3], True)})
                split(("kv", l), 1, {2: lambda: scale("ncross", l, 0, x), 3: lambda: scale("ncross", l, 1, x),
                                     4: lambda: head_means(("kv", l, 0), *args), 6: xkh(0)})
                split(("kv", l), 2, {4: lambda: head_means(("kv", l, 1), *args), 6: xkh(1)})
                split_next()
                for m in range(TM):
                    tile_lo(("ncross", l, m), ah, al, m, KD)
                    if m + 2 < TM:
                        scale("ncross", l, m + 2, x)
                for r in range(2):
                    b = round_done(dve, ("xkT", l, r))
                    for j in range(4):
                        ins = dve.tensor_scalar(xkT[:, 4 * r + j, :], ps[:, b + j, 0:MEM], xkg[:, l, j % 2:j % 2 + 1],
                                                None, ALU.mult)
                    ins.then_inc(took(("xkT", l, r)), 1)
                args = (TM, 2, X_DIM)
                xqh = lambda c: lambda: head_scales(("xq", l, c), *args, lambda m: xqn[:, m, 512 * c:512 * (c + 1)])
                split(("xq", l), 0)
                split(("xq", l), 1, {3: lambda: head_means(("xq", l, 0), *args), 5: xqh(0)})
                split(("kv", l), 3, {3: lambda: head_means(("xq", l, 1), *args), 7: xqh(1)})
                split_next()
                attention("x", l, items_x, lambda i: MM, {})
                split(("xo", l), 0)
                split(("xo", l), 1, {3: lambda: residual(("xo", l, 0), 512, False)})
                residual(("xo", l, 1), 512, True)

            def route(l):
                dve.tensor_copy(iotac[:, :], iota[:, :])
                dve.memset(hh[:, :], 0.0)
                link(dve.memset(gpad[:, :, :], -3.0e38))
                b = round_done(dve, ("logits", l, 0))
                lv = ps[:, b, 0:TM * 64].rearrange("p (m n) -> p m n", n=64)[:, :, 0:36]
                dve.tensor_tensor(lg[:, :, :], lv, rbias[:, l, :].unsqueeze(1).to_broadcast([P, TM, 36]),
                                  ALU.add).then_inc(took(("logits", l, 0)), 1)
                wait_taken(dve, ("logits", l, 0))
                link(dve.tensor_copy(gpad[:, :, 0:GROUPS], lg[:, :, 0:GROUPS]))
                for m in range(TM):
                    ins = dve.max(gm8[:, m, :], gpad[:, m, :])
                link(ins)
                for m in range(TM):
                    ins = dve.max_index(gi8[:, m, :], gm8[:, m, :], gpad[:, m, :])
                link(ins)
                link(dve.tensor_copy(gif[:, :, :], gi8[:, :, 0:1]))
                dve.tensor_tensor(ge[:, :, :], lg[:, :, 0:GROUPS], gm8[:, :, 0:1].to_broadcast([P, TM, GROUPS]),
                                  ALU.subtract).then_inc(S["g_sub"], 1)
                link(dve.tensor_tensor(oh4[:, :, :], iota[:, 0:GROUPS].unsqueeze(1).to_broadcast([P, TM, GROUPS]),
                                       gif[:, :, :].to_broadcast([P, TM, GROUPS]), ALU.is_equal))
                link(dve.tensor_tensor(etmp[:, :, :, :],
                                       lg[:, :, GROUPS:36].rearrange("p m (g j) -> p m j g", g=GROUPS),
                                       oh4[:, :, :].unsqueeze(2).to_broadcast([P, TM, PER_GROUP, GROUPS]), ALU.mult))
                link(dve.tensor_reduce(esel[:, :, :], etmp[:, :, :, :], AX.X, ALU.add))
                for m in range(TM):
                    ins = dve.max(em8[:, m, :], esel[:, m, :])
                link(ins)
                for m in range(TM):
                    ins = dve.max_index(ei8[:, m, :], em8[:, m, :], esel[:, m, :])
                link(ins)
                dve.tensor_tensor(ed[:, :, :], em8[:, :, 1:2], em8[:, :, 0:1], ALU.subtract).then_inc(S["e_sub"], 1)
                link(dve.tensor_copy(eid[:, :, :], ei8[:, :, 0:2]))
                link(dve.scalar_tensor_tensor(out=eid[:, :, :], in0=gif[:, :, :].to_broadcast([P, TM, 2]),
                                              scalar=float(PER_GROUP), in1=eid[:, :, :], op0=ALU.mult, op1=ALU.add))
                ids = iota[:, 0:EXPERTS].unsqueeze(1).to_broadcast([P, TM, EXPERTS])
                link(dve.tensor_tensor(sel0[:, :, :], ids, eid[:, :, 0:1].to_broadcast([P, TM, EXPERTS]), ALU.is_equal))
                link(dve.tensor_tensor(sel1[:, :, :], ids, eid[:, :, 1:2].to_broadcast([P, TM, EXPERTS]), ALU.is_equal))
                dve.tensor_tensor(cnt[:, :, :], sel0[:, :, :], sel1[:, :, :], ALU.add).then_inc(S["cnt_ready"], 1)
                dve.wait_ge(S["g_exp"], l + 1)
                link(dve.tensor_reduce(gw[:, :, 0], gee[:, :, :], AX.X, ALU.add))
                link(dve.reciprocal(gw[:, :, :], gw[:, :, :]))
                dve.wait_ge(S["e_exp"], l + 1)
                link(dve.tensor_scalar(w01[:, :, 0:1], ex[:, :, :], 1.0, None, ALU.add))
                link(dve.reciprocal(w01[:, :, 0:1], w01[:, :, 0:1]))
                link(dve.tensor_tensor(w01[:, :, 0:1], w01[:, :, 0:1], gw[:, :, :], ALU.mult))
                link(dve.tensor_tensor(w01[:, :, 1:2], w01[:, :, 0:1], ex[:, :, :], ALU.mult))
                full = [P, TM, EXPERTS]
                link(dve.tensor_tensor(rt1[:, :, :], sel0[:, :, :], w01[:, :, 0:1].to_broadcast(full), ALU.mult))
                link(dve.tensor_tensor(rt2[:, :, :], sel1[:, :, :], w01[:, :, 1:2].to_broadcast(full), ALU.mult))
                tb = lambda j: tab[:, :, :, j].rearrange("p e m -> p m e")
                link(dve.tensor_tensor(tb(1), rt1[:, :, :], rt2[:, :, :], ALU.add))
                b = round_done(dve, ("rank", l, 0))
                link(dve.scalar_tensor_tensor(out=rt1[:, :, :], 
                                              in0=ps[:, b, 0:TM * EXPERTS].rearrange("p (m e) -> p m e", e=EXPERTS),
                                              scalar=1.0, in1=cnt[:, :, :], op0=ALU.add, op1=ALU.mult))
                link(dve.tensor_scalar(tb(0), rt1[:, :, :], -1.0, None, ALU.add))
                link(dve.tensor_reduce(most[:, :], ps[:, b, TM * EXPERTS:(TM + 1) * EXPERTS], AX.X, ALU.max))
                link(dve.tensor_copy(mosti[:, :], most[:, :]))
                dve.engine_nop().then_inc(took(("rank", l, 0)), 1)
                dve.engine_nop().then_inc(over_step[l], 1)
                dve.engine_nop().then_inc(S["tab_ready"], 1)

            def columns(src, q, stage):
                stage(dve.tensor_copy(te[:, :, :, :], tab[:, bass.ds(q * 2, 2), :, :]))
                for e in range(2):
                    ins = dve.tensor_tensor(oh[:, :, e * SLOTS:(e + 1) * SLOTS],
                                            src[:, :].unsqueeze(1).to_broadcast([P, TM, SLOTS]),
                                            te[:, e, :, 0:1].to_broadcast([P, TM, SLOTS]), ALU.is_equal)
                    if e == 0:
                        stage(ins)
                return ins

            def tokens_out():
                return dve.tensor_copy(xg[:, :, :].rearrange("p (a k) n -> p a (k n)", a=2), ps[:, 0:2, :])

            def info_out():
                return (dve.tensor_copy(wcol[:, :, 0], ps[:, 7, 0:2]), dve.tensor_copy(selT[:, :], ps[:, 3, :]))

            def hidden():
                return dve.tensor_tensor(hh[0:SLOTS, :], ps[SLOTS:P, 2, :], sg[SLOTS:P, :], ALU.mult)

            def results_lo(p):
                q = slice(p * SLOTS, (p + 1) * SLOTS)
                return dve.tensor_tensor(yl[q, :], yw[q, :], yh[q, :].bitcast(F32), ALU.subtract)

            def add(m):
                b = 0 if m % 2 == 0 else 5
                return dve.tensor_tensor(x[:, m, :], ps[:, b:b + 2, :].rearrange("p a n -> p (a n)"), x[:, m, :], ALU.add)

            def xn_los(l):
                all_taken(dve, ("route", l, 0))
                for m in range(TM):
                    dve.wait_ge(S["xn_hi"], TM * l + m + 1)
                    ins = dve.tensor_tensor(xnl[:, m, :], xn[:, m, :], xnh[:, m, :].bitcast(F32), ALU.subtract)
                ins.then_inc(S["xn_lo"], 1)

            def experts(l):
                e0, q0 = EXPERTS * l, PAIRS * l

                def prepare(q):
                    after(dve, S["slots_done"], q + q0)
                    n = [0]

                    def stage(ins):
                        n[0] += 1
                        ins.then_inc(dve_loop, 1)
                        dve.wait_ge(dve_loop, q * 2 + (2 * q0 + n[0]))
                    columns(iota, q, stage).then_inc(S["oh_ready"], 1)

                def take(q):
                    dve.wait_ge(S["rows_T"], q + (q0 + 1))
                    after(dve, S["gu_done"], q * 2 + e0)
                    tokens_out().then_inc(S["xg_ready"], 1)

                def info(q):
                    dve.wait_ge(S["slots_done"], q + (q0 + 1))
                    after(dve, S["yw_ready"], q * 2 + e0)
                    after(dve, S["mixed"], q * 4 + 4 * q0)
                    info_out()[1].then_inc(S["info_ready"], 1)

                def hide(e):
                    dve.wait_ge(S["silu_done"], e + (e0 + 1))
                    after(dve, S["hT_done"], e + e0)
                    hidden().then_inc(S["h_ready"], 1)

                def lo(e, p):
                    dve.wait_ge(S["yh_ready"], e + (e0 + 1))
                    results_lo(p).then_inc(S["y_split"], 1)

                def adds(q):
                    for m in range(TM):
                        dve.wait_ge(S["mixed"], q * 4 + (4 * q0 + m + 1))
                        add(m).then_inc(S["y_added"], 1)

                def pair(q, last=False):
                    hide(q * 2)
                    info(q)
                    lo(q * 2, 0)
                    hide(q * 2 + 1)
                    if not last:
                        take(q + 1)

                prepare(0)
                take(0)
                prepare(1)
                pair(0)
                with dve.Fori(1, PAIRS - 1) as i:
                    prepare(i + 1)
                    lo(i * 2 - 1, 1)
                    adds(i - 1)
                    pair(i)
                lo(EXPERTS - 3, 1)
                adds(PAIRS - 2)
                pair(PAIRS - 1, last=True)
                lo(EXPERTS - 1, 1)
                adds(PAIRS - 1)
                n = dve.value_load(mosti[0:1, 0:1], min_val=0, max_val=T)
                with dve.If(n > SLOTS):
                    with dve.Fori(1, PASSES) as c:
                        with dve.If(n > c * SLOTS):
                            dve.tensor_scalar(iotac[:, :], iotac[:, :], float(SLOTS), None, ALU.add)
                            dve.drain()
                            with dve.Fori(0, PAIRS) as e:
                                at_ = lambda k: c * (OVER * PAIRS) + e * OVER + (1 - OVER * PAIRS + k)
                                dve.wait_ge(over_step[l], at_(0))
                                n_ = [0]

                                def stage(ins):
                                    n_[0] += 1
                                    ins.then_inc(over_step[l], 1)
                                    dve.wait_ge(over_step[l], at_(n_[0]))
                                columns(iotac, e, stage).then_inc(over_step[l], 1)
                                dve.wait_ge(over_step[l], at_(6))
                                tokens_out().then_inc(over_step[l], 1)
                                for ins in info_out():
                                    ins.then_inc(over_step[l], 1)
                                for p in range(2):
                                    dve.wait_ge(over_step[l], at_(11 + 9 * p))
                                    hidden().then_inc(over_step[l], 1)
                                    dve.wait_ge(over_step[l], at_(17 + 9 * p))
                                    results_lo(p).then_inc(over_step[l], 1)
                                for m in range(TM):
                                    dve.wait_ge(over_step[l], at_(28 + 2 * m))
                                    add(m).then_inc(over_step[l], 1)
                            dve.wait_ge(over_step[l], c * (OVER * PAIRS) + 1)
                            settle(dve)
                        dve.nop()
                dve.nop()
                dve.wait_ge(S["y_added"], TM * PAIRS * (l + 1))
                dve.engine_nop().then_inc(res_added, TM)

            for l in range(LAYERS):
                norm("nmix", l)
                fox(l) if l % 2 == 0 else gmlp(l)
                cross(l)
                dve.wait_ge(S["small_hi"], l + 2)
                dve.tensor_tensor(thin_view(wls), wsmall[:, :, :], thin_view(whs).bitcast(F32),
                                  ALU.subtract).then_inc(S["small_lo"], 1)
                norm("nffn", l)
                xn_los(l)
                route(l)
                experts(l)
        @block.gpsimd
        def _(pool):
            links = [0]

            def link(ins):
                links[0] += 1
                ins.then_inc(pchain, 1)
                pool.wait_ge(pchain, links[0])

            def load_gain(kind, l):
                n = NORMS.index((kind, l))
                if n >= 2:
                    pool.wait_ge(nat_ready, nats_upto(*NORMS[n - 2]))
                pool.dma_start(gain[:, n % 2, :], row_bcast(A["norm_" + kind][l], D)).then_inc(gain_loaded[n % 2], 16)

            load_gain("mix", 0)
            pool.dma_start(wsmall[:, :, 0:A_HEADS], kcols(A["ab_w_in"][0], 3 * A_W, A_HEADS)).then_inc(S["small_loaded0"], 16)
            link(pool.memset(halfp[:, :], -0.5))
            link(pool.memset(ident[:, :], 0.0))
            link(pool.affine_select(out=ident[:, :], in_=ident[:, :], compare_op=ALU.not_equal, fill=1.0, base=0,
                               pattern=[[-1, P]], channel_multiplier=1))
            pool.engine_nop().then_inc(consts_ready, 1)

            powers, nsq = [0], [0]

            def power(n):
                powers[0] += 1
                pool.wait_ge(var_ready, powers[0])
                link(pool.tensor_scalar(rstd[:, 0:n], ss[:, 0:n], EPS, None, ALU.add))
                pool.tensor_tensor(rstd[:, 0:n], rstd[:, 0:n], halfp[:, 0:n], ALU.pow).then_inc(rstd_ready, 1)

            def norm_power(tiles):
                for m in range(tiles):
                    nsq[0] += 1
                    pool.wait_ge(squares, nsq[0])
                    link(pool.tensor_scalar(rnorm[:, m:m + 1], mean[:, m:m + 1], EPS, None, ALU.add))
                    pool.tensor_tensor(rnorm[:, m:m + 1], rnorm[:, m:m + 1], halfp[:, 0:1], ALU.pow)\
                        .then_inc(norm_rstd, 1)

            def constants():
                link(pool.memset(whs[:, :].bitcast(F32), 0.0))
                link(pool.memset(wls[:, :].bitcast(F32), 0.0))
                link(pool.memset(onecol[:, :], 1.0))
                link(pool.memset(ones[:, :], 1.0))
                link(pool.memset(qT[A_DIM:A_DIM + 1, :, :], 1.0))
                link(pool.memset(causal[:, :], 0.0))
                link(pool.affine_select(out=causal[:, :], in_=causal[:, :], compare_op=ALU.is_ge, fill=-BIG, base=0,
                                        pattern=[[-1, P]], channel_multiplier=1))
                link(pool.affine_select(out=before[:, :], in_=ones[:, :], compare_op=ALU.is_ge, fill=0.0, base=-1,
                                        pattern=[[1, P]], channel_multiplier=-1))
                link(pool.iota(iota[:, :], pattern=[[1, SLOTS]], base=0, channel_multiplier=0,
                               allow_small_or_imprecise_dtypes=True))
                pool.engine_nop().then_inc(consts_ready, 1)

            pool.dma_start(small[:, 0:PACKED], A["packed"]).then_inc(params, 16)
            pool.dma_start(wblk[:, :, :, :].rearrange("p a m n -> p (a m n)"), A["blocks"]).then_inc(params, 16)
            for l in range(LAYERS):
                norm_power(TM)
                if l % 2 == 0:
                    constants()
                    power(TM * A_HEADS)
                    power(TM * A_HEADS)
                    pool.wait_ge(S["rec_ready"], 4)
                    pool.wait_ge(heads_ready, 1)
                else:
                    round_done(pool, ("nmix", l, TM - 1))
                    pool.dma_start(vbias[:, :], row_bcast(A["c_b_in"][0, C_W:2 * C_W], C_W)).then_inc(S["vbias_loaded"], 16)
                    pool.dma_start(bs[:, :, :], A["c_b_s"][0].rearrange("(a g) t -> a g t", a=1)
                                   .to_broadcast([P, C_GROUPS, P])).then_inc(S["bs_loaded"], 16)
                    power(TM)
                    pool.wait_ge(S["v_pre"], 4 * TM)
                pool.dma_start(mem[:, :, :], mem_in).then_inc(S["mem_loaded"], 16)
                load_gain("mem", l)
                load_gain("cross", l)
                norm_power(MM)
                if l % 2:
                    for kt in range(16):
                        pool.wait_ge(S["gt_hi"], kt + 1)
                        pool.tensor_tensor(gl[:, kt, :], gt[:, kt % 2, :], gh[:, kt, :].bitcast(F32),
                                           ALU.subtract).then_inc(S["gt_lo"], 1)
                norm_power(TM)
                load_gain("ffn", l)
                power(2 * MM)
                power(2 * MM)
                power(2 * TM)
                power(2 * TM)
                pool.wait_ge(S["o_copied"], GROUP0["x", l] + X_HEADS)
                pool.dma_start(wsmall[:, :, 0:GROUPS], A["moe_wg"][l].rearrange("(k p) n -> p k n", p=P))\
                    .then_inc(S[f"small_loaded{l + 1}"], 16)
                pool.dma_start(wsmall[:, :, GROUPS:36], A["moe_we"][l].rearrange("(k p) n -> p k n", p=P))\
                    .then_inc(S[f"small_loaded{l + 1}"], 16)
                norm_power(TM)
                if l + 1 < LAYERS:
                    load_gain("mix", l + 1)
                    pool.dma_start(wsn[:, :, :], A["c_w_s"][0].rearrange("g t s -> t g s")).then_inc(S["ws_loaded"], 16)
                    pool.wait_ge(S["ws_loaded"], 16)
                    pool.affine_select(out=wsn[:, :, :], in_=wsn[:, :, :], compare_op=ALU.is_ge, fill=0.0, base=0,
                                       pattern=[[0, C_GROUPS], [-1, P]], channel_multiplier=1).then_inc(S["ws_masked"], 1)



_BIG = ["x", "mem", "norm_mix", "norm_cross", "norm_mem", "norm_ffn", "ab_w_in", "ab_w_out", "c_w_in", "c_b_in",
        "c_w_s", "c_b_s", "c_w_out", "x_wq", "x_wkv", "x_wo", "moe_wg", "moe_we", "moe_w_gate", "moe_w_up", "moe_w_down"]


def layout(inputs):
    import numpy as np
    a = {n: np.asarray(inputs[n]) for n in inputs}
    arrays = {n: np.ascontiguousarray(a[n]) for n in _BIG}
    packed = np.zeros((P, PACKED), np.float32)

    def put(name, value):
        lo, n, parts, _ = PACK[name]
        packed[0:parts, lo:lo + n] = value

    cols = lambda v: v.reshape(-1, P).T
    put("fbias", a["ab_f_bias"][0][:, None])
    put("qg", a["ab_q_gain"][0][:, None])
    put("kg", a["ab_k_gain"][0][:, None])
    put("convw", a["ab_conv_w"][0].reshape(CONV, 4, P).transpose(2, 1, 0).reshape(P, 4 * CONV))
    for name, key in (("convb", "ab_conv_b"), ("bab", "ab_ba"), ("bxb", "ab_bx"), ("lam", "ab_lambda"),
                      ("vg", "c_v_gain")):
        put(name, cols(a[key][0]))
    put("ub", cols(a["c_b_in"][0, 0:C_W]))
    for name, key in (("xqg", "x_q_gain"), ("xkg", "x_k_gain")):
        put(name, np.concatenate([cols(a[key][l]) for l in range(LAYERS)], axis=1))
    put("rbias", np.concatenate([a["moe_bg"], a["moe_be"]], axis=1).reshape(1, -1))
    arrays["packed"] = packed
    blocks = np.zeros((P, 2, 4, P), np.float32)
    for j, key in enumerate(("ab_wa", "ab_wx")):
        for g in range(8):
            q = 64 * (g % 2)
            blocks[q:q + 64, j, g // 2, q:q + 64] = a[key][0, g]
    arrays["blocks"] = blocks.reshape(P, 8 * P)
    return arrays


def kernel(**inputs):
    import concourse.bacc as _bacc
    from concourse.bass_utils import run_bass_kernel_spmd as _run

    nc = _bacc.Bacc("TRN2", target_bir_lowering=False, num_devices=1)
    arrays = layout(inputs)
    aps = {n: nc.dram_tensor(f"in_{n}", v.shape, F32, kind="ExternalInput").ap() for n, v in arrays.items()}
    out = nc.dram_tensor("out_x", (1, T, D), F32, kind="ExternalOutput").ap()
    program(nc, aps, out)
    r = _run(nc, [{f"in_{n}": v for n, v in arrays.items()}], core_ids=[0])
    return r.results[0]["out_x"]
```
